# Optimizing a Trainium2 kernel written in Bass

```python
import math
import jax, jax.numpy as jnp
from jax import lax
import numpy as np

D_MODEL = 1024
BATCH = 1
SEQ = 512
DEPTH = 1

HEAD_DIM = 64
DIL_GROUPS = ((128, 1), (512, 4), (2048, 16))
HEADS_PER_GROUP = 4
N_HEADS_A = HEADS_PER_GROUP * len(DIL_GROUPS)
MAX_WINDOW = 2048
N_HEADS_B = 8
QBLOCK = 128
REL_BUCKETS = 32
REL_MAX_DIST = 2048
N_EXPERTS = 64
TOP_K = 8
D_EXPERT = 256
D_SHARED = 256
ROUTE_SCALE = 2.5
TOKEN_BLOCK = 128
EPS = 1e-6

WIDTH_A = 3 * N_HEADS_A * HEAD_DIM
WIDTH_B = 3 * N_HEADS_B * HEAD_DIM
D_IN = WIDTH_A + WIDTH_B + N_HEADS_B
OUT_A = HEADS_PER_GROUP * HEAD_DIM
OUT_B = N_HEADS_B * HEAD_DIM

kernel_name = "hybrid_dilated_fox_moe_block"

def rmsnorm(x, g):
    xf = x.astype(jnp.float32)
    y = xf * lax.rsqrt(jnp.mean(xf * xf, axis=-1, keepdims=True) + EPS)
    return (y * g.astype(jnp.float32)).astype(x.dtype)

def rel_bucket(dist):
    max_exact = REL_BUCKETS // 2
    n = jnp.maximum(dist.astype(jnp.float32), 1.0)
    large = max_exact + (jnp.log(n / max_exact) / math.log(REL_MAX_DIST / max_exact)
                         * (REL_BUCKETS - max_exact)).astype(jnp.int32)
    large = jnp.minimum(large, REL_BUCKETS - 1)
    return jnp.where(dist < max_exact, dist, large)

def swiglu(x, w_g, w_u, w_d):
    return (jax.nn.silu(x @ w_g) * (x @ w_u)) @ w_d

def dilated_attention(q, k, v, rel_bias):
    b, _, s, dh = q.shape
    pad = ((0, 0), (0, 0), (MAX_WINDOW, 0), (0, 0))
    k_pad = jnp.pad(k, pad)
    v_pad = jnp.pad(v, pad)
    groups = []
    for g, (w, d) in enumerate(DIL_GROUPS):
        hs = slice(g * HEADS_PER_GROUP, (g + 1) * HEADS_PER_GROUP)
        offs = d * jnp.arange(w // d + 1, dtype=jnp.int32)
        bias = rel_bias[rel_bucket(offs)][:, hs].T.astype(jnp.float32)
        groups.append((q[:, hs], k_pad[:, hs], v_pad[:, hs], offs, bias))

    def block(n):
        t = n * QBLOCK + jnp.arange(QBLOCK, dtype=jnp.int32)
        outs, lses = [], []
        for qg, kg_all, vg_all, offs, bias in groups:
            q_blk = lax.dynamic_slice_in_dim(qg, n * QBLOCK, QBLOCK, axis=2)
            pos = t[:, None] - offs[None, :]
            idx = pos + MAX_WINDOW
            kg = kg_all[:, :, idx]
            vg = vg_all[:, :, idx]
            sc = jnp.einsum('bhqd,bhqjd->bhqj', q_blk, kg).astype(jnp.float32)
            sc = sc + bias[None, :, None, :]
            sc = jnp.where((pos >= 0)[None, None], sc, -jnp.inf)
            lse = jax.nn.logsumexp(sc, axis=-1)
            p = jnp.exp(sc - lse[..., None])
            outs.append(jnp.einsum('bhqj,bhqjd->bhqd', p.astype(vg.dtype), vg))
            lses.append(lse)
        wgt = jax.nn.softmax(jnp.stack(lses, 0), axis=0)
        o = jnp.sum(jnp.stack(outs, 0).astype(jnp.float32) * wgt[..., None], axis=0)
        return o.astype(q.dtype)

    o = lax.map(block, jnp.arange(s // QBLOCK))
    return o.transpose(1, 0, 3, 2, 4).reshape(b, s, OUT_A)

def forgetting_attention(q, k, v, cum_logf):
    b, _, s, dh = q.shape
    kpos = jnp.arange(s, dtype=jnp.int32)

    def block(n):
        t = n * QBLOCK + jnp.arange(QBLOCK, dtype=jnp.int32)
        q_blk = lax.dynamic_slice_in_dim(q, n * QBLOCK, QBLOCK, axis=2)
        c_q = lax.dynamic_slice_in_dim(cum_logf, n * QBLOCK, QBLOCK, axis=2)
        sc = jnp.einsum('bhqd,bhkd->bhqk', q_blk, k).astype(jnp.float32)
        sc = sc + c_q[..., None] - cum_logf[:, :, None, :]
        sc = jnp.where((t[:, None] >= kpos[None, :])[None, None], sc, -jnp.inf)
        p = jax.nn.softmax(sc, axis=-1)
        return jnp.einsum('bhqk,bhkd->bhqd', p.astype(v.dtype), v)

    o = lax.map(block, jnp.arange(s // QBLOCK))
    return o.transpose(1, 0, 3, 2, 4).reshape(b, s, OUT_B)

def moe_ffn(h, w_router, router_bias, w_gate_e, w_up_e, w_down_e, w_gate_s, w_up_s, w_down_s):
    n, d = h.shape
    scores = jax.nn.sigmoid(h.astype(jnp.float32) @ w_router.astype(jnp.float32))
    _, top_idx = lax.top_k(scores + router_bias.astype(jnp.float32), TOP_K)
    top_s = jnp.take_along_axis(scores, top_idx, axis=-1)
    top_w = top_s / jnp.sum(top_s, axis=-1, keepdims=True) * ROUTE_SCALE
    gates = jnp.sum(jax.nn.one_hot(top_idx, N_EXPERTS, dtype=jnp.float32) * top_w[..., None], axis=1)
    gates = gates.astype(h.dtype)

    def block(args):
        xb, gb = args
        hg = jnp.einsum('td,edf->tef', xb, w_gate_e)
        hu = jnp.einsum('td,edf->tef', xb, w_up_e)
        hmid = jax.nn.silu(hg) * hu * gb[..., None]
        return jnp.einsum('tef,efd->td', hmid, w_down_e)

    nb = n // TOKEN_BLOCK
    routed = lax.map(block, (h.reshape(nb, TOKEN_BLOCK, d), gates.reshape(nb, TOKEN_BLOCK, N_EXPERTS)))
    return routed.reshape(n, d) + swiglu(h, w_gate_s, w_up_s, w_down_s)

def setup_inputs(seed: int = 0) -> dict:
    key = jax.random.key(seed)
    ks = jax.random.split(key, 24)
    nrm = lambda k, shape, scale: jax.random.normal(k, shape, jnp.float32) * scale
    D = D_MODEL
    return {
        "x": nrm(ks[0], (BATCH, SEQ, D), 1.0),
        "g_mix": 1.0 + nrm(ks[1], (D,), 0.02),
        "w_in": nrm(ks[2], (D, D_IN), D ** -0.5),
        "q_norm_a": 1.0 + nrm(ks[3], (HEAD_DIM,), 0.02),
        "k_norm_a": 1.0 + nrm(ks[4], (HEAD_DIM,), 0.02),
        "q_norm_b": 1.0 + nrm(ks[5], (HEAD_DIM,), 0.02),
        "k_norm_b": 1.0 + nrm(ks[6], (HEAD_DIM,), 0.02),
        "rel_bias": nrm(ks[7], (REL_BUCKETS, N_HEADS_A), 0.5),
        "b_forget": 3.0 + nrm(ks[8], (N_HEADS_B,), 0.5),
        "w_gate": nrm(ks[9], (D, 2 * D), D ** -0.5),
        "b_gate": nrm(ks[10], (2 * D,), 0.02),
        "w_proj_a": nrm(ks[11], (OUT_A, D), OUT_A ** -0.5),
        "w_proj_b": nrm(ks[12], (OUT_B, D), OUT_B ** -0.5),
        "w_out": nrm(ks[13], (D, D), D ** -0.5),
        "g_ffn": 1.0 + nrm(ks[14], (D,), 0.02),
        "w_router": nrm(ks[15], (D, N_EXPERTS), D ** -0.5),
        "router_bias": nrm(ks[16], (N_EXPERTS,), 0.01),
        "w_gate_e": nrm(ks[17], (N_EXPERTS, D, D_EXPERT), D ** -0.5),
        "w_up_e": nrm(ks[18], (N_EXPERTS, D, D_EXPERT), D ** -0.5),
        "w_down_e": nrm(ks[19], (N_EXPERTS, D_EXPERT, D), D_EXPERT ** -0.5),
        "w_gate_s": nrm(ks[20], (D, D_SHARED), D ** -0.5),
        "w_up_s": nrm(ks[21], (D, D_SHARED), D ** -0.5),
        "w_down_s": nrm(ks[22], (D_SHARED, D), D_SHARED ** -0.5),
    }

def reference(x, g_mix, w_in, q_norm_a, k_norm_a, q_norm_b, k_norm_b, rel_bias, b_forget,
              w_gate, b_gate, w_proj_a, w_proj_b, w_out, g_ffn, w_router, router_bias,
              w_gate_e, w_up_e, w_down_e, w_gate_s, w_up_s, w_down_s):
    b, s, d = x.shape
    scale = HEAD_DIM ** -0.5
    for _ in range(DEPTH):
        h = rmsnorm(x, g_mix)
        proj = h @ w_in
        pa = proj[..., :WIDTH_A].reshape(b, s, 3, N_HEADS_A, HEAD_DIM)
        pb = proj[..., WIDTH_A:WIDTH_A + WIDTH_B].reshape(b, s, 3, N_HEADS_B, HEAD_DIM)
        f_logit = proj[..., WIDTH_A + WIDTH_B:]

        qa = (rmsnorm(pa[:, :, 0], q_norm_a) * scale).transpose(0, 2, 1, 3)
        ka = rmsnorm(pa[:, :, 1], k_norm_a).transpose(0, 2, 1, 3)
        va = pa[:, :, 2].transpose(0, 2, 1, 3)
        y_a = dilated_attention(qa, ka, va, rel_bias)

        qb = (rmsnorm(pb[:, :, 0], q_norm_b) * scale).transpose(0, 2, 1, 3)
        kb = rmsnorm(pb[:, :, 1], k_norm_b).transpose(0, 2, 1, 3)
        vb = pb[:, :, 2].transpose(0, 2, 1, 3)
        log_f = jax.nn.log_sigmoid(f_logit.astype(jnp.float32) + b_forget.astype(jnp.float32))
        cum_logf = jnp.cumsum(log_f, axis=1).transpose(0, 2, 1)
        y_b = forgetting_attention(qb, kb, vb, cum_logf)

        gates = jax.nn.sigmoid(h @ w_gate + b_gate)
        merged = gates[..., :d] * (y_a @ w_proj_a) + gates[..., d:] * (y_b @ w_proj_b)
        x = x + merged @ w_out

        h2 = rmsnorm(x, g_ffn).reshape(b * s, d)
        ffn = moe_ffn(h2, w_router, router_bias, w_gate_e, w_up_e, w_down_e,
                      w_gate_s, w_up_s, w_down_s)
        x = x + ffn.reshape(b, s, d)
    return x


_drawn_inputs = setup_inputs


def setup_inputs(seed=0):
    import zlib

    import numpy as np

    out = dict(_drawn_inputs(seed))
    spreads = {}
    factors = {'q_norm_a': 3.041,
     'k_norm_a': 3.919,
     'b_gate': 5.398,
     'q_norm_b': 2.934,
     'k_norm_b': 2.737}
    for name, (base, spread) in spreads.items():
        noise = np.random.default_rng([zlib.crc32(name.encode()), seed]).standard_normal(out[name].shape)
        drawn = base * np.exp(spread * noise) if base else spread * noise
        out[name] = __import__('jax').numpy.asarray(drawn.astype(out[name].dtype))
    for name, factor in factors.items():
        out[name] = (out[name] * factor).astype(out[name].dtype)
    return out
```

```python
import math
from contextlib import ExitStack

import numpy as np
import concourse.bass as bass
from concourse import mybir

P = 128
HEAD_DIM = 64
DIL_GROUPS = ((128, 1), (512, 4), (2048, 16))
HEADS_PER_GROUP = 4
REL_BUCKETS, REL_MAX_DIST = 32, 2048
TOP_K = 8
ROUTE_SCALE = 2.5
EPS = 1e-6
MASKED = -1e30
NEVER = -3e38
SLOTS = 96
NO_TOKEN = 1024
SEQ = 512
DIST = SEQ + P


def layer(nc, x, g_mix, w_in, q_norm_a, k_norm_a, q_norm_b, k_norm_b, rel_bias, b_forget, w_gate, b_gate,
          w_proj_a, w_proj_b, w_out, g_ffn, w_router, router_bias, w_gate_e, w_up_e, w_down_e,
          w_gate_s, w_up_s, w_down_s, consts, bias_table, out):
    f32, bf16, i32, u32 = mybir.dt.float32, mybir.dt.bfloat16, mybir.dt.int32, mybir.dt.uint32
    ALU, ACT, AX = mybir.AluOpType, mybir.ActivationFunctionType, mybir.AxisListType
    E, D, F = w_gate_e.shape
    N = x.shape[1]
    x_rows, out_rows = x[0], out[0]
    NT, ND, NF = N // P, D // P, F // P
    HG = HEADS_PER_GROUP
    NG = len(DIL_GROUPS)
    HA, HB = HG * NG, b_forget.shape[0]
    WA, WB = HA * HEAD_DIM, HB * HEAD_DIM
    COLS = 512
    ROUNDS = -(-N // SLOTS)
    SH = NT
    ITEMS = SH + E

    hn_dram = nc.dram_tensor("hn_dram", [N, D], f32, kind="Internal").ap()
    vec_dram = nc.dram_tensor("vec_dram", [HA, P, DIST], f32, kind="Internal")
    negc_dram = nc.dram_tensor("negc_dram", [HB, N], f32, kind="Internal").ap()

    in_chunks = [("qk", 0, COLS), ("qk", COLS, COLS), ("qk", 2 * COLS, COLS), ("va", 3 * COLS, COLS),
                 ("va", 4 * COLS, 3 * WA - 4 * COLS), ("qb", 3 * WA, WB), ("kb", 3 * WA + WB, WB), ("vb", 3 * WA + 2 * WB, WB)]
    NIN = len(in_chunks)
    NCHUNK = NIN + 2 * D // COLS
    A_UNITS, B_UNITS, G_UNITS = 5 * NT, NIN * NT, NIN * NT + 2 * D // P
    unit_kind = lambda n: in_chunks[n // NT][0] if n < B_UNITS else "gate"
    makes_qk = lambda n: 0 <= n < B_UNITS and unit_kind(n) in ("qk", "qb", "kb")
    UA, UB = HG * NT, HB * 2

    def key_blocks_a(u):
        i = u % NT
        return [(0 if g else max(0, i - 1), i + 1) for g in range(NG)]

    def blocks_a(u):
        return [(g, b) for g, (b0, b1) in enumerate(key_blocks_a(u)) for b in range(b0, b1)]

    def tiles_b(v):
        return (v % 2, NT - 1 - v % 2)

    def blocks_b(v):
        return [(i, b) for i in tiles_b(v) for b in range(i + 1)]

    uses, order = [0, 0], {}

    def number(key, bank):
        order[key] = (bank, uses[bank])
        uses[bank] += 1

    for t in range(NT):
        for b in range(2):
            number(("x", t, b), b)
    for n in range(A_UNITS):
        if makes_qk(n - 1):
            number(("qk", n - 1), n % 2)
    for u in range(UA + 1):
        if u >= 1:
            for r in range(-(-len(blocks_a(u - 1)) // 4)):
                number(("pa", u - 1, r), r % 2)
            if makes_qk(A_UNITS + u - 2):
                number(("qk", A_UNITS + u - 2), 1)
    for v in range(1, UB + 1):
        for r in range(2):
            number(("pb", v - 1, r), r)
    for r in range(2 + 4):
        number(("y", r), r % 2)
    for t in range(NT):
        for b in range(2):
            number(("h", t, b), b)

    ctx = ExitStack()
    with ctx:
        def sb(name, shape, dt=f32):
            return ctx.enter_context(nc.sbuf_tensor(name, shape, dt))

        def sem(name):
            return ctx.enter_context(nc.semaphore(name))

        xres = sb("xres", [P, NT, D])
        cst = sb("cst", [P, 4 * P + NT + 1 + ROUNDS])
        ident = cst[:, 0:P]
        thresholds = cst[:, 4 * P + NT + 1:4 * P + NT + ROUNDS]
        iota_b, tri_b, mask_b, ident_b, ones_b = (sb(n, [P, P], bf16) for n in ("iota_b", "tri_b", "mask_b", "ident_b", "ones_b"))
        gmixT, gffnT, bgateT = sb("gmixT", [P, ND]), sb("gffnT", [P, ND]), sb("bgateT", [P, 2 * D // P])
        gains = sb("gains", [P, 4])
        bforget = sb("bforget", [HB, 1])
        relb = sb("relb", [REL_BUCKETS + 1, HA])
        wf = sb("wf", [P, ND, HB])
        minus_half = sb("minus_half", [P, HB])
        sumsq = sb("sumsq", [P, 2, HB]); mean = sb("mean", [P, 2, HB]); rnorm = sb("rnorm", [P, 2, HB])
        rowmax = sb("rowmax", [P, 2, 2]); negmax = sb("negmax", [P, 2, 2]); rowsum = sb("rowsum", [P, 2, 2]); rowinv = sb("rowinv", [P, 2, 2])
        cq = sb("cq", [P, NT, HB])
        turn = sb("turn", [16, 1])
        cmax = sb("cmax", [P, 1]); over = sb("over", [P, ROUNDS]); oround = sb("oround", [P, 1]); rounds_i = sb("rounds_i", [P, 1], i32)
        gsum = sb("gsum", [P, NT]); ginv = sb("ginv", [P, NT]); m8 = sb("m8", [P, NT, 8])
        gate = sb("gate", [P, 4])
        idxg = [sb(f"idxg{i}", [P, 1], u32) for i in range(4)]
        idxs = [sb(f"idxs{i}", [P, 1], u32) for i in range(4)]
        hn_ss, hn_ms, hn_r = sb("hn_ss", [P, NT]), sb("hn_ms", [P, NT]), sb("hn_r", [P, NT])
        rbias = sb("rbias", [P, E])

        KB = 256
        arena = sb("arena", [P, 184 * KB])

        def at(kb, cols):
            return arena[:, int(kb * KB):int(kb * KB) + cols]

        ring = [at(16 * i, ND * COLS).rearrange("p (j c) -> p j c", j=ND) for i in range(3)]
        qTa, kTa = (at(k, HA // 2 * N).rearrange("p (h t) -> p h t", h=HA // 2) for k in (48, 60))
        va = at(72, NT * WA).rearrange("p (t c) -> p t c", t=NT)
        bias = at(84, HA * N).rearrange("p (h u) -> p h u", h=HA)
        qTb, kTb = (at(k, HB // 2 * N).rearrange("p (h t) -> p h t", h=HB // 2) for k in (108, 116))
        vb = at(124, NT * WB).rearrange("p (t c) -> p t c", t=NT)
        xn = [at(108 + 4 * i, D) for i in range(2)]
        fx, fa, fe, fl = (arena[0:HB, (124 + 2 * i) * KB:(124 + 2 * i) * KB + N] for i in range(4))
        sc_a = [at(132 + 5 * i, 10 * P) for i in range(2)]
        pT_a = [at(142 + 5 * i, 10 * P).rearrange("p (b q) -> p b q", q=P) for i in range(2)]
        sc_b = [at(132 + 2.5 * i, 5 * P) for i in range(2)]
        pT_b = [at(137 + 2.5 * i, 5 * P).rearrange("p (b q) -> p b q", q=P) for i in range(2)]
        hT = at(152, ND * N).rearrange("p (j t) -> p j t", j=ND)
        yTa = at(152, 2 * N).rearrange("p (j t) -> p j t", j=2)
        yTb = at(156, 4 * N).rearrange("p (j t) -> p j t", j=4)
        sq = at(168, D)
        qkrow = [at(172 + 2 * i, COLS) for i in range(2)]
        table_b = arena[0:REL_BUCKETS + 1, 132 * KB:132 * KB + NG * DIST]
        vec = arena[0:HG, 140 * KB:140 * KB + NG * DIST]
        yrow_a = at(176, NT * HG * HEAD_DIM).rearrange("p (t c) -> p t c", t=NT)
        yrow_b = at(100, NT * WB).rearrange("p (t c) -> p t c", t=NT)
        negc = at(48, HB * N).rearrange("p (h t) -> p h t", h=HB)
        gates = at(64, 2 * D // P * N).rearrange("p (m t) -> p m t", m=2 * D // P)
        wpa = at(142, 2 * D).rearrange("p (j c) -> p j c", j=2)
        wpb = [at(k, D) for k in (96, 168, 172, 180)]
        merged = at(48, ND * N).rearrange("p (m t) -> p m t", m=ND)
        wout = at(0, ND * D).rearrange("p (j c) -> p j c", j=ND)
        gated = [at(132 + 2 * i, N) for i in range(2)]
        sq_h = at(168, D)
        hn = at(88, NT * D).rearrange("p (t d) -> p t d", t=NT)
        h2T = at(152, ND * N).rearrange("p (j t) -> p j t", j=ND)
        wgu = [at(k, 2 * ND * F).rearrange("p (j c) -> p j c", j=ND) for k in (108, 32, 0, 64)]
        wd = [at(k, NF * D).rearrange("p (j c) -> p j c", j=NF) for k in (124, 132, 16, 80)]
        y = [at(24 + 4 * i, D) for i in range(2)]
        xg = [at(88 + 4 * i, D) for i in range(4)]
        table = at(104, NT * E * 3).bitcast(bf16).rearrange("p (t e c) -> p t e c", t=NT, e=E)
        xT = [at(140 + 4 * i, ND * P).rearrange("p (j s) -> p j s", j=ND) for i in range(2)]
        silu = [at(148 + i, F) for i in range(2)]
        mid = [at(150 + i, F) for i in range(2)]
        midT = [at(58 + i, NF * P).rearrange("p (j s) -> p j s", j=NF) for i in range(2)]
        onehot = [at(56 + i, NT * P // 2).bitcast(bf16).rearrange("p (t s) -> p t s", t=NT) for i in range(2)]
        scores, sel, rep, M, gt, gres = (at(48 + i, NT * E).rearrange("p (t e) -> p t e", t=NT) for i in range(6))
        Mb = at(54, NT * E // 2).bitcast(bf16).rearrange("p (t e) -> p t e", t=NT)
        pos = at(55, NT * E).rearrange("p (t e) -> p t e", t=NT)
        wr = at(180, ND * E).rearrange("p (j e) -> p j e", j=ND)

        bank = [ctx.enter_context(nc.psum_tensor(f"bank{i}", [P, 512], f32)) for i in range(8)]
        psD, psS, psT, psV = bank[0:2], bank[2:5], bank[5:7], bank[7]
        psG, psY, psM, psI = bank[0:2], bank[2:4], bank[4], bank[7]

        x_in = [sem(f"x_in{t}") for t in range(NT)]
        const_in, small_in, table_in, forget_in = sem("const_in"), sem("small_in"), sem("table_in"), sem("forget_in")
        chunk_in = [sem(f"chunk_in{i}") for i in range(3)]
        vec_free, vec_stored, bias_in = sem("vec_free"), sem("vec_stored"), sem("bias_in")
        vec_psum, negc_ready, negc_stored = sem("vec_psum"), sem("negc_ready"), sem("negc_stored")
        negc_in = [sem(f"negc_in{i}") for i in range(4)]
        cq_psum = sem("cq_psum")
        squared, mean_ready, rnorm_ready = sem("squared"), sem("mean_ready"), sem("rnorm_ready")
        xn_ready, setup_done = sem("xn_ready"), sem("setup_done")
        dense_ready = sem("dense_ready")
        dense_used = [sem(f"dense_used{i}") for i in range(2)]
        summed = sem("summed"); qkrow_ready = sem("qkrow_ready")
        tr_ready = [sem(f"tr_ready{i}") for i in range(2)]
        tr_used = [sem(f"tr_used{i}") for i in range(2)]
        scores_psum, scores_ready, exp_ready = sem("scores_psum"), sem("scores_ready"), sem("exp_ready")
        pv_psum, y_norm = sem("pv_psum"), sem("y_norm")
        f_psum, f_x, f_abs, f_exp, f_ln = sem("f_psum"), sem("f_x"), sem("f_abs"), sem("f_exp"), sem("f_ln")
        proj_in, wout_in = sem("proj_in"), [sem(f"wout_in{i}") for i in range(2)]
        sig_ready, proj_psum, merged_ready = sem("sig_ready"), sem("proj_psum"), sem("merged_ready")
        out_psum, x1_ready = sem("out_psum"), sem("x1_ready")
        hn_ready, hn_stored = sem("hn_ready"), sem("hn_stored")
        dve_chain, act_chain = sem("dve_chain"), sem("act_chain")
        shared_in, router_in = sem("shared_in"), sem("router_in")
        logits_psum, scores_sig, mask_ready, counts_psum, routed = (
            sem("logits_psum"), sem("scores_sig"), sem("mask_ready"), sem("counts_psum"), sem("routed"))
        w_in_sem = [[sem(f"w_slot{n}_{k}") for k in "gud"] for n in range(4)]
        onehot_ready, idx_psum, idx_ready, idx_kept = sem("onehot_ready"), sem("idx_psum"), sem("idx_ready"), sem("idx_kept")
        gathered = [sem(f"gathered{i}") for i in range(4)]
        xT_psum, xT_ready, gu_psum, silu_ready = sem("xT_psum"), sem("xT_ready"), sem("gu_psum"), sem("silu_ready")
        mid_ready, midT_psum, midT_ready = sem("mid_ready"), sem("midT_psum"), sem("midT_ready")
        y_psum, y_ready = sem("y_psum"), sem("y_ready")
        based = [sem(f"based{i}") for i in range(2)]
        scattered, pool_set, turns = sem("scattered"), sem("pool_set"), sem("turns")
        o_free, o_pos, o_onehot, o_idx_psum, o_idx, o_gathered = (
            sem("o_free"), sem("o_pos"), sem("o_onehot"), sem("o_idx_psum"), sem("o_idx"), sem("o_gathered"))
        o_xT_psum, o_xT, o_gu, o_silu, o_mid, o_midT_psum, o_midT, o_y_psum, o_y, o_scattered = (
            sem(n) for n in ("o_xT_psum", "o_xT", "o_gu", "o_silu", "o_mid", "o_midT_psum", "o_midT", "o_y_psum", "o_y", "o_scattered"))

        def after(eng, s, n):
            if not isinstance(n, int) or n > 0:
                eng.wait_ge(s, n)

        def lands(k, per, slot):
            if isinstance(k, int):
                return per * (k // 4 + 1)
            return (k - slot) * (per // 4) + per

        block = ctx.enter_context(nc.Block())

        @block.sync
        def _(sp):
            for t in range(NT):
                sp.dma_start(xres[:, t, :], x_rows[t * P:(t + 1) * P, :]).then_inc(x_in[t], 16)
                if t == 0:
                    sp.dma_start(cst[:], consts).then_inc(const_in, 16)
                    sp.dma_start(gmixT[:], g_mix.rearrange("(p j) -> p j", p=P)).then_inc(const_in, 16)

            def load_chunk(c):
                if c < NIN:
                    _, c0, cols = in_chunks[c]
                    src = w_in[:, c0:c0 + cols]
                else:
                    cols = COLS
                    src = w_gate[:, (c - NIN) * COLS:(c - NIN + 1) * COLS]
                after(sp, dense_ready, NT * (c - 2))
                sp.dma_start(ring[c % 3][:, :, 0:cols], src.rearrange("(p j) c -> p j c", p=P)).then_inc(chunk_in[c % 3], 16)

            sp.dma_start(wf[:], w_in[:, 3 * WA + 3 * WB:3 * WA + 3 * WB + HB].rearrange("(p j) h -> p j h", p=P)).then_inc(forget_in, 16)
            load_chunk(0)
            sp.dma_start(bforget[:], b_forget.rearrange("(h o) -> h o", o=1)).then_inc(forget_in, 16)
            for c, g in enumerate((q_norm_a, k_norm_a, q_norm_b, k_norm_b)):
                for half in range(2):
                    sp.dma_start(gains[half * HEAD_DIM:(half + 1) * HEAD_DIM, c:c + 1], g.rearrange("(d o) -> d o", o=1)).then_inc(small_in, 16)
            sp.dma_start(relb[0:REL_BUCKETS, :], rel_bias).then_inc(table_in, 16)
            sp.dma_start(table_b, bias_table).then_inc(table_in, 16)
            load_chunk(1)
            sp.dma_start(bgateT[:], b_gate).then_inc(small_in, 16)
            sp.dma_start(gffnT[:], g_ffn.rearrange("(p j) -> p j", p=P)).then_inc(small_in, 16)
            sp.dma_start(rbias[:], router_bias.rearrange("(o e) -> o e", o=1).broadcast_to([P, E])).then_inc(small_in, 16)
            load_chunk(2)
            sp.wait_ge(vec_free, 2 * NG)
            for g in range(NG):
                row = vec[:, g * DIST:(g + 1) * DIST].unsqueeze(1).broadcast_to([HG, P, DIST])
                sp.dma_start(vec_dram.ap()[g * HG:(g + 1) * HG], row).then_inc(vec_stored, 16)
            sp.wait_ge(vec_stored, 16 * NG)
            for g in range(NG):
                for h in range(HG):
                    toeplitz = bass.AP(vec_dram, (g * HG + h) * P * DIST + P - 1, [[DIST - 1, P], [1, N]])
                    sp.dma_start(bias[:, g * HG + h, :], toeplitz).then_inc(bias_in, 16)
            sp.wait_ge(negc_ready, 1)
            sp.dma_start(negc_dram, fe).then_inc(negc_stored, 16)
            for c in range(3, NIN):
                load_chunk(c)
            load_chunk(NIN)
            load_chunk(NIN + 1)
            sp.wait_ge(scores_ready, UA)
            sp.wait_ge(negc_stored, 16)
            for i in range(4):
                sp.dma_start(negc[:, 2 * i:2 * i + 2, :], negc_dram[2 * i:2 * i + 2, :].rearrange("(o h) t -> o h t", o=1).broadcast_to([P, 2, N])).then_inc(negc_in[i], 16)
            sp.wait_ge(pv_psum, UA)
            sp.dma_start(wpa, w_proj_a.rearrange("(j p) c -> p j c", p=P)).then_inc(proj_in, 16)
            for j in range(4):
                sp.dma_start(wpb[j], w_proj_b[j * P:(j + 1) * P, :]).then_inc(proj_in, 16)
            for c in range(NIN + 2, NCHUNK):
                load_chunk(c)
            w_out_v = w_out.rearrange("(j p) c -> p j c", p=P)
            sp.wait_ge(dense_ready, NT * (NCHUNK - 1))
            for i in range(2):
                sp.dma_start(wout[:, 4 * i:4 * i + 4, :], w_out_v[:, 4 * i:4 * i + 4, :]).then_inc(wout_in[i], 16)

            def load_w(n, k, e):
                t = (w_gate_e, w_up_e, w_down_e)[k]
                src = t[bass.ds(e, 1)].rearrange("o (p j) f -> p (o j) f", p=P)
                dst = (wgu[n][:, :, 0:F], wgu[n][:, :, F:2 * F], wd[n])[k]
                sp.dma_start(dst, src).then_inc(w_in_sem[n][k], 16)

            sp.wait_ge(pv_psum, UA + UB)
            for k in range(3):
                load_w(0, k, 0)
            sp.wait_ge(dense_ready, NT * NCHUNK)
            load_w(1, 0, 1)
            load_w(1, 1, 1)
            sp.wait_ge(merged_ready, ND)
            load_w(1, 2, 1)
            sp.dma_start(wgu[3][:, :, 0:F], w_gate_s.rearrange("(p j) f -> p j f", p=P)).then_inc(shared_in, 16)
            sp.dma_start(wgu[3][:, :, F:2 * F], w_up_s.rearrange("(p j) f -> p j f", p=P)).then_inc(shared_in, 16)
            sp.dma_start(wd[3], w_down_s.rearrange("(p j) f -> p j f", p=P)).then_inc(shared_in, 16)
            sp.dma_start(wr, w_router.rearrange("(p j) e -> p j e", p=P)).then_inc(router_in, 16)
            for t in range(NT):
                sp.wait_ge(hn_ready, t + 1)
                sp.dma_start(hn_dram[t * P:(t + 1) * P, :], hn[:, t, :]).then_inc(hn_stored, 16)
            sp.wait_ge(out_psum, 2 * NT)
            for k in range(3):
                load_w(2, k, 2)
            for t in range(SH):
                sp.wait_ge(y_ready, 2 * (t + 1))
                sp.dma_start(out_rows[t * P:(t + 1) * P, :], y[t % 2]).then_inc(based[t % 2], 16)
            sp.wait_ge(y_psum, 2 * SH)
            for k in range(3):
                load_w(3, k, 3)

            regs = [sp.alloc_register(f"turn_value{i}") for i in range(4)]
            with sp.Fori(1, E // 4) as m:
                for n in range(4):
                    k = 4 * m + n
                    last = (n - 1) % 4
                    for reg, v in zip(regs, (lands(k - 1, 16, last), lands(k, 16, n), SH + k - 3, 2 * (SH + k - 3))):
                        sp.reg_mov(reg, v)
                    before, own, read_gu, read_d = (bass.RuntimeValue.of_register_unchecked(r, min_val=1, max_val=2 * 16 * E) for r in regs)
                    sp.wait_ge(w_in_sem[last][1], before)
                    sp.wait_ge(gu_psum, read_gu)
                    load_w(n, 0, k)
                    sp.wait_ge(w_in_sem[last][2], before)
                    load_w(n, 1, k)
                    sp.wait_ge(w_in_sem[n][0], own)
                    sp.wait_ge(y_psum, read_d)
                    load_w(n, 2, k)

            more = sp.value_load(rounds_i[0:1, 0:1], min_val=0, max_val=ROUNDS - 1)
            with sp.If(more > 0):
                with sp.Fori(0, more * E) as it:
                    sp.wait_ge(o_free, it + 1)
                    for k in range(3):
                        load_w(0, k, it % E)
            with sp.Else():
                pass

        @block.gpsimd
        def _(pool):
            nc.gpsimd.memset(minus_half[:], -0.5).then_inc(pool_set, 1)
            pool.wait_ge(pool_set, 1)

            def root(dst, src, n, width):
                pool.wait_ge(mean_ready, n)
                nc.gpsimd.tensor_tensor(dst, src, minus_half[:, 0:width], ALU.pow).then_inc(rnorm_ready, 1)

            n = 0
            for t in range(NT):
                n += 1
                root(hn_r[:, t:t + 1], hn_ms[:, t:t + 1], n, 1)
            for q in range(B_UNITS):
                if makes_qk(q):
                    n += 1
                    root(rnorm[:, q % 2, :], mean[:, q % 2, :], n, HB)
            for t in range(NT):
                n += 1
                root(hn_r[:, t:t + 1], hn_ms[:, t:t + 1], n, 1)
            pool.wait_ge(hn_stored, 16 * NT)
            for b in range(2):
                pool.wait_ge(tr_ready[b], uses[b])
            for i in range(4):
                nc.gpsimd.memset(xg[i], 0.0).then_inc(pool_set, 1)
            pool.wait_ge(pool_set, 5)
            last_row = pool.to_reg(N - 1)

            def take_turn(before):
                after(pool, turns, before)
                nc.gpsimd.tensor_tensor(turn[:], minus_half[0:16, 0:1], minus_half[0:16, 0:1], ALU.add).then_inc(turns, 1)

            def gather(slot, before, done):
                take_turn(before)
                pool.indirect_dma_start(out=xg[slot][0:SLOTS, :], out_offset=None, in_=hn_dram,
                                        in_offset=bass.IndirectOffsetOnAxis(idxg[slot][0:SLOTS, 0:1], 0),
                                        bounds_check=last_row, oob_is_err=False).then_inc(done, 16)

            def scatter(slot, idx, before, done):
                take_turn(before)
                pool.indirect_dma_start(out=out_rows, out_offset=bass.IndirectOffsetOnAxis(idx[0:SLOTS, 0:1], 0),
                                        in_=y[slot][0:SLOTS, :], in_offset=None, bounds_check=last_row, oob_is_err=False,
                                        compute_op=ALU.add).then_inc(done, 16)

            def gather_k(k, slot, before):
                after(pool, xT_psum, k - 3)
                pool.wait_ge(idx_ready, k + 1)
                gather(slot, before, gathered[slot])

            def scatter_k(k, u, before):
                pool.wait_ge(y_ready, 2 * (SH + k + 1))
                pool.wait_ge(idx_kept, k + 1)
                after(pool, scattered, 16 * k)
                scatter(u % 2, idxs[u], before, scattered)

            for k in range(5):
                gather_k(k, k % 4, k)
            for b in based:
                pool.wait_ge(b, 8 * SH)

            def pair(k, u):
                scatter_k(k, u, 5 + 2 * k)
                gather_k(k + 5, (u + 1) % 4, 6 + 2 * k)

            for k in range(4):
                pair(k, k)
            with pool.Fori(1, (E - 5) // 4) as m:
                for u in range(4):
                    pair(4 * m + u, u)
            for k in range((E - 5) // 4 * 4, E - 5):
                pair(k, k % 4)
            for k in range(E - 5, E):
                scatter_k(k, k % 4, 5 + 2 * (E - 5) + k - (E - 5))
            pool.wait_ge(scattered, 16 * E)

            more = pool.value_load(rounds_i[0:1, 0:1], min_val=0, max_val=ROUNDS - 1)
            with pool.If(more > 0):
                with pool.Fori(0, more * E) as it:
                    pool.wait_ge(o_idx, it + 1)
                    gather(0, 2 * E + 2 * it, o_gathered)
                    pool.wait_ge(o_y, it + 1)
                    scatter(0, idxg[0], 2 * E + 2 * it + 1, o_scattered)
                    pool.wait_ge(o_scattered, 16 * it + 16)
            with pool.Else():
                pass

        @block.scalar
        def _(act):
            chain = [0]

            def link(ins):
                chain[0] += 1
                ins.then_inc(act_chain, 1)
                act.wait_ge(act_chain, chain[0])

            sums = [0]

            def square(out_, in_, **kw):
                sums[0] += 1
                nc.scalar.activation(out_, in_, ACT.Square, **kw).then_inc(squared, 1)

            for t in range(NT):
                act.wait_ge(x_in[t], 16)
                after(act, squared, sums[0])
                square(sq, xres[:, t, :], accum_out=hn_ss[:, t:t + 1])
            act.wait_ge(f_abs, 1)
            nc.scalar.activation(fe, fa, ACT.Exp, scale=-1.0).then_inc(f_exp, 1)
            act.wait_ge(f_exp, 1)
            nc.scalar.activation(fl, fe, ACT.Ln, bias=1.0).then_inc(f_ln, 1)

            def copy_qk(n):
                b, c = order[("qk", n)]
                act.wait_ge(tr_ready[b], c + 1)
                t = n % NT
                kind = unit_kind(n)
                cols = slice(t * P, (t + 1) * P)
                src = psT[b][:].rearrange("p (h q) -> p h q", q=P)
                if kind == "qk":
                    p0 = 4 * (n // NT)
                    cut = min(max(HA // 2 - p0, 0), 4)
                    parts = [(0, qTa, p0, 0, cut), (1, kTa, p0 - HA // 2, cut, 4)]
                else:
                    parts = [(2, qTb, 0, 0, 4)] if kind == "qb" else [(3, kTb, 0, 0, 4)]
                parts = [x for x in parts if x[3] < x[4]]
                for gain, dst, p0, a, z in parts:
                    last = nc.scalar.activation(dst[:, p0 + a:p0 + z, cols], src[:, a:z, :], ACT.Copy, scale=gains[:, gain:gain + 1])
                last.then_inc(tr_used[b], 1)

            def dense(n):
                kind, t, ps = unit_kind(n), n % NT, psD[n % 2]
                act.wait_ge(dense_ready, n + 1)
                if makes_qk(n):
                    after(act, summed, sq_count[0])
                    sq_count[0] += 1
                    square(sq[:, 0:COLS], ps[:])
                elif kind == "gate":
                    m = n - B_UNITS
                    nc.scalar.activation(gates[:, m, :], ps[:], ACT.Identity, bias=bgateT[:, m:m + 1]).then_inc(dense_used[n % 2], 1)
                else:
                    _, c0, cols = in_chunks[n // NT]
                    if kind == "vb":
                        act.wait_ge(negc_stored, 16)
                    dst = va[:, t, c0 - 2 * WA:c0 - 2 * WA + cols] if kind == "va" else vb[:, t, :]
                    nc.scalar.activation(dst, ps[:, 0:cols], ACT.Copy).then_inc(dense_used[n % 2], 1)

            sq_count = [0]
            act.wait_ge(setup_done, 1)
            act.wait_ge(squared, NT)
            for n in range(A_UNITS):
                dense(n)
                if makes_qk(n - 1):
                    copy_qk(n - 1)

            def copy_p(key, dst):
                b, c = order[key]
                act.wait_ge(tr_ready[b], c + 1)
                w = dst.shape[1]
                nc.scalar.activation(dst, psT[b][:, 0:w * P].rearrange("p (b q) -> p b q", q=P), ACT.Copy).then_inc(tr_used[b], 1)

            for u in range(UA + 1):
                if u >= 1:
                    nb = len(blocks_a(u - 1))
                    after(act, pv_psum, u - 2)
                    for r in range(0, -(-nb // 4), 2):
                        copy_p(("pa", u - 1, r), pT_a[(u - 1) % 2][:, 4 * r:min(4 * r + 4, nb), :])
                if u < UA:
                    act.wait_ge(scores_ready, u + 1)
                    w = P * len(blocks_a(u))
                    nc.scalar.activation(sc_a[u % 2][:, 0:w], sc_a[u % 2][:, 0:w], ACT.Exp, bias=negmax[:, u % 2, 0:1],
                                         accum_out=rowsum[:, u % 2, 0:1]).then_inc(exp_ready, 1)
                n = A_UNITS + u - 1
                if u >= 1:
                    if makes_qk(n - 1):
                        copy_qk(n - 1)
                    if n < B_UNITS:
                        dense(n)
            for v in range(UB + 1):
                if v >= 1:
                    after(act, pv_psum, UA + v - 2)
                    copy_p(("pb", v - 1, 0), pT_b[(v - 1) % 2][:, 0:4, :])
                if v < UB:
                    act.wait_ge(scores_ready, UA + v + 1)
                    c0 = 0
                    for s, i in enumerate(tiles_b(v)):
                        w = P * (i + 1)
                        last = nc.scalar.activation(sc_b[v % 2][:, c0:c0 + w], sc_b[v % 2][:, c0:c0 + w], ACT.Exp,
                                                    bias=negmax[:, v % 2, s:s + 1], accum_out=rowsum[:, v % 2, s:s + 1])
                        c0 += w
                    last.then_inc(exp_ready, 1)
                if v >= 1:
                    dense(B_UNITS + v - 1)
            act.wait_ge(dense_used[0], G_UNITS // 2)
            act.wait_ge(dense_used[1], G_UNITS // 2)
            for m in range(ND):
                for g in (m, ND + m):
                    nc.scalar.activation(gates[:, g, :], gates[:, g, :], ACT.Sigmoid).then_inc(sig_ready, 1)
            for t in range(NT):
                act.wait_ge(x1_ready, 2 * (t + 1))
                act.wait_ge(squared, sums[0])
                square(sq_h, xres[:, t, :], accum_out=hn_ss[:, t:t + 1])
            act.wait_ge(logits_psum, 1)
            nc.scalar.activation(scores, psI[:, 0:NT * E].rearrange("p (t e) -> p t e", t=NT), ACT.Sigmoid).then_inc(scores_sig, 1)

            def silu_of(n, rows):
                return nc.scalar.activation(silu[n][0:rows, :], psG[n][0:rows, 0:F], ACT.Silu)

            def copy_midT(n, rows):
                return nc.scalar.activation(midT[n][:, :, 0:rows], psM[:, 0:NF * P].rearrange("p (j s) -> p j s", j=NF)[:, :, 0:rows], ACT.Copy)

            def copy_y(n, h):
                return nc.scalar.activation(y[n][0:SLOTS, h * 512:(h + 1) * 512], psY[h][0:SLOTS, :], ACT.Copy)

            def silu_i(it, n, rows):
                act.wait_ge(gu_psum, it + 1)
                after(act, mid_ready, it - 1)
                silu_of(n, rows).then_inc(silu_ready, 1)

            def y_i(it, n):
                after(act, scattered, 16 * (it - SH - 1))
                for h in range(2):
                    act.wait_ge(y_psum, 2 * it + h + 1)
                    copy_y(n, h).then_inc(y_ready, 1)

            def midT_i(it, n, rows):
                act.wait_ge(midT_psum, it + 1)
                after(act, y_psum, 2 * (it - 1))
                copy_midT(n, rows).then_inc(midT_ready, 1)

            def step(it, n):
                silu_i(it, n, SLOTS)
                y_i(it - 1, 1 - n)
                midT_i(it, n, SLOTS)

            for it in range(SH + 1):
                silu_i(it, it % 2, P if it < SH else SLOTS)
                midT_i(it, it % 2, P if it < SH else SLOTS)
            for b in based:
                act.wait_ge(b, 8 * SH)
            step(SH + 1, 1)
            with act.Fori(SH // 2 + 1, ITEMS // 2) as m:
                for n in range(2):
                    step(2 * m + n, n)
            y_i(ITEMS - 1, 1)

            more = act.value_load(rounds_i[0:1, 0:1], min_val=0, max_val=ROUNDS - 1)
            with act.If(more > 0):
                with act.Fori(0, more * E) as it:
                    act.wait_ge(o_gu, it + 1)
                    silu_of(0, SLOTS).then_inc(o_silu, 1)
                    act.wait_ge(o_midT_psum, it + 1)
                    copy_midT(0, SLOTS).then_inc(o_midT, 1)
                    act.wait_ge(o_y_psum, it + 1)
                    copy_y(0, 0)
                    copy_y(0, 1).then_inc(o_y, 1)
            with act.Else():
                pass

        @block.vector
        def _(dve):
            chain = [0]

            def link(ins):
                chain[0] += 1
                ins.then_inc(dve_chain, 1)
                dve.wait_ge(dve_chain, chain[0])

            means = [0]

            def mean_of(dst, src, count):
                means[0] += 1
                nc.vector.tensor_scalar(dst, src, 1.0 / count, EPS, ALU.mult, ALU.add).then_inc(mean_ready, 1)
                dve.wait_ge(rnorm_ready, means[0])

            nc.vector.memset(relb[REL_BUCKETS:REL_BUCKETS + 1, :], 1.0)
            nc.vector.memset(ones_b[:], 1.0)
            dve.wait_ge(const_in, 32)
            nc.vector.tensor_copy(iota_b[:], cst[:, P:2 * P])
            nc.vector.tensor_copy(tri_b[:], cst[:, 2 * P:3 * P])
            nc.vector.tensor_copy(mask_b[:], cst[:, 3 * P:4 * P])
            nc.vector.tensor_copy(ident_b[:], ident)

            def copy_wide(key, dst, g):
                for b in range(2):
                    k, c = order[(*key, b)]
                    dve.wait_ge(tr_ready[k], c + 1)
                    h = ND // 2
                    nc.vector.tensor_tensor(dst[:, b * h:(b + 1) * h, key[1] * P:(key[1] + 1) * P],
                                            psT[k][:].rearrange("p (j q) -> p j q", q=P),
                                            g[:, b * h:(b + 1) * h].unsqueeze(2).broadcast_to([P, h, P]), ALU.mult).then_inc(tr_used[k], 1)

            for t in range(NT):
                dve.wait_ge(squared, t + 1)
                mean_of(hn_ms[:, t:t + 1], hn_ss[:, t:t + 1], D)
                if t >= 2:
                    b, c = order[("x", t - 2, 1)]
                    dve.wait_ge(tr_ready[b], c + 1)
                nc.vector.tensor_scalar(xn[t % 2], xres[:, t, :], hn_r[:, t:t + 1], None, ALU.mult).then_inc(xn_ready, 1)
                if t >= 1:
                    copy_wide(("x", t - 1), hT, gmixT)
            copy_wide(("x", NT - 1), hT, gmixT)
            dve.wait_ge(small_in, 16 * 11)
            for c in (0, 2):
                last = nc.vector.tensor_scalar(gains[:, c:c + 1], gains[:, c:c + 1], HEAD_DIM ** -0.5, None, ALU.mult)
            last.then_inc(setup_done, 1)
            for g in range(NG):
                for h in range(2):
                    dve.wait_ge(vec_psum, 2 * g + h + 1)
                    last = nc.vector.tensor_copy(vec[:, g * DIST + h * (DIST // 2):g * DIST + (h + 1) * (DIST // 2)], psS[h][0:HG, 0:DIST // 2])
                    last.then_inc(vec_free, 1)
            dve.wait_ge(f_psum, 1)
            dve.wait_ge(forget_in, 32)
            link(nc.vector.tensor_scalar(fx, psV[0:HB, :], bforget[:, 0:1], None, ALU.add))
            nc.vector.scalar_tensor_tensor(fa, fx, -1.0, fx, ALU.mult, ALU.max).then_inc(f_abs, 1)
            dve.wait_ge(f_ln, 1)
            link(nc.vector.scalar_tensor_tensor(fx, fx, 0.0, fl, ALU.min, ALU.subtract))
            link(nc.vector.memset(fl, 1.0))
            link(nc.vector.tensor_tensor_scan(fa, fl, fx, 0.0, ALU.mult, ALU.add))
            nc.vector.tensor_scalar(fe, fa, -1.0, None, ALU.mult).then_inc(negc_ready, 1)
            dve.wait_ge(cq_psum, 1)
            nc.vector.tensor_copy(cq[:], psV[:, 0:NT * HB].rearrange("p (t h) -> p t h", t=NT)).then_inc(y_norm, 1)

            def dense(n):
                if not makes_qk(n):
                    return
                ps = psD[n % 2]
                s = n % 2
                rows[0] += 1
                dve.wait_ge(squared, NT + rows[0])
                nc.vector.tensor_reduce(sumsq[:, s, :], sq[:, 0:COLS].rearrange("p (h d) -> p h d", d=HEAD_DIM), AX.X, ALU.add).then_inc(summed, 1)
                dve.wait_ge(summed, rows[0])
                mean_of(mean[:, s, :], sumsq[:, s, :], HEAD_DIM)
                if n >= 2 and makes_qk(n - 2):
                    b, c = order[("qk", n - 2)]
                    dve.wait_ge(tr_ready[b], c + 1)
                nc.vector.tensor_tensor(qkrow[s].rearrange("p (h d) -> p h d", d=HEAD_DIM), ps[:].rearrange("p (h d) -> p h d", d=HEAD_DIM),
                                        rnorm[:, s, :].unsqueeze(2).broadcast_to([P, HB, HEAD_DIM]), ALU.mult).then_inc(dense_used[s], 1)

            rows = [0]
            for n in range(A_UNITS):
                dense(n)

            def copy_p(key, dst):
                b, c = order[key]
                dve.wait_ge(tr_ready[b], c + 1)
                nc.vector.tensor_copy(dst, psT[b][:, 0:dst.shape[1] * P].rearrange("p (b q) -> p b q", q=P)).then_inc(tr_used[b], 1)

            def maxima(buf, n, sizes):
                c0 = 0
                for s, w in enumerate(sizes):
                    last = nc.vector.reduce_max(rowmax[:, n % 2, s:s + 1], buf[:, c0:c0 + w], AX.X)
                    c0 += w
                link(last)
                nc.vector.tensor_scalar(negmax[:, n % 2, 0:len(sizes)], rowmax[:, n % 2, 0:len(sizes)], -1.0, None, ALU.mult).then_inc(scores_ready, 1)

            dve.wait_ge(bias_in, 16 * HA)
            for u in range(UA + 1):
                if u < UA:
                    h, i = u // NT, u % NT
                    dve.wait_ge(scores_psum, u + 1)
                    if u >= 2:
                        dve.wait_ge(pv_psum, u - 1)
                    c0 = 0
                    for g, (b0, b1) in enumerate(key_blocks_a(u)):
                        w = P * (b1 - b0)
                        u0 = P * (b0 - i) + N - P
                        last = nc.vector.tensor_tensor(sc_a[u % 2][:, c0:c0 + w], psS[g][:, 0:w], bias[:, g * HG + h, u0:u0 + w], ALU.add)
                        c0 += w
                    link(last)
                    maxima(sc_a[u % 2], u, [c0])
                if u >= 1:
                    nb = len(blocks_a(u - 1))
                    if nb > 4:
                        copy_p(("pa", u - 1, 1), pT_a[(u - 1) % 2][:, 4:min(8, nb), :])
                    dve.wait_ge(exp_ready, u)
                    link(nc.vector.reciprocal(rowinv[:, (u - 1) % 2, 0:1], rowsum[:, (u - 1) % 2, 0:1]))
                    n = A_UNITS + u - 1
                    if n < B_UNITS:
                        dense(n)
                    dve.wait_ge(pv_psum, u)
                    h, i = (u - 1) // NT, (u - 1) % NT
                    nc.vector.tensor_scalar(yrow_a[:, i, h * HEAD_DIM:(h + 1) * HEAD_DIM], psV[:, 0:HEAD_DIM], rowinv[:, (u - 1) % 2, 0:1], None,
                                            ALU.mult).then_inc(y_norm, 1)
            for v in range(UB + 1):
                if v < UB:
                    h = v // 2
                    dve.wait_ge(scores_psum, UA + v + 1)
                    dve.wait_ge(negc_in[h // 2], 16)
                    if v >= 2:
                        dve.wait_ge(pv_psum, UA + v - 1)
                    c0 = 0
                    for s, i in enumerate(tiles_b(v)):
                        w = P * (i + 1)
                        last = nc.vector.scalar_tensor_tensor(sc_b[v % 2][:, c0:c0 + w], psS[s][:, 0:w], cq[:, i, h:h + 1], negc[:, h, 0:w],
                                                              ALU.add, ALU.add)
                        c0 += w
                    link(last)
                    maxima(sc_b[v % 2], v, [P * (i + 1) for i in tiles_b(v)])
                if v >= 1:
                    copy_p(("pb", v - 1, 1), pT_b[(v - 1) % 2][:, 4:5, :])
                    dve.wait_ge(exp_ready, UA + v)
                    link(nc.vector.reciprocal(rowinv[:, (v - 1) % 2, :], rowsum[:, (v - 1) % 2, :]))
                    dve.wait_ge(pv_psum, UA + v)
                    h = (v - 1) // 2
                    for s, i in enumerate(tiles_b(v - 1)):
                        last = nc.vector.tensor_scalar(yrow_b[:, i, h * HEAD_DIM:(h + 1) * HEAD_DIM], psV[:, s * HEAD_DIM:(s + 1) * HEAD_DIM],
                                                       rowinv[:, (v - 1) % 2, s:s + 1], None, ALU.mult)
                    last.then_inc(y_norm, 1)
            for r in range(6):
                b, c = order[("y", r)]
                dve.wait_ge(tr_ready[b], c + 1)
                nc.vector.tensor_copy(yTa[:, r, :] if r < 2 else yTb[:, r - 2, :], psT[b][:]).then_inc(tr_used[b], 1)
            for m in range(ND):
                dve.wait_ge(proj_psum, m + 1)
                dve.wait_ge(sig_ready, 2 * m + 2)
                nc.vector.tensor_tensor(gated[0], psD[m % 2][:], gates[:, m, :], ALU.mult)
                link(nc.vector.tensor_tensor(gated[1], psS[m % 2][:], gates[:, ND + m, :], ALU.mult))
                nc.vector.tensor_tensor(merged[:, m, :], gated[0], gated[1], ALU.add).then_inc(merged_ready, 1)
                dve.wait_ge(merged_ready, m + 1)

            def norm_x1(t):
                dve.wait_ge(squared, NT + rows[0] + t + 1)
                mean_of(hn_ms[:, t:t + 1], hn_ss[:, t:t + 1], D)
                nc.vector.tensor_scalar(hn[:, t, :], xres[:, t, :], hn_r[:, t:t + 1], None, ALU.mult).then_inc(hn_ready, 1)

            for t in range(NT):
                for h in range(2):
                    dve.wait_ge(out_psum, 2 * t + h + 1)
                    nc.vector.tensor_tensor(xres[:, t, h * 512:(h + 1) * 512], psD[h][:], xres[:, t, h * 512:(h + 1) * 512], ALU.add).then_inc(x1_ready, 1)
                norm_x1(t)
                if t >= 1:
                    copy_wide(("h", t - 1), h2T, gffnT)
            for t in range(NT):
                nc.vector.tensor_copy(table[:, t, :, 0], cst[:, 4 * P + t:4 * P + t + 1].broadcast_to([P, E]))
                nc.vector.tensor_copy(table[:, t, :, 1], cst[:, 4 * P + NT:4 * P + NT + 1].broadcast_to([P, E]))
            nc.vector.memset(table[:, :, :, 2:3], 1.0)
            copy_wide(("h", NT - 1), h2T, gffnT)
            dve.wait_ge(scores_sig, 1)
            link(nc.vector.tensor_tensor(sel, scores, rbias[:, :].unsqueeze(1).broadcast_to([P, NT, E]), ALU.add))
            for t in range(NT):
                last = nc.vector.max(m8[:, t, :], sel[:, t, :])
            link(last)
            for t in range(NT):
                last = nc.vector.match_replace(rep[:, t, :], m8[:, t, :], sel[:, t, :], NEVER)
            link(last)
            link(nc.vector.tensor_tensor(M, rep, sel, ALU.not_equal))
            nc.vector.tensor_copy(Mb, M).then_inc(mask_ready, 1)
            link(nc.vector.tensor_tensor(gt, M, scores, ALU.mult))
            link(nc.vector.tensor_reduce(gsum[:], gt, AX.X, ALU.add))
            link(nc.vector.reciprocal(ginv[:], gsum[:]))
            for t in range(NT):
                last = nc.vector.tensor_scalar(gt[:, t, :], gt[:, t, :], ginv[:, t:t + 1], ROUTE_SCALE, ALU.mult, ALU.mult)
            link(last)
            link(nc.vector.tensor_copy(table[:, :, :, 3], gt))
            link(nc.vector.tensor_tensor(gres, gt, table[:, :, :, 3], ALU.subtract))
            link(nc.vector.tensor_copy(table[:, :, :, 4], gres))
            link(nc.vector.tensor_tensor(gt, gres, table[:, :, :, 4], ALU.subtract))
            nc.vector.tensor_copy(table[:, :, :, 5], gt)
            dve.wait_ge(counts_psum, 1)
            link(nc.vector.tensor_tensor(gres, psI[:, 0:NT * E].rearrange("p (t e) -> p t e", t=NT), M, ALU.mult))
            link(nc.vector.tensor_scalar(pos, gres, -1.0, None, ALU.add))
            link(nc.vector.reduce_max(cmax[:], psM[:, 0:E], AX.X))
            link(nc.vector.tensor_scalar(over[:, 0:ROUNDS - 1], thresholds, cmax[:, 0:1], None, ALU.is_lt))
            link(nc.vector.reduce_sum(oround[:], over[:, 0:ROUNDS - 1], AX.X))
            nc.vector.tensor_copy(rounds_i[:], oround[:]).then_inc(routed, 1)

            def make_onehot(n, e):
                col = pos[:, :, bass.ds(e, 1)]
                return nc.vector.tensor_tensor(onehot[n][:, :, 0:SLOTS], iota_b[:, 0:SLOTS].unsqueeze(1).broadcast_to([P, NT, SLOTS]),
                                               col.broadcast_to([P, NT, SLOTS]), ALU.is_equal)

            def read_idx(slot, done):
                nc.vector.tensor_scalar(idxg[slot][0:SLOTS, :], psI[0:SLOTS, 0:1], psI[0:SLOTS, 1:2], float(NO_TOKEN), ALU.add, ALU.add)
                nc.vector.tensor_scalar(gate[0:SLOTS, slot:slot + 1], psI[0:SLOTS, 3:4], psI[0:SLOTS, 4:5], psI[0:SLOTS, 5:6], ALU.add, ALU.add).then_inc(done, 1)

            def copy_xT(n):
                h = ND // 2
                for c in range(2):
                    last = nc.vector.tensor_tensor(xT[n][:, c * h:(c + 1) * h, 0:SLOTS], psT[c][:].rearrange("p (j s) -> p j s", j=h)[:, :, 0:SLOTS],
                                                   gffnT[:, c * h:(c + 1) * h].unsqueeze(2).broadcast_to([P, h, SLOTS]), ALU.mult)
                return last

            def times_up(n, rows_, g):
                return nc.vector.scalar_tensor_tensor(mid[n][0:rows_, :], silu[n][0:rows_, :], g, psG[n][0:rows_, F:2 * F], ALU.mult, ALU.mult)

            def onehot_k(k, n):
                after(dve, idx_psum, k - 1)
                make_onehot(n, k).then_inc(onehot_ready, 1)

            def idx_k(k, slot):
                dve.wait_ge(idx_psum, k + 1)
                read_idx(slot, idx_ready)

            def xT_k(k, n):
                dve.wait_ge(xT_psum, k + 1)
                after(dve, gu_psum, SH + k - 1)
                copy_xT(n).then_inc(xT_ready, 1)

            def mid_i(it, n, rows_, g):
                dve.wait_ge(silu_ready, it + 1)
                after(dve, midT_psum, it - 1)
                times_up(n, rows_, g).then_inc(mid_ready, 1)

            def y_shared(t):
                if t >= 2:
                    dve.wait_ge(based[t % 2], 16 * (t // 2))
                for h in range(2):
                    dve.wait_ge(y_psum, 2 * t + h + 1)
                    nc.vector.tensor_tensor(y[t % 2][:, h * 512:(h + 1) * 512], psY[h][:], xres[:, t, h * 512:(h + 1) * 512], ALU.add).then_inc(y_ready, 1)

            dve.wait_ge(routed, 1)
            onehot_k(0, 0)
            for it in range(SH):
                mid_i(it, it % 2, P, 1.0)
                if it >= 1:
                    y_shared(it - 1)
                if it == SH - 1:
                    xT_k(0, 0)
                idx_k(it, it)
                onehot_k(it + 1, (it + 1) % 2)

            def expert(k, u, ix=True, oh=True, xt=True):
                dve.wait_ge(idx_ready, k + 1)
                mid_i(SH + k, u % 2, SLOTS, gate[0:SLOTS, u:u + 1])
                if xt:
                    xT_k(k + 1, (u + 1) % 2)
                if isinstance(k, int) and k == 0:
                    y_shared(SH - 1)
                after(dve, scattered, 16 * (k - 3))
                nc.vector.tensor_copy(idxs[u][0:SLOTS, :], idxg[u][0:SLOTS, :]).then_inc(idx_kept, 1)
                if ix:
                    dve.wait_ge(mid_ready, SH + k + 1)
                    dve.wait_ge(idx_kept, k + 1)
                    idx_k(k + 4, u)
                if oh:
                    onehot_k(k + 5, (u + 1) % 2)

            for k in range(4):
                expert(k, k)
            with dve.Fori(1, E // 4 - 2) as m:
                for u in range(4):
                    expert(4 * m + u, u)
            for k in range(E - 8, E):
                expert(k, k % 4, ix=k + 4 < E, oh=k + 5 < E, xt=k + 1 < E)

            more = dve.value_load(rounds_i[0:1, 0:1], min_val=0, max_val=ROUNDS - 1)
            with dve.If(more > 0):
                with dve.Fori(0, more) as r:
                    nc.vector.tensor_scalar(pos, pos, -float(SLOTS), None, ALU.add).then_inc(o_pos, 1)
                    with dve.Fori(0, E) as e:
                        it = r * E + e
                        dve.wait_ge(o_pos, r + 1)
                        make_onehot(0, e).then_inc(o_onehot, 1)
                        dve.wait_ge(o_idx_psum, it + 1)
                        read_idx(0, o_idx)
                        dve.wait_ge(o_xT_psum, it + 1)
                        copy_xT(0).then_inc(o_xT, 1)
                        dve.wait_ge(o_silu, it + 1)
                        times_up(0, SLOTS, gate[0:SLOTS, 0:1]).then_inc(o_mid, 1)
                        dve.wait_ge(o_scattered, 16 * it + 16)
            with dve.Else():
                pass

        @block.tensor
        def _(pe):
            def transposes(key, parts):
                b, c = order[key]
                after(pe, tr_used[b], c)
                for n, (src, k) in enumerate(parts):
                    last = nc.tensor.transpose(psT[b][0:src.shape[1], n * P:n * P + k], src, ident[0:k, 0:k])
                last.then_inc(tr_ready[b], 1)

            pe.wait_ge(const_in, 32)
            for t in range(NT):
                pe.wait_ge(xn_ready, t + 1)
                for b in range(2):
                    transposes(("x", t, b), [(xn[t % 2][:, j::ND], P) for j in range(b * ND // 2, (b + 1) * ND // 2)])
            for b in range(2):
                pe.wait_ge(tr_used[b], NT)
            pe.wait_ge(forget_in, 32)
            for j in range(ND):
                last = nc.tensor.matmul(psV[0:HB, :], wf[:, j, :], hT[:, j, :], start=(j == 0), stop=(j == ND - 1))
            last.then_inc(f_psum, 1)
            pe.wait_ge(table_in, 32)
            pe.wait_ge(setup_done, 1)
            for g in range(NG):
                for h in range(2):
                    after(pe, vec_free, 2 * (g - 1) + h + 1)
                    nc.tensor.matmul(psS[h][0:HG, 0:DIST // 2], relb[:, g * HG:(g + 1) * HG],
                                     table_b[:, g * DIST + h * (DIST // 2):g * DIST + (h + 1) * (DIST // 2)], start=True, stop=True).then_inc(vec_psum, 1)

            def dense(n):
                after(pe, dense_used[n % 2], n // 2)
                c = n // NT if n < B_UNITS else NIN + (n - B_UNITS) // (COLS // P)
                w = ring[c % 3]
                pe.wait_ge(chunk_in[c % 3], 16 * (c // 3 + 1))
                for j in range(ND):
                    if n < B_UNITS:
                        cols = in_chunks[c][2]
                        last = nc.tensor.matmul(psD[n % 2][:, 0:cols], hT[:, j, n % NT * P:(n % NT + 1) * P], w[:, j, 0:cols],
                                                start=(j == 0), stop=(j == ND - 1))
                    else:
                        m = (n - B_UNITS) % (COLS // P)
                        last = nc.tensor.matmul(psD[n % 2][:], w[:, j, m * P:(m + 1) * P], hT[:, j, :], start=(j == 0), stop=(j == ND - 1))
                last.then_inc(dense_ready, 1)

            def transpose_qk(n):
                pe.wait_ge(qkrow_done(n)[0], qkrow_done(n)[1])
                transposes(("qk", n), [(qkrow[n % 2][:, i * P:(i + 1) * P], P) for i in range(4)])

            def qkrow_done(n):
                return dense_used[n % 2], n // 2 + 1

            for n in range(A_UNITS):
                dense(n)
                if makes_qk(n - 1):
                    transpose_qk(n - 1)
                if n == 0:
                    pe.wait_ge(negc_ready, 1)
                    for t in range(NT):
                        last = nc.tensor.transpose(psV[:, t * HB:(t + 1) * HB], fa[:, t * P:(t + 1) * P], ident[0:HB, 0:HB])
                    last.then_inc(cq_psum, 1)

            def scores_a(u):
                h, i = u // NT, u % NT
                after(pe, scores_ready, u)
                for g, (b0, b1) in enumerate(key_blocks_a(u)):
                    head = g * HG + h
                    rows = slice(head % 2 * HEAD_DIM, (head % 2 + 1) * HEAD_DIM)
                    last = nc.tensor.matmul(psS[g][:, 0:P * (b1 - b0)], qTa[rows, head // 2, i * P:(i + 1) * P],
                                            kTa[rows, head // 2, b0 * P:b1 * P], start=True, stop=True)
                last.then_inc(scores_psum, 1)

            def transpose_pa(u):
                pe.wait_ge(exp_ready, u + 1)
                nb = len(blocks_a(u))
                for r in range(-(-nb // 4)):
                    transposes(("pa", u, r), [(sc_a[u % 2][:, b * P:(b + 1) * P], P) for b in range(4 * r, min(4 * r + 4, nb))])

            def weighted_a(u):
                h = u // NT
                found = blocks_a(u)
                for r in range(-(-len(found) // 4)):
                    b, c = order[("pa", u, r)]
                    pe.wait_ge(tr_used[b], c + 1)
                after(pe, y_norm, u + 1)
                for n, (g, b) in enumerate(found):
                    head = g * HG + h
                    last = nc.tensor.matmul(psV[:, 0:HEAD_DIM], pT_a[u % 2][:, n, :], va[:, b, head * HEAD_DIM:(head + 1) * HEAD_DIM],
                                            start=(n == 0), stop=(n == len(found) - 1))
                last.then_inc(pv_psum, 1)

            for u in range(UA + 1):
                n = A_UNITS + u - 1
                if u == 0:
                    pe.wait_ge(vec_free, 2 * NG)
                    for b in range(2):
                        pe.wait_ge(dense_used[b], A_UNITS // 2)
                        pe.wait_ge(tr_used[b], max(c + 1 for (k, *r), (bb, c) in order.items() if k == "qk" and bb == b and r[0] < A_UNITS))
                if u < UA:
                    scores_a(u)
                if u >= 1:
                    transpose_pa(u - 1)
                    if makes_qk(n - 1):
                        transpose_qk(n - 1)
                    if n < B_UNITS:
                        dense(n)
                    weighted_a(u - 1)

            def scores_b(v):
                h = v // 2
                rows = slice(h % 2 * HEAD_DIM, (h % 2 + 1) * HEAD_DIM)
                after(pe, scores_ready, UA + v)
                for s, i in enumerate(tiles_b(v)):
                    nc.tensor.matmul(psS[s][:, 0:P * (i + 1)], qTb[rows, h // 2, i * P:(i + 1) * P], kTb[rows, h // 2, 0:(i + 1) * P],
                                     start=True, stop=False)
                    last = nc.tensor.matmul(psS[s][:, i * P:(i + 1) * P], ident_b[:], mask_b[:], start=False, stop=True)
                last.then_inc(scores_psum, 1)

            def weighted_b(v):
                h = v // 2
                for r in range(2):
                    b, c = order[("pb", v, r)]
                    pe.wait_ge(tr_used[b], c + 1)
                pe.wait_ge(y_norm, UA + v + 1)
                found = blocks_b(v)
                for n, (i, b) in enumerate(found):
                    s = tiles_b(v).index(i)
                    last = nc.tensor.matmul(psV[:, s * HEAD_DIM:(s + 1) * HEAD_DIM], pT_b[v % 2][:, n, :], vb[:, b, h * HEAD_DIM:(h + 1) * HEAD_DIM],
                                            start=(b == 0), stop=(b == i))
                last.then_inc(pv_psum, 1)

            for b in range(2):
                pe.wait_ge(dense_used[b], B_UNITS // 2)
                pe.wait_ge(tr_used[b], max(c + 1 for (k, *r), (bb, c) in order.items() if k in ("qk", "pa") and bb == b))
            for v in range(UB + 1):
                if v < UB:
                    scores_b(v)
                if v >= 1:
                    pe.wait_ge(exp_ready, UA + v)
                    for r, (b0, b1) in enumerate(((0, 4), (4, 5))):
                        transposes(("pb", v - 1, r), [(sc_b[(v - 1) % 2][:, b * P:(b + 1) * P], P) for b in range(b0, b1)])
                    dense(B_UNITS + v - 1)
                    weighted_b(v - 1)
            pe.wait_ge(y_norm, UA + UB + 1)
            for r in range(6):
                rows, c = (yrow_a, r) if r < 2 else (yrow_b, r - 2)
                transposes(("y", r), [(rows[:, t, c * P:(c + 1) * P], P) for t in range(NT)])
            for b in range(2):
                pe.wait_ge(tr_used[b], order[("y", 4 + b)][1] + 1)
                pe.wait_ge(dense_used[b], G_UNITS // 2)
            pe.wait_ge(proj_in, 16 * 5)
            for m in range(ND):
                after(pe, merged_ready, m - 1)
                for j in range(2):
                    nc.tensor.matmul(psD[m % 2][:], wpa[:, j, m * P:(m + 1) * P], yTa[:, j, :], start=(j == 0), stop=(j == 1))
                for j in range(4):
                    last = nc.tensor.matmul(psS[m % 2][:], wpb[j][:, m * P:(m + 1) * P], yTb[:, j, :], start=(j == 0), stop=(j == 3))
                last.then_inc(proj_psum, 1)
            def transpose_h(t):
                pe.wait_ge(hn_ready, t + 1)
                for b in range(2):
                    transposes(("h", t, b), [(hn[:, t, j::ND], P) for j in range(b * ND // 2, (b + 1) * ND // 2)])

            pe.wait_ge(merged_ready, ND)
            for i in range(2):
                pe.wait_ge(wout_in[i], 16)
            for t in range(NT):
                for h in range(2):
                    after(pe, x1_ready, 2 * (t - 1) + h + 1)
                    for j in range(ND):
                        last = nc.tensor.matmul(psD[h][:], merged[:, j, t * P:(t + 1) * P], wout[:, j, h * 512:(h + 1) * 512],
                                                start=(j == 0), stop=(j == ND - 1))
                    last.then_inc(out_psum, 1)
                if t >= 1:
                    transpose_h(t - 1)
            transpose_h(NT - 1)
            pe.wait_ge(router_in, 16)
            for b in range(2):
                pe.wait_ge(tr_used[b], uses[b])
            for t in range(NT):
                for j in range(ND):
                    last = nc.tensor.matmul(psI[:, t * E:(t + 1) * E], h2T[:, j, t * P:(t + 1) * P], wr[:, j, :], start=(j == 0), stop=(j == ND - 1))
            last.then_inc(logits_psum, 1)

            def gate_up(n, rows, lhs, slot):
                for j in range(ND):
                    last = nc.tensor.matmul(psG[n][0:rows, :], lhs[:, j, 0:rows], wgu[slot][:, j, :], start=(j == 0), stop=(j == ND - 1))
                return last

            def transpose_mid(n, rows):
                for j in range(NF):
                    last = nc.tensor.transpose(psM[:, j * P:j * P + rows], mid[n][0:rows, j::NF], ident[0:rows, 0:rows])
                return last

            def down(n, h, rows, slot):
                for j in range(NF):
                    last = nc.tensor.matmul(psY[h][0:rows, :], midT[n][:, j, 0:rows], wd[slot][:, j, h * 512:(h + 1) * 512],
                                            start=(j == 0), stop=(j == NF - 1))
                return last

            def find_slots(n, e):
                for t in range(NT):
                    last = nc.tensor.matmul(psI[0:SLOTS, 0:6], onehot[n][:, t, 0:SLOTS], table[:, t, bass.ds(e, 1), :].rearrange("p a b -> p (a b)"),
                                            start=(t == 0), stop=(t == NT - 1))
                return last

            def transpose_rows(slot):
                for j in range(ND):
                    c = j % (ND // 2) * P
                    last = nc.tensor.transpose(psT[j // (ND // 2)][:, c:c + SLOTS], xg[slot][0:SLOTS, j::ND], ident[0:SLOTS, 0:SLOTS])
                return last

            def is_shared(it):
                return isinstance(it, int) and it < SH

            def up_i(it, n, slot):
                after(pe, mid_ready, it - 1)
                if is_shared(it):
                    pe.wait_ge(shared_in, 48)
                    gate_up(n, P, h2T[:, :, it * P:(it + 1) * P], 3).then_inc(gu_psum, 1)
                else:
                    for k in range(2):
                        pe.wait_ge(w_in_sem[slot][k], lands(it - SH, 16, slot))
                    pe.wait_ge(xT_ready, it - SH + 1)
                    gate_up(n, SLOTS, xT[n], slot).then_inc(gu_psum, 1)

            def down_i(it, n, slot):
                pe.wait_ge(midT_ready, it + 1)
                if not is_shared(it):
                    pe.wait_ge(w_in_sem[slot][2], lands(it - SH, 16, slot))
                for h in range(2):
                    after(pe, y_ready, 2 * (it - 1) + h + 1)
                    down(n, h, P if is_shared(it) else SLOTS, 3 if is_shared(it) else slot).then_inc(y_psum, 1)

            def step(it, u, xt=True, ix=True):
                n = u % 2
                up_i(it, n, u)
                if xt:
                    k, slot = it + 1 - SH, (u + 1) % 4
                    pe.wait_ge(gathered[slot], lands(k, 16, slot))
                    after(pe, xT_ready, k)
                    transpose_rows(slot).then_inc(xT_psum, 1)
                if not (isinstance(it, int) and it == 0):
                    down_i(it - 1, 1 - n, (u - 1) % 4)
                else:
                    pe.wait_ge(mask_ready, 1)
                    pe.wait_ge(scores_sig, 1)
                    for t in range(NT):
                        for s in range(t + 1):
                            nc.tensor.matmul(psI[:, t * E:(t + 1) * E], tri_b[:] if s == t else ones_b[:], Mb[:, s, :], start=(s == 0), stop=(s == t))
                    for t in range(NT):
                        last = nc.tensor.matmul(psM[:, 0:E], ones_b[:], Mb[:, t, :], start=(t == 0), stop=(t == NT - 1))
                    last.then_inc(counts_psum, 1)
                    pe.wait_ge(routed, 1)
                pe.wait_ge(mid_ready, it + 1)
                after(pe, midT_ready, it)
                transpose_mid(n, P if is_shared(it) else SLOTS).then_inc(midT_psum, 1)
                if ix:
                    pe.wait_ge(onehot_ready, it + 1)
                    after(pe, idx_ready, it)
                    find_slots(n, it).then_inc(idx_psum, 1)

            for it in range(SH + 4):
                step(it, it % 4, xt=it + 1 >= SH)
            with pe.Fori(2, ITEMS // 4 - 1) as m:
                for u in range(4):
                    step(4 * m + u, u)
            for it in range(ITEMS - 4, ITEMS):
                step(it, it % 4, xt=it + 1 < ITEMS, ix=False)
            down_i(ITEMS - 1, 1, 3)

            more = pe.value_load(rounds_i[0:1, 0:1], min_val=0, max_val=ROUNDS - 1)
            with pe.If(more > 0):
                pe.wait_ge(scattered, 16 * E)
                with pe.Fori(0, more * E) as it:
                    nc.tensor.matmul(psM[0:1, 0:1], ident_b[:, 0:1], ident_b[:, 0:1], start=True, stop=True).then_inc(o_free, 1)
                    pe.wait_ge(o_onehot, it + 1)
                    find_slots(0, it % E).then_inc(o_idx_psum, 1)
                    pe.wait_ge(o_gathered, 16 * it + 16)
                    transpose_rows(0).then_inc(o_xT_psum, 1)
                    pe.wait_ge(o_xT, it + 1)
                    for k in range(2):
                        pe.wait_ge(w_in_sem[0][k], 4 * E + 16 * it + 16)
                    gate_up(0, SLOTS, xT[0], 0).then_inc(o_gu, 1)
                    pe.wait_ge(o_mid, it + 1)
                    transpose_mid(0, SLOTS).then_inc(o_midT_psum, 1)
                    pe.wait_ge(o_midT, it + 1)
                    pe.wait_ge(w_in_sem[0][2], 4 * E + 16 * it + 16)
                    down(0, 0, SLOTS, 0)
                    down(0, 1, SLOTS, 0).then_inc(o_y_psum, 1)
                    pe.wait_ge(o_y, it + 1)
            with pe.Else():
                pass


_INS = ["x", "g_mix", "w_in", "q_norm_a", "k_norm_a", "q_norm_b", "k_norm_b", "rel_bias", "b_forget", "w_gate", "b_gate",
        "w_proj_a", "w_proj_b", "w_out", "g_ffn", "w_router", "router_bias", "w_gate_e", "w_up_e", "w_down_e",
        "w_gate_s", "w_up_s", "w_down_s"]


def shape_constants():
    tiles = SEQ // P
    rounds = -(-SEQ // SLOTS)
    c = np.zeros((P, 4 * P + tiles + 1 + rounds), np.float32)
    c[:, 0:P] = np.eye(P)
    c[:, P:2 * P] = np.arange(P)[None]
    c[:, 2 * P:3 * P] = np.triu(np.ones((P, P)))
    c[:, 3 * P:4 * P] = np.triu(np.full((P, P), MASKED), 1)
    c[:, 4 * P:4 * P + tiles] = np.arange(tiles)[None] * P - NO_TOKEN
    c[:, 4 * P + tiles] = np.arange(P)
    c[:, 4 * P + tiles + 1:] = SLOTS * np.arange(1, rounds + 1)[None]
    dist = SEQ - 1 - np.arange(DIST)
    exact = REL_BUCKETS // 2
    n = np.maximum(dist, 1).astype(np.float32)
    large = exact + (np.log(n / np.float32(exact)) / np.float32(math.log(REL_MAX_DIST / exact)) * np.float32(REL_BUCKETS - exact)).astype(np.int32)
    bucket = np.where(dist < exact, dist, np.minimum(large, REL_BUCKETS - 1))
    table = np.zeros((REL_BUCKETS + 1, len(DIL_GROUPS), DIST), np.float32)
    for g, (window, step) in enumerate(DIL_GROUPS):
        seen = (dist >= 0) & (dist <= window) & (dist % step == 0)
        for b in range(REL_BUCKETS):
            table[b, g] = seen & (bucket == b)
        table[REL_BUCKETS, g] = np.where(seen, 0.0, MASKED)
    return c, table.reshape(REL_BUCKETS + 1, -1)


def kernel(**inputs):
    import concourse.bacc as bacc
    from concourse import mybir as mb
    from concourse.bass_utils import run_bass_kernel_spmd as run

    nc = bacc.Bacc("TRN2", target_bir_lowering=False, num_devices=1)
    consts, bias_table = shape_constants()
    given = {name: np.ascontiguousarray(inputs[name]) for name in _INS}
    given["b_gate"] = np.ascontiguousarray(given["b_gate"].reshape(-1, P).T)
    given |= {"consts": consts, "bias_table": bias_table}
    args = [nc.dram_tensor(f"in_{name}", a.shape, mb.dt.from_np(a.dtype), kind="ExternalInput").ap() for name, a in given.items()]
    out = nc.dram_tensor("out_0", given["x"].shape, mb.dt.float32, kind="ExternalOutput").ap()
    layer(nc, *args, out)
    r = run(nc, [{f"in_{name}": a for name, a in given.items()}], core_ids=[0])
    return r.results[0]["out_0"]
```

```python
import math
from contextlib import ExitStack

import numpy as np
import concourse.bass as bass
from concourse import mybir

P = 128
HEAD_DIM = 64
DIL_GROUPS = ((128, 1), (512, 4), (2048, 16))
HEADS_PER_GROUP = 4
REL_BUCKETS, REL_MAX_DIST = 32, 2048
TOP_K = 8
ROUTE_SCALE = 2.5
EPS = 1e-6
MASKED = -1e30
NEVER = -3e38
SLOTS = 96
NO_TOKEN = 1024
SEQ = 512
DIST = SEQ + P


def layer(nc, x, g_mix, w_in, q_norm_a, k_norm_a, q_norm_b, k_norm_b, rel_bias, b_forget, w_gate, b_gate,
          w_proj_a, w_proj_b, w_out, g_ffn, w_router, router_bias, w_gate_e, w_up_e, w_down_e,
          w_gate_s, w_up_s, w_down_s, consts, bias_table, out):
    f32, bf16, i32, u32 = mybir.dt.float32, mybir.dt.bfloat16, mybir.dt.int32, mybir.dt.uint32
    ALU, ACT, AX = mybir.AluOpType, mybir.ActivationFunctionType, mybir.AxisListType
    E, D, F = w_gate_e.shape
    N = x.shape[1]
    x_rows, out_rows = x[0], out[0]
    NT, ND, NF = N // P, D // P, F // P
    HG = HEADS_PER_GROUP
    NG = len(DIL_GROUPS)
    HA, HB = HG * NG, b_forget.shape[0]
    WA, WB = HA * HEAD_DIM, HB * HEAD_DIM
    COLS = 512
    HALF = ND // 2
    RING = ND + HALF
    ROUNDS = -(-N // SLOTS)
    SH = NT
    ITEMS = SH + E

    hn_dram = nc.dram_tensor("hn_dram", [N, D], f32, kind="Internal").ap()
    vec_dram = nc.dram_tensor("vec_dram", [HA, P, DIST], f32, kind="Internal")
    negc_dram = nc.dram_tensor("negc_dram", [HB, N], f32, kind="Internal").ap()

    in_chunks = [("qk", 0, COLS), ("qk", COLS, COLS), ("qk", 2 * COLS, COLS), ("va", 3 * COLS, COLS),
                 ("va", 4 * COLS, 3 * WA - 4 * COLS), ("qb", 3 * WA, WB), ("kb", 3 * WA + WB, WB), ("vb", 3 * WA + 2 * WB, WB)]
    NIN = len(in_chunks)
    NCHUNK = NIN + 2 * D // COLS
    A_UNITS, B_UNITS, G_UNITS = 5 * NT, NIN * NT, NIN * NT + 2 * D // P
    O_UNITS = G_UNITS + D // COLS * NT
    unit_kind = lambda n: in_chunks[n // NT][0] if n < B_UNITS else "gate"
    makes_qk = lambda n: 0 <= n < B_UNITS and unit_kind(n) in ("qk", "qb", "kb")
    UA, UB = HG * NT, HB * 2

    def key_blocks_a(u):
        i = u % NT
        return [(0 if g else max(0, i - 1), i + 1) for g in range(NG)]

    def blocks_a(u):
        return [(g, b) for g, (b0, b1) in enumerate(key_blocks_a(u)) for b in range(b0, b1)]

    def tiles_b(v):
        return (v % 2, NT - 1 - v % 2)

    def blocks_b(v):
        return [(i, b) for i in tiles_b(v) for b in range(i + 1)]

    uses, order = [0, 0], {}

    def number(key, bank):
        order[key] = (bank, uses[bank])
        uses[bank] += 1

    for t in range(NT):
        for b in range(2):
            number(("x", t, b), b)
    for n in range(A_UNITS):
        if makes_qk(n - 1):
            number(("qk", n - 1), n % 2)
    for u in range(UA + 1):
        if u >= 1:
            for r in range(-(-len(blocks_a(u - 1)) // 4)):
                number(("pa", u - 1, r), r % 2)
            if makes_qk(A_UNITS + u - 2):
                number(("qk", A_UNITS + u - 2), 1)
    for v in range(1, UB + 1):
        for r in range(2):
            number(("pb", v - 1, r), r)
    for r in range(2 + 4):
        number(("y", r), r % 2)
    for t in range(NT):
        for b in range(2):
            number(("h", t, b), b)

    ctx = ExitStack()
    with ctx:
        def sb(name, shape, dt=f32):
            return ctx.enter_context(nc.sbuf_tensor(name, shape, dt))

        def sem(name):
            return ctx.enter_context(nc.semaphore(name))

        cst = sb("cst", [P, 4 * P + NT + 1 + ROUNDS])
        ident = cst[:, 0:P]
        thresholds = cst[:, 4 * P + NT + 1:4 * P + NT + ROUNDS]
        iota_b, tri_b, mask_b, ident_b, ones_b = (sb(n, [P, P], bf16) for n in ("iota_b", "tri_b", "mask_b", "ident_b", "ones_b"))
        gmixT, gffnT, bgateT = sb("gmixT", [P, ND]), sb("gffnT", [P, ND]), sb("bgateT", [P, 2 * D // P])
        gains = sb("gains", [P, 4])
        bforget = sb("bforget", [HB, 1])
        relb = sb("relb", [REL_BUCKETS + 1, HA])
        wf = sb("wf", [P, ND, HB])
        minus_half = sb("minus_half", [P, HB])
        sumsq = sb("sumsq", [P, 2, HB]); mean = sb("mean", [P, 2, HB]); rnorm = sb("rnorm", [P, 2, HB])
        rowmax = sb("rowmax", [P, 2, 2]); negmax = sb("negmax", [P, 2, 2]); rowsum = sb("rowsum", [P, 2, 2]); rowinv = sb("rowinv", [P, 2, 2])
        cq = sb("cq", [P, NT, HB])
        turn = sb("turn", [16, 1])
        cmax = sb("cmax", [P, 1]); over = sb("over", [P, ROUNDS]); oround = sb("oround", [P, 1]); rounds_i = sb("rounds_i", [P, 1], i32)
        gsum = sb("gsum", [P, NT]); ginv = sb("ginv", [P, NT]); m8 = sb("m8", [P, NT, 8])
        gate = sb("gate", [P, 4])
        idxg = [sb(f"idxg{i}", [P, 1], u32) for i in range(4)]
        idxs = [sb(f"idxs{i}", [P, 1], u32) for i in range(4)]
        hn_ss, hn_ms, hn_r = sb("hn_ss", [P, NT]), sb("hn_ms", [P, NT]), sb("hn_r", [P, NT])
        rbias = sb("rbias", [P, E])

        KB = 256
        arena = sb("arena", [P, 121 * KB])
        with ExitStack() as split_ctx:
            def split(name, blocks):
                return split_ctx.enter_context(nc.sbuf_tensor(name, [P, blocks, N], mybir.dt.float32r))

            hT_hi, hT_lo = split("hT_hi", ND), split("hT_lo", ND)
            w_hi, w_lo = split("w_hi", RING), split("w_lo", RING)
        arena_x = sb("arena_x", [P, 80 * KB])

        def at(kb, cols):
            a, k = (arena, kb) if kb < 121 else (arena_x, kb - 121)
            return a[:, int(k * KB):int(k * KB) + cols]

        raw = [at(8 * i, ND // 2 * COLS).rearrange("p (j c) -> p j c", j=ND // 2) for i in range(4)]
        qTa, kTa = (at(k, HA // 2 * N).rearrange("p (h t) -> p h t", h=HA // 2) for k in (16, 28))
        va = at(40, NT * WA).rearrange("p (t c) -> p t c", t=NT)
        bias_near = at(52, HG * 2 * P).rearrange("p (h u) -> p h u", h=HG)
        bias_far = at(56, (HA - HG) * N).rearrange("p (h u) -> p h u", h=HA - HG)
        qTb, kTb = (at(k, HB // 2 * N).rearrange("p (h t) -> p h t", h=HB // 2) for k in (72, 80))
        vb = at(88, NT * WB).rearrange("p (t c) -> p t c", t=NT)
        sc_a = [at(96 + 5 * i, 10 * P) for i in range(2)]
        pT_a = at(106, 10 * P).rearrange("p (b q) -> p b q", q=P)
        sc_b = [at(96 + 2.5 * i, 5 * P) for i in range(2)]
        pT_b = [at(106 + 2.5 * i, 5 * P).rearrange("p (b q) -> p b q", q=P) for i in range(2)]
        sq = at(111, COLS)
        qkrow = [at(113 + 2 * i, COLS) for i in range(2)]
        yrow_a = at(117, NT * HG * HEAD_DIM).rearrange("p (t c) -> p t c", t=NT)
        xin = [at(16 + 4 * i, D) for i in range(NT)]
        xn = [at(32 + 4 * i, D) for i in range(2)]
        hT = at(72, ND * N).rearrange("p (j t) -> p j t", j=ND)
        fx, fa, fe, fl = (arena[0:HB, (88 + 2 * i) * KB:(88 + 2 * i) * KB + N] for i in range(4))
        table_b = arena[0:REL_BUCKETS + 1, 96 * KB:96 * KB + NG * DIST]
        vec = arena[0:HG, 96 * KB + NG * DIST:96 * KB + 2 * NG * DIST]
        sq_x = at(113, D)
        negc = at(16, HB * N).rearrange("p (h t) -> p h t", h=HB)
        yrow_b = at(32, NT * WB).rearrange("p (t c) -> p t c", t=NT)
        gates = at(40, 2 * D // P * N).rearrange("p (m t) -> p m t", m=2 * D // P)
        wpa = [at(k, D) for k in (101, 111)]
        wpb = [at(4 * i, D) for i in range(4)]
        yTa = at(72, 2 * N).rearrange("p (j t) -> p j t", j=2)
        yTb = at(76, 4 * N).rearrange("p (j t) -> p j t", j=4)
        merged = [at(84 + 2 * i, N) for i in range(2)]
        gated = [at(88 + 2 * i, N) for i in range(2)]
        x1 = [at(k, D) for k in (32, 36, 92, 117)]
        sq_h = at(88, D)
        hn = at(72, NT * D).rearrange("p (t d) -> p t d", t=NT)
        h2T = at(96, ND * N).rearrange("p (j t) -> p j t", j=ND)
        wgu = [at(k, 2 * ND * F).rearrange("p (j c) -> p j c", j=ND) for k in (40, 121, 153, 0)]
        wd = [at(k, NF * D).rearrange("p (j c) -> p j c", j=NF) for k in (56, 137, 169, 64)]
        y = [at(177 + 4 * i, D) for i in range(2)]
        xg = [at(72 + 4 * i, D) for i in range(4)]
        table = at(145, NT * E * 3).bitcast(bf16).rearrange("p (t e c) -> p t e c", t=NT, e=E)
        xT = [at(185 + 4 * i, ND * P).rearrange("p (j s) -> p j s", j=ND) for i in range(2)]
        silu = [at(193 + i, F) for i in range(2)]
        mid = [at(195 + i, F) for i in range(2)]
        midT = [at(197 + i, NF * P).rearrange("p (j s) -> p j s", j=NF) for i in range(2)]
        onehot = [at(199 + i, NT * P // 2).bitcast(bf16).rearrange("p (t s) -> p t s", t=NT) for i in range(2)]
        scores, sel, rep, M, gt, gres = (at(16 + i, NT * E).rearrange("p (t e) -> p t e", t=NT) for i in range(6))
        Mb = at(22, NT * E // 2).bitcast(bf16).rearrange("p (t e) -> p t e", t=NT)
        pos = at(23, NT * E).rearrange("p (t e) -> p t e", t=NT)
        wr = at(112, ND * E).rearrange("p (j e) -> p j e", j=ND)

        bank = [ctx.enter_context(nc.psum_tensor(f"bank{i}", [P, 512], f32)) for i in range(8)]
        psD, psS, psT, psV = bank[0:2], bank[2:5], bank[5:7], bank[7]
        psG, psY, psM, psI = bank[0:2], bank[2:4], bank[4], bank[7]

        x_in = [sem(f"x_in{t}") for t in range(NT)]
        const_in, small_in, table_in, forget_in = sem("const_in"), sem("small_in"), sem("table_in"), sem("forget_in")
        chunk_in = [sem(f"chunk_in{i}") for i in range(2)]
        split_hi, split_lo, half_used = sem("split_hi"), sem("split_lo"), sem("half_used")
        hT_hi_ready, hT_lo_ready = sem("hT_hi_ready"), sem("hT_lo_ready")
        merged_hi = sem("merged_hi")
        vec_free, vec_stored, bias_in = sem("vec_free"), sem("vec_stored"), sem("bias_in")
        vec_psum, negc_ready, negc_stored = sem("vec_psum"), sem("negc_ready"), sem("negc_stored")
        negc_in = [sem(f"negc_in{i}") for i in range(4)]
        cq_psum = sem("cq_psum")
        squared, mean_ready, rnorm_ready = sem("squared"), sem("mean_ready"), sem("rnorm_ready")
        xn_ready, setup_done = sem("xn_ready"), sem("setup_done")
        dense_ready = sem("dense_ready")
        dense_used = [sem(f"dense_used{i}") for i in range(2)]
        summed = sem("summed"); qkrow_ready = sem("qkrow_ready")
        tr_ready = [sem(f"tr_ready{i}") for i in range(2)]
        tr_used = [sem(f"tr_used{i}") for i in range(2)]
        scores_psum, scores_ready, exp_ready = sem("scores_psum"), sem("scores_ready"), sem("exp_ready")
        scores_added = sem("scores_added")
        pv_psum, y_norm = sem("pv_psum"), sem("y_norm")
        f_psum, f_x, f_abs, f_exp, f_ln = sem("f_psum"), sem("f_x"), sem("f_abs"), sem("f_exp"), sem("f_ln")
        proj_in, x1_in = sem("proj_in"), [sem(f"x1_in{t}") for t in range(NT)]
        sig_ready, proj_psum, merged_ready = sem("sig_ready"), sem("proj_psum"), sem("merged_ready")
        added, x1_ready = sem("added"), sem("x1_ready")
        hn_ready, hn_stored = sem("hn_ready"), sem("hn_stored")
        dve_chain, act_chain = sem("dve_chain"), sem("act_chain")
        shared_in, router_in = sem("shared_in"), sem("router_in")
        logits_psum, scores_sig, mask_ready, counts_psum, routed = (
            sem("logits_psum"), sem("scores_sig"), sem("mask_ready"), sem("counts_psum"), sem("routed"))
        w_in_sem = [[sem(f"w_slot{n}_{k}") for k in "gud"] for n in range(4)]
        onehot_ready, idx_psum, idx_ready, idx_kept = sem("onehot_ready"), sem("idx_psum"), sem("idx_ready"), sem("idx_kept")
        gathered = [sem(f"gathered{i}") for i in range(4)]
        xT_psum, xT_ready, gu_psum, silu_ready = sem("xT_psum"), sem("xT_ready"), sem("gu_psum"), sem("silu_ready")
        mid_ready, midT_psum, midT_ready = sem("mid_ready"), sem("midT_psum"), sem("midT_ready")
        y_psum, y_ready = sem("y_psum"), sem("y_ready")
        based = [sem(f"based{i}") for i in range(2)]
        scattered, pool_set, turns = sem("scattered"), sem("pool_set"), sem("turns")
        o_free, o_pos, o_onehot, o_idx_psum, o_idx, o_gathered = (
            sem("o_free"), sem("o_pos"), sem("o_onehot"), sem("o_idx_psum"), sem("o_idx"), sem("o_gathered"))
        o_xT_psum, o_xT, o_gu, o_silu, o_mid, o_midT_psum, o_midT, o_y_psum, o_y, o_scattered = (
            sem(n) for n in ("o_xT_psum", "o_xT", "o_gu", "o_silu", "o_mid", "o_midT_psum", "o_midT", "o_y_psum", "o_y", "o_scattered"))

        def after(eng, s, n):
            if not isinstance(n, int) or n > 0:
                eng.wait_ge(s, n)

        def lands(k, per, slot):
            if isinstance(k, int):
                return per * (k // 4 + 1)
            return (k - slot) * (per // 4) + per

        def chunk_cols(c):
            return in_chunks[c][2] if c < NIN else COLS

        def raw_of(c, j):
            return raw[j // HALF + (2 if c >= NCHUNK else 0)][:, j % HALF, 0:chunk_cols(c)]

        def split_of(t, c, j):
            return t[:, (ND * c + j) % RING, 0:chunk_cols(c)]

        def to_split(n):
            c, t = n // NT + 1, n % NT
            if c == NCHUNK or c >= NCHUNK + D // COLS:
                return []
            return [(c, j) for j in ({0: (0, 1), 1: (2, 3), NT - 1: range(HALF, ND)}.get(t, ()))]

        block = ctx.enter_context(nc.Block())

        @block.sync
        def _(sp):
            for t in range(NT):
                sp.dma_start(xin[t], x_rows[t * P:(t + 1) * P, :]).then_inc(x_in[t], 16)
                if t == 0:
                    sp.dma_start(cst[:], consts).then_inc(const_in, 16)
                    sp.dma_start(gmixT[:], g_mix.rearrange("(p j) -> p j", p=P)).then_inc(const_in, 16)

            def load_half(c, i):
                cols = chunk_cols(c)
                if c < NIN:
                    src = w_in[:, in_chunks[c][1]:in_chunks[c][1] + cols].rearrange("(p j) c -> p j c", p=P)
                elif c < NCHUNK:
                    src = w_gate[:, (c - NIN) * COLS:(c - NIN + 1) * COLS].rearrange("(p j) c -> p j c", p=P)
                else:
                    src = w_out[:, (c - NCHUNK) * COLS:(c - NCHUNK + 1) * COLS].rearrange("(j p) c -> p j c", p=P)
                if c != NCHUNK:
                    after(sp, split_lo, ND * (c - 1) + HALF * (i + 1) if c else 0)
                sp.dma_start(raw[i + (2 if c >= NCHUNK else 0)][:, :, 0:cols], src[:, i * HALF:(i + 1) * HALF, :]).then_inc(chunk_in[i], 16)

            def load_chunk(c):
                for i in range(2):
                    load_half(c, i)

            sp.dma_start(wf[:], w_in[:, 3 * WA + 3 * WB:3 * WA + 3 * WB + HB].rearrange("(p j) h -> p j h", p=P)).then_inc(forget_in, 16)
            load_chunk(0)
            sp.dma_start(bforget[:], b_forget.rearrange("(h o) -> h o", o=1)).then_inc(forget_in, 16)
            for c, g in enumerate((q_norm_a, k_norm_a, q_norm_b, k_norm_b)):
                for half in range(2):
                    sp.dma_start(gains[half * HEAD_DIM:(half + 1) * HEAD_DIM, c:c + 1], g.rearrange("(d o) -> d o", o=1)).then_inc(small_in, 16)
            sp.dma_start(relb[0:REL_BUCKETS, :], rel_bias).then_inc(table_in, 16)
            sp.dma_start(table_b, bias_table).then_inc(table_in, 16)
            load_chunk(1)
            sp.dma_start(bgateT[:], b_gate).then_inc(small_in, 16)
            sp.dma_start(gffnT[:], g_ffn.rearrange("(p j) -> p j", p=P)).then_inc(small_in, 16)
            sp.dma_start(rbias[:], router_bias.rearrange("(o e) -> o e", o=1).broadcast_to([P, E])).then_inc(small_in, 16)
            sp.wait_ge(vec_free, 2 * NG)
            for g in range(NG):
                row = vec[:, g * DIST:(g + 1) * DIST].unsqueeze(1).broadcast_to([HG, P, DIST])
                sp.dma_start(vec_dram.ap()[g * HG:(g + 1) * HG], row).then_inc(vec_stored, 16)
            sp.wait_ge(vec_stored, 16 * NG)
            for head in range(HA):
                w = 2 * P if head < HG else N
                toeplitz = bass.AP(vec_dram, head * P * DIST + P - 1 + N - w, [[DIST - 1, P], [1, w]])
                sp.dma_start(bias_near[:, head, :] if head < HG else bias_far[:, head - HG, :], toeplitz).then_inc(bias_in, 16)
            sp.wait_ge(negc_ready, 1)
            sp.dma_start(negc_dram, fe).then_inc(negc_stored, 16)
            for c in range(2, NIN + 2):
                load_chunk(c)
            sp.wait_ge(scores_ready, UA)
            sp.wait_ge(negc_stored, 16)
            for i in range(4):
                sp.dma_start(negc[:, 2 * i:2 * i + 2, :], negc_dram[2 * i:2 * i + 2, :].rearrange("(o h) t -> o h t", o=1).broadcast_to([P, 2, N])).then_inc(negc_in[i], 16)
            for c in range(NIN + 2, NCHUNK):
                load_chunk(c)
            sp.wait_ge(pv_psum, UA)
            for j in range(2):
                sp.dma_start(wpa[j], w_proj_a[j * P:(j + 1) * P, :]).then_inc(proj_in, 16)
            sp.wait_ge(split_lo, ND * NCHUNK)
            for j in range(4):
                sp.dma_start(wpb[j], w_proj_b[j * P:(j + 1) * P, :]).then_inc(proj_in, 16)
            sp.wait_ge(scores_added, UA + UB)
            load_chunk(NCHUNK)
            b, c = order[("y", 5)]
            sp.wait_ge(tr_ready[b], c + 1)
            for t in range(NT):
                sp.dma_start(x1[t], x_rows[t * P:(t + 1) * P, :]).then_inc(x1_in[t], 16)
            load_chunk(NCHUNK + 1)

            def load_w(n, k, e):
                t = (w_gate_e, w_up_e, w_down_e)[k]
                src = t[bass.ds(e, 1)].rearrange("o (p j) f -> p (o j) f", p=P)
                dst = (wgu[n][:, :, 0:F], wgu[n][:, :, F:2 * F], wd[n])[k]
                sp.dma_start(dst, src).then_inc(w_in_sem[n][k], 16)

            sp.wait_ge(merged_ready, ND)
            sp.dma_start(wgu[3][:, :, 0:F], w_gate_s.rearrange("(p j) f -> p j f", p=P)).then_inc(shared_in, 16)
            sp.dma_start(wgu[3][:, :, F:2 * F], w_up_s.rearrange("(p j) f -> p j f", p=P)).then_inc(shared_in, 16)
            sp.dma_start(wd[3], w_down_s.rearrange("(p j) f -> p j f", p=P)).then_inc(shared_in, 16)
            sp.dma_start(wr, w_router.rearrange("(p j) e -> p j e", p=P)).then_inc(router_in, 16)
            for k in range(3):
                load_w(0, k, 0)
            for t in range(NT):
                sp.wait_ge(hn_ready, t + 1)
                sp.dma_start(hn_dram[t * P:(t + 1) * P, :], hn[:, t, :]).then_inc(hn_stored, 16)
            sp.wait_ge(dense_ready, O_UNITS)
            for n in (1, 2):
                for k in range(3):
                    load_w(n, k, n)
            for t in range(SH):
                sp.wait_ge(y_ready, 2 * (t + 1))
                sp.dma_start(out_rows[t * P:(t + 1) * P, :], y[t % 2]).then_inc(based[t % 2], 16)
            sp.wait_ge(y_psum, 2 * SH)
            for k in range(3):
                load_w(3, k, 3)

            regs = [sp.alloc_register(f"turn_value{i}") for i in range(4)]
            with sp.Fori(1, E // 4) as m:
                for n in range(4):
                    k = 4 * m + n
                    last = (n - 1) % 4
                    for reg, v in zip(regs, (lands(k - 1, 16, last), lands(k, 16, n), SH + k - 3, 2 * (SH + k - 3))):
                        sp.reg_mov(reg, v)
                    before, own, read_gu, read_d = (bass.RuntimeValue.of_register_unchecked(r, min_val=1, max_val=2 * 16 * E) for r in regs)
                    sp.wait_ge(w_in_sem[last][1], before)
                    sp.wait_ge(gu_psum, read_gu)
                    load_w(n, 0, k)
                    sp.wait_ge(w_in_sem[last][2], before)
                    load_w(n, 1, k)
                    sp.wait_ge(w_in_sem[n][0], own)
                    sp.wait_ge(y_psum, read_d)
                    load_w(n, 2, k)

            more = sp.value_load(rounds_i[0:1, 0:1], min_val=0, max_val=ROUNDS - 1)
            with sp.If(more > 0):
                with sp.Fori(0, more * E) as it:
                    sp.wait_ge(o_free, it + 1)
                    for k in range(3):
                        load_w(0, k, it % E)
            with sp.Else():
                pass

        @block.gpsimd
        def _(pool):
            nc.gpsimd.memset(minus_half[:], -0.5).then_inc(pool_set, 1)
            pool.wait_ge(pool_set, 1)

            def root(dst, src, n, width):
                pool.wait_ge(mean_ready, n)
                nc.gpsimd.tensor_tensor(dst, src, minus_half[:, 0:width], ALU.pow).then_inc(rnorm_ready, 1)

            n = 0
            for t in range(NT):
                n += 1
                root(hn_r[:, t:t + 1], hn_ms[:, t:t + 1], n, 1)
            for q in range(B_UNITS):
                if makes_qk(q):
                    n += 1
                    root(rnorm[:, q % 2, :], mean[:, q % 2, :], n, HB)
            for t in range(NT):
                n += 1
                root(hn_r[:, t:t + 1], hn_ms[:, t:t + 1], n, 1)
            pool.wait_ge(hn_stored, 16 * NT)
            for b in range(2):
                pool.wait_ge(tr_ready[b], uses[b])
            for i in range(4):
                nc.gpsimd.memset(xg[i], 0.0).then_inc(pool_set, 1)
            pool.wait_ge(pool_set, 5)
            last_row = pool.to_reg(N - 1)

            def take_turn(before):
                after(pool, turns, before)
                nc.gpsimd.tensor_tensor(turn[:], minus_half[0:16, 0:1], minus_half[0:16, 0:1], ALU.add).then_inc(turns, 1)

            def gather(slot, before, done):
                take_turn(before)
                pool.indirect_dma_start(out=xg[slot][0:SLOTS, :], out_offset=None, in_=hn_dram,
                                        in_offset=bass.IndirectOffsetOnAxis(idxg[slot][0:SLOTS, 0:1], 0),
                                        bounds_check=last_row, oob_is_err=False).then_inc(done, 16)

            def scatter(slot, idx, before, done):
                take_turn(before)
                pool.indirect_dma_start(out=out_rows, out_offset=bass.IndirectOffsetOnAxis(idx[0:SLOTS, 0:1], 0),
                                        in_=y[slot][0:SLOTS, :], in_offset=None, bounds_check=last_row, oob_is_err=False,
                                        compute_op=ALU.add).then_inc(done, 16)

            def gather_k(k, slot, before):
                after(pool, xT_psum, k - 3)
                pool.wait_ge(idx_ready, k + 1)
                gather(slot, before, gathered[slot])

            def scatter_k(k, u, before):
                pool.wait_ge(y_ready, 2 * (SH + k + 1))
                pool.wait_ge(idx_kept, k + 1)
                after(pool, scattered, 16 * k)
                scatter(u % 2, idxs[u], before, scattered)

            for k in range(5):
                gather_k(k, k % 4, k)
            for b in based:
                pool.wait_ge(b, 8 * SH)

            def pair(k, u):
                scatter_k(k, u, 5 + 2 * k)
                gather_k(k + 5, (u + 1) % 4, 6 + 2 * k)

            for k in range(4):
                pair(k, k)
            with pool.Fori(1, (E - 5) // 4) as m:
                for u in range(4):
                    pair(4 * m + u, u)
            for k in range((E - 5) // 4 * 4, E - 5):
                pair(k, k % 4)
            for k in range(E - 5, E):
                scatter_k(k, k % 4, 5 + 2 * (E - 5) + k - (E - 5))
            pool.wait_ge(scattered, 16 * E)

            more = pool.value_load(rounds_i[0:1, 0:1], min_val=0, max_val=ROUNDS - 1)
            with pool.If(more > 0):
                with pool.Fori(0, more * E) as it:
                    pool.wait_ge(o_idx, it + 1)
                    gather(0, 2 * E + 2 * it, o_gathered)
                    pool.wait_ge(o_y, it + 1)
                    scatter(0, idxg[0], 2 * E + 2 * it + 1, o_scattered)
                    pool.wait_ge(o_scattered, 16 * it + 16)
            with pool.Else():
                pass

        @block.scalar
        def _(act):
            chain = [0]

            def link(ins):
                chain[0] += 1
                ins.then_inc(act_chain, 1)
                act.wait_ge(act_chain, chain[0])

            sums = [0]

            def square(out_, in_, **kw):
                sums[0] += 1
                nc.scalar.activation(out_, in_, ACT.Square, **kw).then_inc(squared, 1)

            for t in range(NT):
                act.wait_ge(x_in[t], 16)
                after(act, squared, sums[0])
                square(sq_x, xin[t], accum_out=hn_ss[:, t:t + 1])

            def split_block(c, j):
                act.wait_ge(chunk_in[j // HALF], 16 * (c + 1))
                if j < HALF:
                    after(act, dense_ready, NT * (c - 1))
                else:
                    after(act, half_used, c)
                nc.scalar.activation(split_of(w_hi, c, j), raw_of(c, j), ACT.Copy).then_inc(split_hi, 1)

            for t in range(NT):
                for b in range(2):
                    act.wait_ge(tr_used[b], t + 1)
                cols = slice(t * P, (t + 1) * P)
                nc.scalar.activation(hT_hi[:, :, cols], hT[:, :, cols], ACT.Copy).then_inc(hT_hi_ready, 1)
                for j in range(2 * t, 2 * t + 2):
                    split_block(0, j)
            act.wait_ge(f_abs, 1)
            nc.scalar.activation(fe, fa, ACT.Exp, scale=-1.0).then_inc(f_exp, 1)
            act.wait_ge(f_exp, 1)
            nc.scalar.activation(fl, fe, ACT.Ln, bias=1.0).then_inc(f_ln, 1)

            def copy_qk(n):
                b, c = order[("qk", n)]
                act.wait_ge(tr_ready[b], c + 1)
                t = n % NT
                kind = unit_kind(n)
                cols = slice(t * P, (t + 1) * P)
                src = psT[b][:].rearrange("p (h q) -> p h q", q=P)
                if kind == "qk":
                    p0 = 4 * (n // NT)
                    cut = min(max(HA // 2 - p0, 0), 4)
                    parts = [(0, qTa, p0, 0, cut), (1, kTa, p0 - HA // 2, cut, 4)]
                else:
                    parts = [(2, qTb, 0, 0, 4)] if kind == "qb" else [(3, kTb, 0, 0, 4)]
                parts = [x for x in parts if x[3] < x[4]]
                for gain, dst, p0, a, z in parts:
                    last = nc.scalar.activation(dst[:, p0 + a:p0 + z, cols], src[:, a:z, :], ACT.Copy, scale=gains[:, gain:gain + 1])
                last.then_inc(tr_used[b], 1)

            def dense(n):
                kind, t, ps = unit_kind(n), n % NT, psD[n % 2]
                for c, j in to_split(n):
                    split_block(c, j)
                act.wait_ge(dense_ready, n + 1)
                if makes_qk(n):
                    after(act, summed, sq_count[0])
                    sq_count[0] += 1
                    square(sq[:, 0:COLS], ps[:])
                elif kind == "gate":
                    m = n - B_UNITS
                    nc.scalar.activation(gates[:, m, :], ps[:], ACT.Identity, bias=bgateT[:, m:m + 1]).then_inc(dense_used[n % 2], 1)
                else:
                    _, c0, cols = in_chunks[n // NT]
                    if kind == "vb":
                        act.wait_ge(negc_stored, 16)
                    dst = va[:, t, c0 - 2 * WA:c0 - 2 * WA + cols] if kind == "va" else vb[:, t, :]
                    nc.scalar.activation(dst, ps[:, 0:cols], ACT.Copy).then_inc(dense_used[n % 2], 1)

            sq_count = [0]
            act.wait_ge(setup_done, 1)
            act.wait_ge(squared, NT)
            for n in range(A_UNITS):
                dense(n)
                if makes_qk(n - 1):
                    copy_qk(n - 1)

            def copy_p(key, dst):
                b, c = order[key]
                act.wait_ge(tr_ready[b], c + 1)
                w = dst.shape[1]
                nc.scalar.activation(dst, psT[b][:, 0:w * P].rearrange("p (b q) -> p b q", q=P), ACT.Copy).then_inc(tr_used[b], 1)

            def exp_a(u):
                act.wait_ge(scores_ready, u + 1)
                w = P * len(blocks_a(u))
                nc.scalar.activation(sc_a[u % 2][:, 0:w], sc_a[u % 2][:, 0:w], ACT.Exp, bias=negmax[:, u % 2, 0:1],
                                     accum_out=rowsum[:, u % 2, 0:1]).then_inc(exp_ready, 1)

            def exp_b(v):
                act.wait_ge(scores_ready, UA + v + 1)
                c0 = 0
                for s, i in enumerate(tiles_b(v)):
                    w = P * (i + 1)
                    last = nc.scalar.activation(sc_b[v % 2][:, c0:c0 + w], sc_b[v % 2][:, c0:c0 + w], ACT.Exp,
                                                bias=negmax[:, v % 2, s:s + 1], accum_out=rowsum[:, v % 2, s:s + 1])
                    c0 += w
                last.then_inc(exp_ready, 1)

            exp_a(0)
            for u in range(1, UA + 1):
                nb = len(blocks_a(u - 1))
                after(act, pv_psum, u - 1)
                for r in range(0, -(-nb // 4), 2):
                    copy_p(("pa", u - 1, r), pT_a[:, 4 * r:min(4 * r + 4, nb), :])
                if u < UA:
                    exp_a(u)
                else:
                    exp_b(0)
                n = A_UNITS + u - 1
                if n < B_UNITS:
                    dense(n)
                if makes_qk(n - 1):
                    copy_qk(n - 1)
            for v in range(1, UB + 1):
                act.wait_ge(pv_psum, UA + v - 2)
                copy_p(("pb", v - 1, 0), pT_b[(v - 1) % 2][:, 0:4, :])
                if v < UB:
                    exp_b(v)
                dense(B_UNITS + v - 1)
            act.wait_ge(dense_used[0], G_UNITS // 2)
            act.wait_ge(dense_used[1], G_UNITS // 2)
            for m in range(ND):
                for g in (m, ND + m):
                    nc.scalar.activation(gates[:, g, :], gates[:, g, :], ACT.Sigmoid).then_inc(sig_ready, 1)
            for m in range(ND):
                act.wait_ge(added, m + 1)
                nc.scalar.activation(hT_hi[:, m, :], merged[m % 2], ACT.Copy).then_inc(merged_hi, 1)
                split_block(NCHUNK, m)
            for n in range(G_UNITS, O_UNITS):
                for c, j in to_split(n):
                    split_block(c, j)
                if n >= O_UNITS - NT:
                    t = n % NT
                    act.wait_ge(x1_ready, n - G_UNITS + 1)
                    act.wait_ge(squared, sums[0])
                    square(sq_h, x1[t], accum_out=hn_ss[:, t:t + 1])
            act.wait_ge(logits_psum, 1)
            nc.scalar.activation(scores, psI[:, 0:NT * E].rearrange("p (t e) -> p t e", t=NT), ACT.Sigmoid).then_inc(scores_sig, 1)

            def silu_of(n, rows):
                return nc.scalar.activation(silu[n][0:rows, :], psG[n][0:rows, 0:F], ACT.Silu)

            def copy_midT(n, rows):
                return nc.scalar.activation(midT[n][:, :, 0:rows], psM[:, 0:NF * P].rearrange("p (j s) -> p j s", j=NF)[:, :, 0:rows], ACT.Copy)

            def copy_y(n, h):
                return nc.scalar.activation(y[n][0:SLOTS, h * 512:(h + 1) * 512], psY[h][0:SLOTS, :], ACT.Copy)

            def silu_i(it, n, rows):
                act.wait_ge(gu_psum, it + 1)
                after(act, mid_ready, it - 1)
                silu_of(n, rows).then_inc(silu_ready, 1)

            def y_i(it, n):
                after(act, scattered, 16 * (it - SH - 1))
                for h in range(2):
                    act.wait_ge(y_psum, 2 * it + h + 1)
                    copy_y(n, h).then_inc(y_ready, 1)

            def midT_i(it, n, rows):
                act.wait_ge(midT_psum, it + 1)
                after(act, y_psum, 2 * (it - 1))
                copy_midT(n, rows).then_inc(midT_ready, 1)

            def step(it, n):
                silu_i(it, n, SLOTS)
                y_i(it - 1, 1 - n)
                midT_i(it, n, SLOTS)

            for it in range(SH + 1):
                silu_i(it, it % 2, P if it < SH else SLOTS)
                midT_i(it, it % 2, P if it < SH else SLOTS)
            for b in based:
                act.wait_ge(b, 8 * SH)
            step(SH + 1, 1)
            with act.Fori(SH // 2 + 1, ITEMS // 2) as m:
                for n in range(2):
                    step(2 * m + n, n)
            y_i(ITEMS - 1, 1)

            more = act.value_load(rounds_i[0:1, 0:1], min_val=0, max_val=ROUNDS - 1)
            with act.If(more > 0):
                with act.Fori(0, more * E) as it:
                    act.wait_ge(o_gu, it + 1)
                    silu_of(0, SLOTS).then_inc(o_silu, 1)
                    act.wait_ge(o_midT_psum, it + 1)
                    copy_midT(0, SLOTS).then_inc(o_midT, 1)
                    act.wait_ge(o_y_psum, it + 1)
                    copy_y(0, 0)
                    copy_y(0, 1).then_inc(o_y, 1)
            with act.Else():
                pass

        @block.vector
        def _(dve):
            chain = [0]

            def link(ins):
                chain[0] += 1
                ins.then_inc(dve_chain, 1)
                dve.wait_ge(dve_chain, chain[0])

            means = [0]

            def mean_of(dst, src, count):
                means[0] += 1
                nc.vector.tensor_scalar(dst, src, 1.0 / count, EPS, ALU.mult, ALU.add).then_inc(mean_ready, 1)
                dve.wait_ge(rnorm_ready, means[0])

            nc.vector.memset(relb[REL_BUCKETS:REL_BUCKETS + 1, :], 1.0)
            nc.vector.memset(ones_b[:], 1.0)
            dve.wait_ge(const_in, 32)
            nc.vector.tensor_copy(iota_b[:], cst[:, P:2 * P])
            nc.vector.tensor_copy(tri_b[:], cst[:, 2 * P:3 * P])
            nc.vector.tensor_copy(mask_b[:], cst[:, 3 * P:4 * P])
            nc.vector.tensor_copy(ident_b[:], ident)

            def copy_wide(key, dst, g):
                for b in range(2):
                    k, c = order[(*key, b)]
                    dve.wait_ge(tr_ready[k], c + 1)
                    h = ND // 2
                    nc.vector.tensor_tensor(dst[:, b * h:(b + 1) * h, key[1] * P:(key[1] + 1) * P],
                                            psT[k][:].rearrange("p (j q) -> p j q", q=P),
                                            g[:, b * h:(b + 1) * h].unsqueeze(2).broadcast_to([P, h, P]), ALU.mult).then_inc(tr_used[k], 1)

            def split_block(c, j):
                dve.wait_ge(split_hi, ND * c + j + 1)
                nc.vector.tensor_tensor(split_of(w_lo, c, j), raw_of(c, j), split_of(w_hi, c, j).bitcast(f32), ALU.subtract).then_inc(split_lo, 1)

            def low_hT(t):
                cols = slice(t * P, (t + 1) * P)
                dve.wait_ge(hT_hi_ready, t + 1)
                nc.vector.tensor_tensor(hT_lo[:, :, cols], hT[:, :, cols], hT_hi[:, :, cols].bitcast(f32), ALU.subtract).then_inc(hT_lo_ready, 1)

            for t in range(NT):
                dve.wait_ge(squared, t + 1)
                mean_of(hn_ms[:, t:t + 1], hn_ss[:, t:t + 1], D)
                if t >= 2:
                    b, c = order[("x", t - 2, 1)]
                    dve.wait_ge(tr_ready[b], c + 1)
                nc.vector.tensor_scalar(xn[t % 2], xin[t], hn_r[:, t:t + 1], None, ALU.mult).then_inc(xn_ready, 1)
                if t >= 1:
                    copy_wide(("x", t - 1), hT, gmixT)
                if t >= 2:
                    low_hT(t - 2)
            copy_wide(("x", NT - 1), hT, gmixT)
            for t in range(NT - 2, NT):
                low_hT(t)
            for j in range(ND):
                split_block(0, j)
            dve.wait_ge(small_in, 16 * 11)
            for c in (0, 2):
                last = nc.vector.tensor_scalar(gains[:, c:c + 1], gains[:, c:c + 1], HEAD_DIM ** -0.5, None, ALU.mult)
            last.then_inc(setup_done, 1)
            for g in range(NG):
                for h in range(2):
                    dve.wait_ge(vec_psum, 2 * g + h + 1)
                    last = nc.vector.tensor_copy(vec[:, g * DIST + h * (DIST // 2):g * DIST + (h + 1) * (DIST // 2)], psS[h][0:HG, 0:DIST // 2])
                    last.then_inc(vec_free, 1)
            dve.wait_ge(f_psum, 1)
            dve.wait_ge(forget_in, 32)
            link(nc.vector.tensor_scalar(fx, psV[0:HB, :], bforget[:, 0:1], None, ALU.add))
            nc.vector.scalar_tensor_tensor(fa, fx, -1.0, fx, ALU.mult, ALU.max).then_inc(f_abs, 1)
            dve.wait_ge(f_ln, 1)
            link(nc.vector.scalar_tensor_tensor(fx, fx, 0.0, fl, ALU.min, ALU.subtract))
            link(nc.vector.memset(fl, 1.0))
            link(nc.vector.tensor_tensor_scan(fa, fl, fx, 0.0, ALU.mult, ALU.add))
            nc.vector.tensor_scalar(fe, fa, -1.0, None, ALU.mult).then_inc(negc_ready, 1)
            dve.wait_ge(cq_psum, 1)
            nc.vector.tensor_copy(cq[:], psV[:, 0:NT * HB].rearrange("p (t h) -> p t h", t=NT)).then_inc(y_norm, 1)

            def dense(n):
                for c, j in to_split(n):
                    split_block(c, j)
                if not makes_qk(n):
                    return
                ps = psD[n % 2]
                s = n % 2
                rows[0] += 1
                dve.wait_ge(squared, NT + rows[0])
                nc.vector.tensor_reduce(sumsq[:, s, :], sq[:, 0:COLS].rearrange("p (h d) -> p h d", d=HEAD_DIM), AX.X, ALU.add).then_inc(summed, 1)
                dve.wait_ge(summed, rows[0])
                mean_of(mean[:, s, :], sumsq[:, s, :], HEAD_DIM)
                if n >= 2 and makes_qk(n - 2):
                    b, c = order[("qk", n - 2)]
                    dve.wait_ge(tr_ready[b], c + 1)
                nc.vector.tensor_tensor(qkrow[s].rearrange("p (h d) -> p h d", d=HEAD_DIM), ps[:].rearrange("p (h d) -> p h d", d=HEAD_DIM),
                                        rnorm[:, s, :].unsqueeze(2).broadcast_to([P, HB, HEAD_DIM]), ALU.mult).then_inc(dense_used[s], 1)

            rows = [0]
            for n in range(A_UNITS):
                dense(n)

            def copy_p(key, dst):
                b, c = order[key]
                dve.wait_ge(tr_ready[b], c + 1)
                nc.vector.tensor_copy(dst, psT[b][:, 0:dst.shape[1] * P].rearrange("p (b q) -> p b q", q=P)).then_inc(tr_used[b], 1)

            def maxima(buf, n, sizes):
                c0 = 0
                for s, w in enumerate(sizes):
                    last = nc.vector.reduce_max(rowmax[:, n % 2, s:s + 1], buf[:, c0:c0 + w], AX.X)
                    c0 += w
                link(last)
                nc.vector.tensor_scalar(negmax[:, n % 2, 0:len(sizes)], rowmax[:, n % 2, 0:len(sizes)], -1.0, None, ALU.mult).then_inc(scores_ready, 1)

            def add_a(u):
                h, i = u // NT, u % NT
                dve.wait_ge(scores_psum, u + 1)
                if u >= 2:
                    dve.wait_ge(pv_psum, u - 1)
                c0 = 0
                for g, (b0, b1) in enumerate(key_blocks_a(u)):
                    w = P * (b1 - b0)
                    u0 = P * (b0 - i) + N - P
                    row = bias_far[:, (g - 1) * HG + h, :] if g else bias_near[:, h, :]
                    u0 -= 0 if g else N - 2 * P
                    last = nc.vector.tensor_tensor(sc_a[u % 2][:, c0:c0 + w], psS[g][:, 0:w], row[:, u0:u0 + w], ALU.add)
                    c0 += w
                last.then_inc(scores_added, 1)

            def max_a(u):
                dve.wait_ge(scores_added, u + 1)
                maxima(sc_a[u % 2], u, [P * len(blocks_a(u))])

            def add_b(v):
                h = v // 2
                dve.wait_ge(scores_psum, UA + v + 1)
                dve.wait_ge(negc_in[h // 2], 16)
                dve.wait_ge(pv_psum, UA + v - 1)
                c0 = 0
                for s, i in enumerate(tiles_b(v)):
                    w = P * (i + 1)
                    last = nc.vector.scalar_tensor_tensor(sc_b[v % 2][:, c0:c0 + w], psS[s][:, 0:w], cq[:, i, h:h + 1], negc[:, h, 0:w],
                                                          ALU.add, ALU.add)
                    c0 += w
                last.then_inc(scores_added, 1)

            def max_b(v):
                dve.wait_ge(scores_added, UA + v + 1)
                maxima(sc_b[v % 2], v, [P * (i + 1) for i in tiles_b(v)])

            dve.wait_ge(bias_in, 16 * HA)
            add_a(0)
            max_a(0)
            for u in range(1, UA + 1):
                add, find_max, w = (add_a, max_a, u) if u < UA else (add_b, max_b, 0)
                add(w)
                nb = len(blocks_a(u - 1))
                if nb > 4:
                    copy_p(("pa", u - 1, 1), pT_a[:, 4:min(8, nb), :])
                find_max(w)
                dve.wait_ge(exp_ready, u)
                link(nc.vector.reciprocal(rowinv[:, (u - 1) % 2, 0:1], rowsum[:, (u - 1) % 2, 0:1]))
                n = A_UNITS + u - 1
                if n < B_UNITS:
                    dense(n)
                dve.wait_ge(pv_psum, u)
                h, i = (u - 1) // NT, (u - 1) % NT
                nc.vector.tensor_scalar(yrow_a[:, i, h * HEAD_DIM:(h + 1) * HEAD_DIM], psV[:, 0:HEAD_DIM], rowinv[:, (u - 1) % 2, 0:1], None,
                                        ALU.mult).then_inc(y_norm, 1)
            for v in range(1, UB + 1):
                if v < UB:
                    add_b(v)
                copy_p(("pb", v - 1, 1), pT_b[(v - 1) % 2][:, 4:5, :])
                if v < UB:
                    max_b(v)
                dve.wait_ge(exp_ready, UA + v)
                link(nc.vector.reciprocal(rowinv[:, (v - 1) % 2, :], rowsum[:, (v - 1) % 2, :]))
                dense(B_UNITS + v - 1)
                dve.wait_ge(pv_psum, UA + v)
                h = (v - 1) // 2
                for s, i in enumerate(tiles_b(v - 1)):
                    last = nc.vector.tensor_scalar(yrow_b[:, i, h * HEAD_DIM:(h + 1) * HEAD_DIM], psV[:, s * HEAD_DIM:(s + 1) * HEAD_DIM],
                                                   rowinv[:, (v - 1) % 2, s:s + 1], None, ALU.mult)
                last.then_inc(y_norm, 1)
            for r in range(6):
                b, c = order[("y", r)]
                dve.wait_ge(tr_ready[b], c + 1)
                nc.vector.tensor_copy(yTa[:, r, :] if r < 2 else yTb[:, r - 2, :], psT[b][:]).then_inc(tr_used[b], 1)
            def low_merged(m):
                dve.wait_ge(merged_hi, m + 1)
                nc.vector.tensor_tensor(hT_lo[:, m, :], merged[m % 2], hT_hi[:, m, :].bitcast(f32), ALU.subtract).then_inc(merged_ready, 1)

            for m in range(ND):
                dve.wait_ge(proj_psum, m + 1)
                dve.wait_ge(sig_ready, 2 * m + 2)
                nc.vector.tensor_tensor(gated[0], psD[m % 2][:], gates[:, m, :], ALU.mult)
                link(nc.vector.tensor_tensor(gated[1], psS[m % 2][:], gates[:, ND + m, :], ALU.mult))
                nc.vector.tensor_tensor(merged[m % 2], gated[0], gated[1], ALU.add).then_inc(added, 1)
                if m >= 1:
                    low_merged(m - 1)
                    split_block(NCHUNK, m - 1)
                dve.wait_ge(added, m + 1)
            low_merged(ND - 1)
            split_block(NCHUNK, ND - 1)

            def norm_x1(t):
                dve.wait_ge(squared, NT + rows[0] + t + 1)
                mean_of(hn_ms[:, t:t + 1], hn_ss[:, t:t + 1], D)
                nc.vector.tensor_scalar(hn[:, t, :], x1[t], hn_r[:, t:t + 1], None, ALU.mult).then_inc(hn_ready, 1)

            for n in range(G_UNITS, O_UNITS):
                h, t = divmod(n - G_UNITS, NT)
                for c, j in to_split(n):
                    split_block(c, j)
                dve.wait_ge(dense_ready, n + 1)
                dve.wait_ge(x1_in[t], 16)
                cols = slice(h * COLS, (h + 1) * COLS)
                nc.vector.tensor_tensor(x1[t][:, cols], psD[n % 2][:], x1[t][:, cols], ALU.add).then_inc(x1_ready, 1)
                if h == 1:
                    norm_x1(t)
                    if t >= 1:
                        copy_wide(("h", t - 1), h2T, gffnT)
            for t in range(NT):
                nc.vector.tensor_copy(table[:, t, :, 0], cst[:, 4 * P + t:4 * P + t + 1].broadcast_to([P, E]))
                nc.vector.tensor_copy(table[:, t, :, 1], cst[:, 4 * P + NT:4 * P + NT + 1].broadcast_to([P, E]))
            nc.vector.memset(table[:, :, :, 2:3], 1.0)
            copy_wide(("h", NT - 1), h2T, gffnT)
            dve.wait_ge(scores_sig, 1)
            link(nc.vector.tensor_tensor(sel, scores, rbias[:, :].unsqueeze(1).broadcast_to([P, NT, E]), ALU.add))
            for t in range(NT):
                last = nc.vector.max(m8[:, t, :], sel[:, t, :])
            link(last)
            for t in range(NT):
                last = nc.vector.match_replace(rep[:, t, :], m8[:, t, :], sel[:, t, :], NEVER)
            link(last)
            link(nc.vector.tensor_tensor(M, rep, sel, ALU.not_equal))
            nc.vector.tensor_copy(Mb, M).then_inc(mask_ready, 1)
            link(nc.vector.tensor_tensor(gt, M, scores, ALU.mult))
            link(nc.vector.tensor_reduce(gsum[:], gt, AX.X, ALU.add))
            link(nc.vector.reciprocal(ginv[:], gsum[:]))
            for t in range(NT):
                last = nc.vector.tensor_scalar(gt[:, t, :], gt[:, t, :], ginv[:, t:t + 1], ROUTE_SCALE, ALU.mult, ALU.mult)
            link(last)
            link(nc.vector.tensor_copy(table[:, :, :, 3], gt))
            link(nc.vector.tensor_tensor(gres, gt, table[:, :, :, 3], ALU.subtract))
            link(nc.vector.tensor_copy(table[:, :, :, 4], gres))
            link(nc.vector.tensor_tensor(gt, gres, table[:, :, :, 4], ALU.subtract))
            nc.vector.tensor_copy(table[:, :, :, 5], gt)
            dve.wait_ge(counts_psum, 1)
            link(nc.vector.tensor_tensor(gres, psI[:, 0:NT * E].rearrange("p (t e) -> p t e", t=NT), M, ALU.mult))
            link(nc.vector.tensor_scalar(pos, gres, -1.0, None, ALU.add))
            link(nc.vector.reduce_max(cmax[:], psM[:, 0:E], AX.X))
            link(nc.vector.tensor_scalar(over[:, 0:ROUNDS - 1], thresholds, cmax[:, 0:1], None, ALU.is_lt))
            link(nc.vector.reduce_sum(oround[:], over[:, 0:ROUNDS - 1], AX.X))
            nc.vector.tensor_copy(rounds_i[:], oround[:]).then_inc(routed, 1)

            def make_onehot(n, e):
                col = pos[:, :, bass.ds(e, 1)]
                return nc.vector.tensor_tensor(onehot[n][:, :, 0:SLOTS], iota_b[:, 0:SLOTS].unsqueeze(1).broadcast_to([P, NT, SLOTS]),
                                               col.broadcast_to([P, NT, SLOTS]), ALU.is_equal)

            def read_idx(slot, done):
                nc.vector.tensor_scalar(idxg[slot][0:SLOTS, :], psI[0:SLOTS, 0:1], psI[0:SLOTS, 1:2], float(NO_TOKEN), ALU.add, ALU.add)
                nc.vector.tensor_scalar(gate[0:SLOTS, slot:slot + 1], psI[0:SLOTS, 3:4], psI[0:SLOTS, 4:5], psI[0:SLOTS, 5:6], ALU.add, ALU.add).then_inc(done, 1)

            def copy_xT(n):
                h = ND // 2
                for c in range(2):
                    last = nc.vector.tensor_tensor(xT[n][:, c * h:(c + 1) * h, 0:SLOTS], psT[c][:].rearrange("p (j s) -> p j s", j=h)[:, :, 0:SLOTS],
                                                   gffnT[:, c * h:(c + 1) * h].unsqueeze(2).broadcast_to([P, h, SLOTS]), ALU.mult)
                return last

            def times_up(n, rows_, g):
                return nc.vector.scalar_tensor_tensor(mid[n][0:rows_, :], silu[n][0:rows_, :], g, psG[n][0:rows_, F:2 * F], ALU.mult, ALU.mult)

            def onehot_k(k, n):
                after(dve, idx_psum, k - 1)
                make_onehot(n, k).then_inc(onehot_ready, 1)

            def idx_k(k, slot):
                dve.wait_ge(idx_psum, k + 1)
                read_idx(slot, idx_ready)

            def xT_k(k, n):
                dve.wait_ge(xT_psum, k + 1)
                after(dve, gu_psum, SH + k - 1)
                copy_xT(n).then_inc(xT_ready, 1)

            def mid_i(it, n, rows_, g):
                dve.wait_ge(silu_ready, it + 1)
                after(dve, midT_psum, it - 1)
                times_up(n, rows_, g).then_inc(mid_ready, 1)

            def y_shared(t):
                if t >= 2:
                    dve.wait_ge(based[t % 2], 16 * (t // 2))
                for h in range(2):
                    dve.wait_ge(y_psum, 2 * t + h + 1)
                    nc.vector.tensor_tensor(y[t % 2][:, h * 512:(h + 1) * 512], psY[h][:], x1[t][:, h * 512:(h + 1) * 512], ALU.add).then_inc(y_ready, 1)

            dve.wait_ge(routed, 1)
            onehot_k(0, 0)
            for it in range(SH):
                mid_i(it, it % 2, P, 1.0)
                if it >= 1:
                    y_shared(it - 1)
                if it == SH - 1:
                    xT_k(0, 0)
                idx_k(it, it)
                onehot_k(it + 1, (it + 1) % 2)

            def expert(k, u, ix=True, oh=True, xt=True):
                dve.wait_ge(idx_ready, k + 1)
                mid_i(SH + k, u % 2, SLOTS, gate[0:SLOTS, u:u + 1])
                if xt:
                    xT_k(k + 1, (u + 1) % 2)
                if isinstance(k, int) and k == 0:
                    y_shared(SH - 1)
                after(dve, scattered, 16 * (k - 3))
                nc.vector.tensor_copy(idxs[u][0:SLOTS, :], idxg[u][0:SLOTS, :]).then_inc(idx_kept, 1)
                if ix:
                    dve.wait_ge(mid_ready, SH + k + 1)
                    dve.wait_ge(idx_kept, k + 1)
                    idx_k(k + 4, u)
                if oh:
                    onehot_k(k + 5, (u + 1) % 2)

            for k in range(4):
                expert(k, k)
            with dve.Fori(1, E // 4 - 2) as m:
                for u in range(4):
                    expert(4 * m + u, u)
            for k in range(E - 8, E):
                expert(k, k % 4, ix=k + 4 < E, oh=k + 5 < E, xt=k + 1 < E)

            more = dve.value_load(rounds_i[0:1, 0:1], min_val=0, max_val=ROUNDS - 1)
            with dve.If(more > 0):
                with dve.Fori(0, more) as r:
                    nc.vector.tensor_scalar(pos, pos, -float(SLOTS), None, ALU.add).then_inc(o_pos, 1)
                    with dve.Fori(0, E) as e:
                        it = r * E + e
                        dve.wait_ge(o_pos, r + 1)
                        make_onehot(0, e).then_inc(o_onehot, 1)
                        dve.wait_ge(o_idx_psum, it + 1)
                        read_idx(0, o_idx)
                        dve.wait_ge(o_xT_psum, it + 1)
                        copy_xT(0).then_inc(o_xT, 1)
                        dve.wait_ge(o_silu, it + 1)
                        times_up(0, SLOTS, gate[0:SLOTS, 0:1]).then_inc(o_mid, 1)
                        dve.wait_ge(o_scattered, 16 * it + 16)
            with dve.Else():
                pass

        @block.tensor
        def _(pe):
            def transposes(key, parts):
                b, c = order[key]
                after(pe, tr_used[b], c)
                for n, (src, k) in enumerate(parts):
                    last = nc.tensor.transpose(psT[b][0:src.shape[1], n * P:n * P + k], src, ident[0:k, 0:k])
                last.then_inc(tr_ready[b], 1)

            pe.wait_ge(const_in, 32)
            for t in range(NT):
                pe.wait_ge(xn_ready, t + 1)
                for b in range(2):
                    transposes(("x", t, b), [(xn[t % 2][:, j::ND], P) for j in range(b * ND // 2, (b + 1) * ND // 2)])
            for b in range(2):
                pe.wait_ge(tr_used[b], NT)
            pe.wait_ge(forget_in, 32)
            for j in range(ND):
                last = nc.tensor.matmul(psV[0:HB, :], wf[:, j, :], hT[:, j, :], start=(j == 0), stop=(j == ND - 1))
            last.then_inc(f_psum, 1)
            pe.wait_ge(table_in, 32)
            pe.wait_ge(setup_done, 1)
            for g in range(NG):
                for h in range(2):
                    after(pe, vec_free, 2 * (g - 1) + h + 1)
                    nc.tensor.matmul(psS[h][0:HG, 0:DIST // 2], relb[:, g * HG:(g + 1) * HG],
                                     table_b[:, g * DIST + h * (DIST // 2):g * DIST + (h + 1) * (DIST // 2)], start=True, stop=True).then_inc(vec_psum, 1)

            def dense(n):
                if n < G_UNITS:
                    after(pe, dense_used[n % 2], n // 2)
                else:
                    after(pe, x1_ready, n - G_UNITS - 1)
                c, t = n // NT, n % NT
                if n < NT:
                    pe.wait_ge(hT_lo_ready, t + 1)
                for j in range(ND):
                    if t == 0:
                        pe.wait_ge(split_lo, ND * c + j + 1)
                    w = [split_of(x, c, j) for x in (w_hi, w_lo)]
                    h = [x[:, j, :] for x in (hT_hi, hT_lo)]
                    for k, (a, b) in enumerate(((0, 0), (0, 1), (1, 0))):
                        if B_UNITS <= n < G_UNITS:
                            left, right = w[a][:, t * P:(t + 1) * P], h[b]
                        else:
                            left, right = h[a][:, t * P:(t + 1) * P], w[b]
                        last = nc.tensor.matmul(psD[n % 2][:, 0:chunk_cols(c)], left, right, start=(j == 0 and k == 0), stop=(j == ND - 1 and k == 2))
                    if t == NT - 1 and j == HALF - 1:
                        last.then_inc(half_used, 1)
                last.then_inc(dense_ready, 1)

            def transpose_qk(n):
                pe.wait_ge(qkrow_done(n)[0], qkrow_done(n)[1])
                transposes(("qk", n), [(qkrow[n % 2][:, i * P:(i + 1) * P], P) for i in range(4)])

            def qkrow_done(n):
                return dense_used[n % 2], n // 2 + 1

            for n in range(A_UNITS):
                dense(n)
                if makes_qk(n - 1):
                    transpose_qk(n - 1)
                if n == 0:
                    pe.wait_ge(negc_ready, 1)
                    for t in range(NT):
                        last = nc.tensor.transpose(psV[:, t * HB:(t + 1) * HB], fa[:, t * P:(t + 1) * P], ident[0:HB, 0:HB])
                    last.then_inc(cq_psum, 1)

            def scores_a(u):
                h, i = u // NT, u % NT
                after(pe, scores_ready, u)
                for g, (b0, b1) in enumerate(key_blocks_a(u)):
                    head = g * HG + h
                    rows = slice(head % 2 * HEAD_DIM, (head % 2 + 1) * HEAD_DIM)
                    last = nc.tensor.matmul(psS[g][:, 0:P * (b1 - b0)], qTa[rows, head // 2, i * P:(i + 1) * P],
                                            kTa[rows, head // 2, b0 * P:b1 * P], start=True, stop=True)
                last.then_inc(scores_psum, 1)

            def transpose_pa(u):
                pe.wait_ge(exp_ready, u + 1)
                nb = len(blocks_a(u))
                for r in range(-(-nb // 4)):
                    transposes(("pa", u, r), [(sc_a[u % 2][:, b * P:(b + 1) * P], P) for b in range(4 * r, min(4 * r + 4, nb))])

            def weighted_a(u):
                h = u // NT
                found = blocks_a(u)
                for r in range(-(-len(found) // 4)):
                    b, c = order[("pa", u, r)]
                    pe.wait_ge(tr_used[b], c + 1)
                after(pe, y_norm, u + 1)
                for n, (g, b) in enumerate(found):
                    head = g * HG + h
                    last = nc.tensor.matmul(psV[:, 0:HEAD_DIM], pT_a[:, n, :], va[:, b, head * HEAD_DIM:(head + 1) * HEAD_DIM],
                                            start=(n == 0), stop=(n == len(found) - 1))
                last.then_inc(pv_psum, 1)

            def scores_b(v):
                h = v // 2
                rows = slice(h % 2 * HEAD_DIM, (h % 2 + 1) * HEAD_DIM)
                after(pe, scores_ready, UA + v)
                for s, i in enumerate(tiles_b(v)):
                    nc.tensor.matmul(psS[s][:, 0:P * (i + 1)], qTb[rows, h // 2, i * P:(i + 1) * P], kTb[rows, h // 2, 0:(i + 1) * P],
                                     start=True, stop=False)
                    last = nc.tensor.matmul(psS[s][:, i * P:(i + 1) * P], ident_b[:], mask_b[:], start=False, stop=True)
                last.then_inc(scores_psum, 1)

            def weighted_b(v):
                h = v // 2
                for r in range(2):
                    b, c = order[("pb", v, r)]
                    pe.wait_ge(tr_used[b], c + 1)
                pe.wait_ge(y_norm, UA + v + 1)
                found = blocks_b(v)
                for n, (i, b) in enumerate(found):
                    s = tiles_b(v).index(i)
                    last = nc.tensor.matmul(psV[:, s * HEAD_DIM:(s + 1) * HEAD_DIM], pT_b[v % 2][:, n, :], vb[:, b, h * HEAD_DIM:(h + 1) * HEAD_DIM],
                                            start=(b == 0), stop=(b == i))
                last.then_inc(pv_psum, 1)

            def last_use(kinds, bank, below=None):
                return max(c + 1 for (kind, *r), (b, c) in order.items() if kind in kinds and b == bank and (below is None or r[0] < below))

            pe.wait_ge(vec_free, 2 * NG)
            for b in range(2):
                pe.wait_ge(dense_used[b], A_UNITS // 2)
                pe.wait_ge(tr_used[b], last_use(("qk",), b, A_UNITS))
            scores_a(0)
            for u in range(1, UA + 1):
                n = A_UNITS + u - 1
                if u < UA:
                    scores_a(u)
                else:
                    for b in range(2):
                        pe.wait_ge(dense_used[b], B_UNITS // 2)
                        pe.wait_ge(tr_used[b], last_use(("qk",), b))
                    scores_b(0)
                transpose_pa(u - 1)
                if n < B_UNITS:
                    dense(n)
                if makes_qk(n - 1):
                    transpose_qk(n - 1)
                weighted_a(u - 1)
            for v in range(1, UB + 1):
                if v < UB:
                    scores_b(v)
                pe.wait_ge(exp_ready, UA + v)
                for r, (b0, b1) in enumerate(((0, 4), (4, 5))):
                    transposes(("pb", v - 1, r), [(sc_b[(v - 1) % 2][:, b * P:(b + 1) * P], P) for b in range(b0, b1)])
                dense(B_UNITS + v - 1)
                weighted_b(v - 1)
            pe.wait_ge(y_norm, UA + UB + 1)
            for r in range(6):
                rows, c = (yrow_a, r) if r < 2 else (yrow_b, r - 2)
                transposes(("y", r), [(rows[:, t, c * P:(c + 1) * P], P) for t in range(NT)])
            for b in range(2):
                pe.wait_ge(tr_used[b], order[("y", 4 + b)][1] + 1)
                pe.wait_ge(dense_used[b], G_UNITS // 2)
            pe.wait_ge(proj_in, 16 * 6)
            for m in range(ND):
                after(pe, added, m - 1)
                for j in range(2):
                    nc.tensor.matmul(psD[m % 2][:], wpa[j][:, m * P:(m + 1) * P], yTa[:, j, :], start=(j == 0), stop=(j == 1))
                for j in range(4):
                    last = nc.tensor.matmul(psS[m % 2][:], wpb[j][:, m * P:(m + 1) * P], yTb[:, j, :], start=(j == 0), stop=(j == 3))
                last.then_inc(proj_psum, 1)
            def transpose_h(t):
                pe.wait_ge(hn_ready, t + 1)
                for b in range(2):
                    transposes(("h", t, b), [(hn[:, t, j::ND], P) for j in range(b * ND // 2, (b + 1) * ND // 2)])

            pe.wait_ge(merged_ready, ND)
            for n in range(G_UNITS, O_UNITS):
                dense(n)
                if n > O_UNITS - NT:
                    transpose_h(n % NT - 1)
            transpose_h(NT - 1)
            pe.wait_ge(router_in, 16)
            for b in range(2):
                pe.wait_ge(tr_used[b], uses[b])
            for t in range(NT):
                for j in range(ND):
                    last = nc.tensor.matmul(psI[:, t * E:(t + 1) * E], h2T[:, j, t * P:(t + 1) * P], wr[:, j, :], start=(j == 0), stop=(j == ND - 1))
            last.then_inc(logits_psum, 1)

            def gate_up(n, rows, lhs, slot):
                for j in range(ND):
                    last = nc.tensor.matmul(psG[n][0:rows, :], lhs[:, j, 0:rows], wgu[slot][:, j, :], start=(j == 0), stop=(j == ND - 1))
                return last

            def transpose_mid(n, rows):
                for j in range(NF):
                    last = nc.tensor.transpose(psM[:, j * P:j * P + rows], mid[n][0:rows, j::NF], ident[0:rows, 0:rows])
                return last

            def down(n, h, rows, slot):
                for j in range(NF):
                    last = nc.tensor.matmul(psY[h][0:rows, :], midT[n][:, j, 0:rows], wd[slot][:, j, h * 512:(h + 1) * 512],
                                            start=(j == 0), stop=(j == NF - 1))
                return last

            def find_slots(n, e):
                for t in range(NT):
                    last = nc.tensor.matmul(psI[0:SLOTS, 0:6], onehot[n][:, t, 0:SLOTS], table[:, t, bass.ds(e, 1), :].rearrange("p a b -> p (a b)"),
                                            start=(t == 0), stop=(t == NT - 1))
                return last

            def transpose_rows(slot):
                for j in range(ND):
                    c = j % (ND // 2) * P
                    last = nc.tensor.transpose(psT[j // (ND // 2)][:, c:c + SLOTS], xg[slot][0:SLOTS, j::ND], ident[0:SLOTS, 0:SLOTS])
                return last

            def is_shared(it):
                return isinstance(it, int) and it < SH

            def up_i(it, n, slot):
                after(pe, mid_ready, it - 1)
                if is_shared(it):
                    pe.wait_ge(shared_in, 48)
                    gate_up(n, P, h2T[:, :, it * P:(it + 1) * P], 3).then_inc(gu_psum, 1)
                else:
                    for k in range(2):
                        pe.wait_ge(w_in_sem[slot][k], lands(it - SH, 16, slot))
                    pe.wait_ge(xT_ready, it - SH + 1)
                    gate_up(n, SLOTS, xT[n], slot).then_inc(gu_psum, 1)

            def down_i(it, n, slot):
                pe.wait_ge(midT_ready, it + 1)
                if not is_shared(it):
                    pe.wait_ge(w_in_sem[slot][2], lands(it - SH, 16, slot))
                for h in range(2):
                    after(pe, y_ready, 2 * (it - 1) + h + 1)
                    down(n, h, P if is_shared(it) else SLOTS, 3 if is_shared(it) else slot).then_inc(y_psum, 1)

            def step(it, u, xt=True, ix=True):
                n = u % 2
                up_i(it, n, u)
                if xt:
                    k, slot = it + 1 - SH, (u + 1) % 4
                    pe.wait_ge(gathered[slot], lands(k, 16, slot))
                    after(pe, xT_ready, k)
                    transpose_rows(slot).then_inc(xT_psum, 1)
                if not (isinstance(it, int) and it == 0):
                    down_i(it - 1, 1 - n, (u - 1) % 4)
                else:
                    pe.wait_ge(mask_ready, 1)
                    pe.wait_ge(scores_sig, 1)
                    for t in range(NT):
                        for s in range(t + 1):
                            nc.tensor.matmul(psI[:, t * E:(t + 1) * E], tri_b[:] if s == t else ones_b[:], Mb[:, s, :], start=(s == 0), stop=(s == t))
                    for t in range(NT):
                        last = nc.tensor.matmul(psM[:, 0:E], ones_b[:], Mb[:, t, :], start=(t == 0), stop=(t == NT - 1))
                    last.then_inc(counts_psum, 1)
                    pe.wait_ge(routed, 1)
                pe.wait_ge(mid_ready, it + 1)
                after(pe, midT_ready, it)
                transpose_mid(n, P if is_shared(it) else SLOTS).then_inc(midT_psum, 1)
                if ix:
                    pe.wait_ge(onehot_ready, it + 1)
                    after(pe, idx_ready, it)
                    find_slots(n, it).then_inc(idx_psum, 1)

            for it in range(SH + 4):
                step(it, it % 4, xt=it + 1 >= SH)
            with pe.Fori(2, ITEMS // 4 - 1) as m:
                for u in range(4):
                    step(4 * m + u, u)
            for it in range(ITEMS - 4, ITEMS):
                step(it, it % 4, xt=it + 1 < ITEMS, ix=False)
            down_i(ITEMS - 1, 1, 3)

            more = pe.value_load(rounds_i[0:1, 0:1], min_val=0, max_val=ROUNDS - 1)
            with pe.If(more > 0):
                pe.wait_ge(scattered, 16 * E)
                with pe.Fori(0, more * E) as it:
                    nc.tensor.matmul(psM[0:1, 0:1], ident_b[:, 0:1], ident_b[:, 0:1], start=True, stop=True).then_inc(o_free, 1)
                    pe.wait_ge(o_onehot, it + 1)
                    find_slots(0, it % E).then_inc(o_idx_psum, 1)
                    pe.wait_ge(o_gathered, 16 * it + 16)
                    transpose_rows(0).then_inc(o_xT_psum, 1)
                    pe.wait_ge(o_xT, it + 1)
                    for k in range(2):
                        pe.wait_ge(w_in_sem[0][k], 4 * E + 16 * it + 16)
                    gate_up(0, SLOTS, xT[0], 0).then_inc(o_gu, 1)
                    pe.wait_ge(o_mid, it + 1)
                    transpose_mid(0, SLOTS).then_inc(o_midT_psum, 1)
                    pe.wait_ge(o_midT, it + 1)
                    pe.wait_ge(w_in_sem[0][2], 4 * E + 16 * it + 16)
                    down(0, 0, SLOTS, 0)
                    down(0, 1, SLOTS, 0).then_inc(o_y_psum, 1)
                    pe.wait_ge(o_y, it + 1)
            with pe.Else():
                pass


_INS = ["x", "g_mix", "w_in", "q_norm_a", "k_norm_a", "q_norm_b", "k_norm_b", "rel_bias", "b_forget", "w_gate", "b_gate",
        "w_proj_a", "w_proj_b", "w_out", "g_ffn", "w_router", "router_bias", "w_gate_e", "w_up_e", "w_down_e",
        "w_gate_s", "w_up_s", "w_down_s"]


def shape_constants():
    tiles = SEQ // P
    rounds = -(-SEQ // SLOTS)
    c = np.zeros((P, 4 * P + tiles + 1 + rounds), np.float32)
    c[:, 0:P] = np.eye(P)
    c[:, P:2 * P] = np.arange(P)[None]
    c[:, 2 * P:3 * P] = np.triu(np.ones((P, P)))
    c[:, 3 * P:4 * P] = np.triu(np.full((P, P), MASKED), 1)
    c[:, 4 * P:4 * P + tiles] = np.arange(tiles)[None] * P - NO_TOKEN
    c[:, 4 * P + tiles] = np.arange(P)
    c[:, 4 * P + tiles + 1:] = SLOTS * np.arange(1, rounds + 1)[None]
    dist = SEQ - 1 - np.arange(DIST)
    exact = REL_BUCKETS // 2
    n = np.maximum(dist, 1).astype(np.float32)
    large = exact + (np.log(n / np.float32(exact)) / np.float32(math.log(REL_MAX_DIST / exact)) * np.float32(REL_BUCKETS - exact)).astype(np.int32)
    bucket = np.where(dist < exact, dist, np.minimum(large, REL_BUCKETS - 1))
    table = np.zeros((REL_BUCKETS + 1, len(DIL_GROUPS), DIST), np.float32)
    for g, (window, step) in enumerate(DIL_GROUPS):
        seen = (dist >= 0) & (dist <= window) & (dist % step == 0)
        for b in range(REL_BUCKETS):
            table[b, g] = seen & (bucket == b)
        table[REL_BUCKETS, g] = np.where(seen, 0.0, MASKED)
    return c, table.reshape(REL_BUCKETS + 1, -1)


def kernel(**inputs):
    import concourse.bacc as bacc
    from concourse import mybir as mb
    from concourse.bass_utils import run_bass_kernel_spmd as run

    nc = bacc.Bacc("TRN2", target_bir_lowering=False, num_devices=1)
    consts, bias_table = shape_constants()
    given = {name: np.ascontiguousarray(inputs[name]) for name in _INS}
    given["b_gate"] = np.ascontiguousarray(given["b_gate"].reshape(-1, P).T)
    given |= {"consts": consts, "bias_table": bias_table}
    args = [nc.dram_tensor(f"in_{name}", a.shape, mb.dt.from_np(a.dtype), kind="ExternalInput").ap() for name, a in given.items()]
    out = nc.dram_tensor("out_0", given["x"].shape, mb.dt.float32, kind="ExternalOutput").ap()
    layer(nc, *args, out)
    r = run(nc, [{f"in_{name}": a for name, a in given.items()}], core_ids=[0])
    return r.results[0]["out_0"]
```

```python
import math
from contextlib import ExitStack

import numpy as np
import concourse.bass as bass
from concourse import mybir

P = 128
HEAD_DIM = 64
DIL_GROUPS = ((128, 1), (512, 4), (2048, 16))
HEADS_PER_GROUP = 4
REL_BUCKETS, REL_MAX_DIST = 32, 2048
TOP_K = 8
ROUTE_SCALE = 2.5
EPS = 1e-6
MASKED = -1e30
NEVER = -3e38
SLOTS = 96
WARM_UP = 56
NO_TOKEN = 1024
SEQ = 512
DIST = SEQ + P


def layer(nc, x, g_mix, w_in, q_norm_a, k_norm_a, q_norm_b, k_norm_b, rel_bias, b_forget, w_gate, b_gate,
          w_proj_a, w_proj_b, w_out, g_ffn, w_router, router_bias, w_gate_e, w_up_e, w_down_e,
          w_gate_s, w_up_s, w_down_s, consts, bias_table, out):
    f32, bf16, i32, u32 = mybir.dt.float32, mybir.dt.bfloat16, mybir.dt.int32, mybir.dt.uint32
    ALU, ACT, AX = mybir.AluOpType, mybir.ActivationFunctionType, mybir.AxisListType
    E, D, F = w_gate_e.shape
    N = x.shape[1]
    x_rows, out_rows = x[0], out[0]
    NT, ND, NF = N // P, D // P, F // P
    HG = HEADS_PER_GROUP
    NG = len(DIL_GROUPS)
    HA, HB = HG * NG, b_forget.shape[0]
    WA, WB = HA * HEAD_DIM, HB * HEAD_DIM
    COLS = 512
    HALF = ND // 2
    RING = ND + HALF
    ROUNDS = -(-N // SLOTS)
    SH = NT
    ITEMS = SH + E

    hn_dram = nc.dram_tensor("hn_dram", [N, D], f32, kind="Internal").ap()
    vec_dram = nc.dram_tensor("vec_dram", [HA, P, DIST], f32, kind="Internal")
    negc_dram = nc.dram_tensor("negc_dram", [HB, N], f32, kind="Internal").ap()

    in_chunks = [("qk", 0, COLS), ("qk", COLS, COLS), ("qk", 2 * COLS, COLS), ("va", 3 * COLS, COLS),
                 ("va", 4 * COLS, 3 * WA - 4 * COLS), ("qb", 3 * WA, WB), ("kb", 3 * WA + WB, WB), ("vb", 3 * WA + 2 * WB, WB)]
    NIN = len(in_chunks)
    NCHUNK = NIN + 2 * D // COLS
    A_UNITS, B_UNITS, G_UNITS = 5 * NT, NIN * NT, NIN * NT + 2 * D // P
    O_UNITS = G_UNITS + D // COLS * NT
    unit_kind = lambda n: in_chunks[n // NT][0] if n < B_UNITS else "gate"
    makes_qk = lambda n: 0 <= n < B_UNITS and unit_kind(n) in ("qk", "qb", "kb")
    VA_LAST = 4
    UA, UB = HG * NT, HB * 2

    def key_blocks_a(u):
        i = u % NT
        return [(0 if g else max(0, i - 1), i + 1) for g in range(NG)]

    def blocks_a(u):
        return [(g, b) for g, (b0, b1) in enumerate(key_blocks_a(u)) for b in range(b0, b1)]

    def tiles_b(v):
        return (v % 2, NT - 1 - v % 2)

    def blocks_b(v):
        return [(i, b) for i in tiles_b(v) for b in range(i + 1)]

    SPREAD = (B_UNITS - A_UNITS) * ND // UA

    def spread(u):
        return [divmod(A_UNITS * ND + k, ND) for k in range(SPREAD * (u - 1), SPREAD * u)]

    def finishes(u):
        return ([n for n, j in spread(u) if j == ND - 1] + [None])[0] if u else None

    uses, order = [0, 0], {}

    def number(key, bank):
        order[key] = (bank, uses[bank])
        uses[bank] += 1

    for t in range(NT):
        for b in range(2):
            number(("x", t, b), b)
    for n in range(A_UNITS):
        if makes_qk(n - 1):
            number(("qk", n - 1), n % 2)
    for u in range(UA + 1):
        if u >= 1:
            for r in range(-(-len(blocks_a(u - 1)) // 4)):
                number(("pa", u - 1, r), r % 2)
            n = finishes(u)
            if n is not None and makes_qk(n - 1):
                number(("qk", n - 1), 1)
            if u == 1:
                number(("f",), 0)
            if u == 5:
                number(("cq",), 1)
    for v in range(1, UB + 1):
        for r in range(2):
            number(("pb", v - 1, r), r)
    for r in range(2 + 4):
        number(("y", r), r % 2)
    for t in range(NT):
        for b in range(2):
            number(("h", t, b), b)

    ctx = ExitStack()
    with ctx:
        def sb(name, shape, dt=f32):
            return ctx.enter_context(nc.sbuf_tensor(name, shape, dt))

        def sem(name):
            return ctx.enter_context(nc.semaphore(name))

        cst = sb("cst", [P, 4 * P + NT + 1 + ROUNDS])
        ident = cst[:, 0:P]
        thresholds = cst[:, 4 * P + NT + 1:4 * P + NT + ROUNDS]
        iota_b, tri_b, mask_b, ident_b, ones_b = (sb(n, [P, P], bf16) for n in ("iota_b", "tri_b", "mask_b", "ident_b", "ones_b"))
        gmixT, gffnT, bgateT = sb("gmixT", [P, ND]), sb("gffnT", [P, ND]), sb("bgateT", [P, 2 * D // P])
        gains = sb("gains", [P, 4])
        bforget = sb("bforget", [HB, 1])
        relb = sb("relb", [REL_BUCKETS + 1, HA])
        frow = sb("frow", [P, NT, HB])
        minus_half = sb("minus_half", [P, HB])
        sumsq = sb("sumsq", [P, 2, HB]); mean = sb("mean", [P, 2, HB]); rnorm = sb("rnorm", [P, 2, HB])
        rowmax = sb("rowmax", [P, 2, 2]); negmax = sb("negmax", [P, 2, 2]); rowsum = sb("rowsum", [P, 2, 2]); rowinv = sb("rowinv", [P, 2, 2])
        cq = sb("cq", [P, NT, HB])
        turn = sb("turn", [16, 1])
        cmax = sb("cmax", [P, 1]); over = sb("over", [P, ROUNDS]); oround = sb("oround", [P, 1]); rounds_i = sb("rounds_i", [P, 1], i32)
        gsum = sb("gsum", [P, NT]); ginv = sb("ginv", [P, NT]); m8 = sb("m8", [P, NT, TOP_K])
        gate = sb("gate", [P, 4])
        idxg = [sb(f"idxg{i}", [P, 1], u32) for i in range(4)]
        idxs = [sb(f"idxs{i}", [P, 1], u32) for i in range(4)]
        hn_ss, hn_ms, hn_r = sb("hn_ss", [P, NT]), sb("hn_ms", [P, NT]), sb("hn_r", [P, NT])
        rbias = sb("rbias", [P, E])

        KB = 256
        arena = sb("arena", [P, 121 * KB])
        w_lo = sb("w_lo", [P, RING, N], mybir.dt.float32r)
        with ExitStack() as split_ctx:
            hT_hi, hT_lo, w_hi = (split_ctx.enter_context(nc.sbuf_tensor(name, [P, blocks, N], mybir.dt.float32r))
                                  for name, blocks in (("hT_hi", ND), ("hT_lo", ND), ("w_hi", RING)))
        arena_x = sb("arena_x", [P, 56 * KB])

        def at(kb, cols):
            a, k = (arena, kb) if kb < 121 else (arena_x, kb - 121)
            return a[:, int(k * KB):int(k * KB) + cols]

        raw = [at(8 * i, ND // 2 * COLS).rearrange("p (j c) -> p j c", j=ND // 2) for i in range(4)]
        qTa, kTa = (at(k, HA // 2 * N).rearrange("p (h t) -> p h t", h=HA // 2) for k in (16, 28))
        va = at(40, NT * WA).rearrange("p (t c) -> p t c", t=NT)
        bias_near = at(52, HG * 2 * P).rearrange("p (h u) -> p h u", h=HG)
        bias_far = at(56, (HA - HG) * N).rearrange("p (h u) -> p h u", h=HA - HG)
        qTb, kTb = (at(k, HB // 2 * N).rearrange("p (h t) -> p h t", h=HB // 2) for k in (72, 80))
        vb = at(88, NT * WB).rearrange("p (t c) -> p t c", t=NT)
        sc_a = [at(96 + 5 * i, 10 * P) for i in range(2)]
        pT_a = at(106, 10 * P).rearrange("p (b q) -> p b q", q=P)
        sc_b = [at(96 + 2.5 * i, 5 * P) for i in range(2)]
        pT_b = [at(106 + 2.5 * i, 5 * P).rearrange("p (b q) -> p b q", q=P) for i in range(2)]
        sq = at(111, COLS)
        qkrow = [at(113 + 2 * i, COLS) for i in range(2)]
        yrow_a = at(117, NT * HG * HEAD_DIM).rearrange("p (t c) -> p t c", t=NT)
        xin = [at(16 + 4 * i, D) for i in range(NT)]
        xn = [at(32 + 4 * i, D) for i in range(2)]
        hT = at(72, ND * N).rearrange("p (j t) -> p j t", j=ND)
        fx, fa, fe, fl = (arena[0:HB, (88 + 2 * i) * KB:(88 + 2 * i) * KB + N] for i in range(4))
        table_b = arena[0:REL_BUCKETS + 1, 96 * KB:96 * KB + NG * DIST]
        vec = arena[0:HG, 96 * KB + NG * DIST:96 * KB + 2 * NG * DIST]
        sq_x = at(113, D)
        negc = at(16, HB * N).rearrange("p (h t) -> p h t", h=HB)
        yrow_b = at(32, NT * WB).rearrange("p (t c) -> p t c", t=NT)
        gates = at(40, 2 * D // P * N).rearrange("p (m t) -> p m t", m=2 * D // P)
        wpa = [at(k, D) for k in (101, 111)]
        wpb = [at(4 * i, D) for i in range(4)]
        yTa = at(72, 2 * N).rearrange("p (j t) -> p j t", j=2)
        yTb = at(76, 4 * N).rearrange("p (j t) -> p j t", j=4)
        merged = [at(84 + 2 * i, N) for i in range(2)]
        gated = [at(88 + 2 * i, N) for i in range(2)]
        x1 = [at(k, D) for k in (32, 36, 92, 117)]
        sq_h = at(88, D)
        hn = at(72, NT * D).rearrange("p (t d) -> p t d", t=NT)
        h2T = at(96, ND * N).rearrange("p (j t) -> p j t", j=ND)
        wgu = [at(k, 2 * ND * F).rearrange("p (j c) -> p j c", j=ND) for k in (40, 121, 153, 0)]
        wd = [at(k, NF * D).rearrange("p (j c) -> p j c", j=NF) for k in (56, 137, 169, 64)]
        y = [at(24 + 4 * i, D) for i in range(2)]
        xg = [at(72 + 4 * i, D) for i in range(4)]
        table = at(145, NT * E * 3).bitcast(bf16).rearrange("p (t e c) -> p t e c", t=NT, e=E)
        down_parts = w_lo[:].rearrange("p b c -> p (b c)")
        wd_hi, wd_lo = (down_parts[:, i * NF * D:(i + 1) * NF * D].rearrange("p (j c) -> p j c", j=NF) for i in range(2))
        midT = [[down_parts[:, 2 * NF * D + (2 * i + k) * NF * P:2 * NF * D + (2 * i + k + 1) * NF * P].rearrange("p (j s) -> p j s", j=NF)
                 for k in range(2)] for i in range(2)]
        xT = [at(k, ND * P).rearrange("p (j s) -> p j s", j=ND) for k in (88, 112)]
        silu = [at(148 + i, F) for i in range(2)]
        mid = [at(150 + i, F) for i in range(2)]
        onehot = [at(k, NT * P // 2).bitcast(bf16).rearrange("p (t s) -> p t s", t=NT) for k in (152, 116)]
        sel, rep, M, gt, gres = (at(16 + i, NT * E).rearrange("p (t e) -> p t e", t=NT) for i in range(5))
        scoresT = arena[0:E, 24 * KB:24 * KB + N]
        Mb = at(22, NT * E // 2).bitcast(bf16).rearrange("p (t e) -> p t e", t=NT)
        pos = at(23, NT * E).rearrange("p (t e) -> p t e", t=NT)
        wr = at(112, ND * E).rearrange("p (j e) -> p j e", j=ND)

        bank = [ctx.enter_context(nc.psum_tensor(f"bank{i}", [P, 512], f32)) for i in range(8)]
        psD, psS, psT, psV = bank[0:2], bank[2:5], bank[5:7], bank[7]
        psG, psY, psM, psI = bank[0:2], bank[2:4], bank[4], bank[7]
        scores = psT[0][:, 0:NT * E].rearrange("p (t e) -> p t e", t=NT)

        x_in = [sem(f"x_in{t}") for t in range(NT)]
        gains_in, ones_set = sem("gains_in"), sem("ones_set")
        const_in, small_in, table_in, forget_in = sem("const_in"), sem("small_in"), sem("table_in"), sem("forget_in")
        chunk_in = [sem(f"chunk_in{i}") for i in range(2)]
        split_hi, split_lo, half_used = sem("split_hi"), sem("split_lo"), sem("half_used")
        hT_hi_ready, hT_lo_ready = sem("hT_hi_ready"), sem("hT_lo_ready")
        merged_hi = sem("merged_hi")
        vec_free, vec_stored, bias_in = sem("vec_free"), sem("vec_stored"), sem("bias_in")
        vec_psum, negc_ready, negc_stored = sem("vec_psum"), sem("negc_ready"), sem("negc_stored")
        negc_in = [sem(f"negc_in{i}") for i in range(4)]
        squared, mean_ready, rnorm_ready = sem("squared"), sem("mean_ready"), sem("rnorm_ready")
        xn_ready, setup_done = sem("xn_ready"), sem("setup_done")
        dense_ready = sem("dense_ready")
        dense_used = [sem(f"dense_used{i}") for i in range(2)]
        summed = sem("summed")
        tr_ready = [sem(f"tr_ready{i}") for i in range(2)]
        tr_used = [sem(f"tr_used{i}") for i in range(2)]
        scores_psum, scores_ready, exp_ready = sem("scores_psum"), sem("scores_ready"), sem("exp_ready")
        scores_added = sem("scores_added")
        pv_psum, y_norm = sem("pv_psum"), sem("y_norm")
        f_abs, f_exp, f_ln = sem("f_abs"), sem("f_exp"), sem("f_ln")
        proj_in, x1_in = sem("proj_in"), [sem(f"x1_in{t}") for t in range(NT)]
        sig_ready, proj_psum, merged_ready = sem("sig_ready"), sem("proj_psum"), sem("merged_ready")
        added, x1_ready = sem("added"), sem("x1_ready")
        hn_ready, hn_stored = sem("hn_ready"), sem("hn_stored")
        dve_chain, act_chain = sem("dve_chain"), sem("act_chain")
        shared_in, router_in = sem("shared_in"), sem("router_in")
        logits_psum, scores_sig, scores_turned, mask_ready, counts_psum, routed = (
            sem(n) for n in ("logits_psum", "scores_sig", "scores_turned", "mask_ready", "counts_psum", "routed"))
        w_in_sem = [[sem(f"w_slot{n}_{k}") for k in "gud"] for n in range(4)]
        onehot_ready, idx_psum, idx_ready, idx_kept = sem("onehot_ready"), sem("idx_psum"), sem("idx_ready"), sem("idx_kept")
        gathered = [sem(f"gathered{i}") for i in range(4)]
        xT_psum, xT_ready, gu_psum, silu_ready = sem("xT_psum"), sem("xT_ready"), sem("gu_psum"), sem("silu_ready")
        mid_ready, midT_psum, midT_hi, midT_ready = sem("mid_ready"), sem("midT_psum"), sem("midT_hi"), sem("midT_ready")
        wd_hi_ready, wd_ready, o_wd_hi, o_wd, o_midT_hi = sem("wd_hi_ready"), sem("wd_ready"), sem("o_wd_hi"), sem("o_wd"), sem("o_midT_hi")
        y_psum, y_ready = sem("y_psum"), sem("y_ready")
        based = [sem(f"based{i}") for i in range(2)]
        scattered, pool_set, turns = sem("scattered"), sem("pool_set"), sem("turns")
        o_free, o_pos, o_onehot, o_idx_psum, o_idx, o_gathered = (
            sem("o_free"), sem("o_pos"), sem("o_onehot"), sem("o_idx_psum"), sem("o_idx"), sem("o_gathered"))
        o_xT_psum, o_xT, o_gu, o_silu, o_mid, o_midT_psum, o_midT, o_y_psum, o_y, o_scattered = (
            sem(n) for n in ("o_xT_psum", "o_xT", "o_gu", "o_silu", "o_mid", "o_midT_psum", "o_midT", "o_y_psum", "o_y", "o_scattered"))

        def after(eng, s, n):
            if not isinstance(n, int) or n > 0:
                eng.wait_ge(s, n)

        def lands(k, per, slot):
            if isinstance(k, int):
                return per * (k // 4 + 1)
            return (k - slot) * (per // 4) + per

        def chunk_cols(c):
            return in_chunks[c][2] + (HB if c == VA_LAST else 0) if c < NIN else COLS

        def chunk_landed(c):
            return 16 * (c + 1 + (1 if c >= VA_LAST else 0))

        def raw_of(c, j):
            return raw[j // HALF + (2 if c >= NCHUNK else 0)][:, j % HALF, 0:chunk_cols(c)]

        def split_of(t, c, j):
            return t[:, (ND * c + j) % RING, 0:chunk_cols(c)]

        def to_split(n):
            c, t = n // NT + 1, n % NT
            if c == NCHUNK or c >= NCHUNK + D // COLS:
                return []
            return [(c, j) for j in ({0: (0, 1), 1: (2, 3), NT - 1: range(HALF, ND)}.get(t, ()))]

        block = ctx.enter_context(nc.Block())

        @block.sync
        def _(sp):
            for t in range(NT):
                sp.dma_start(xin[t], x_rows[t * P:(t + 1) * P, :]).then_inc(x_in[t], 16)
                if t == 0:
                    sp.dma_start(cst[:], consts).then_inc(const_in, 16)
                    sp.dma_start(gmixT[:], g_mix.rearrange("(p j) -> p j", p=P)).then_inc(const_in, 16)
                if t == 1:
                    sp.dma_start(relb[0:REL_BUCKETS, :], rel_bias).then_inc(table_in, 16)
                    sp.dma_start(table_b, bias_table).then_inc(table_in, 16)

            def load_half(c, i):
                cols = in_chunks[c][2] if c < NIN else COLS
                if c < NIN:
                    src = w_in[:, in_chunks[c][1]:in_chunks[c][1] + cols].rearrange("(p j) c -> p j c", p=P)
                elif c < NCHUNK:
                    src = w_gate[:, (c - NIN) * COLS:(c - NIN + 1) * COLS].rearrange("(p j) c -> p j c", p=P)
                else:
                    src = w_out[:, (c - NCHUNK) * COLS:(c - NCHUNK + 1) * COLS].rearrange("(j p) c -> p j c", p=P)
                if c != NCHUNK:
                    after(sp, split_lo, ND * (c - 1) + HALF * (i + 1) if c else 0)
                sp.dma_start(raw[i + (2 if c >= NCHUNK else 0)][:, :, 0:cols], src[:, i * HALF:(i + 1) * HALF, :]).then_inc(chunk_in[i], 16)
                if c == VA_LAST:
                    c0 = 3 * WA + 3 * WB
                    src = w_in[:, c0:c0 + HB].rearrange("(p j) c -> p j c", p=P)
                    sp.dma_start(raw[i][:, :, cols:cols + HB], src[:, i * HALF:(i + 1) * HALF, :]).then_inc(chunk_in[i], 16)

            def load_chunk(c):
                for i in range(2):
                    load_half(c, i)

            load_chunk(0)
            sp.dma_start(bforget[:], b_forget.rearrange("(h o) -> h o", o=1)).then_inc(forget_in, 16)
            for c, g in enumerate((q_norm_a, k_norm_a, q_norm_b, k_norm_b)):
                for half in range(2):
                    sp.dma_start(gains[half * HEAD_DIM:(half + 1) * HEAD_DIM, c:c + 1], g.rearrange("(d o) -> d o", o=1)).then_inc(gains_in, 16)
            load_chunk(1)
            sp.dma_start(bgateT[:], b_gate).then_inc(small_in, 16)
            sp.dma_start(gffnT[:], g_ffn.rearrange("(p j) -> p j", p=P)).then_inc(small_in, 16)
            sp.dma_start(rbias[:], router_bias.rearrange("(o e) -> o e", o=1).broadcast_to([P, E])).then_inc(small_in, 16)
            load_chunk(2)
            sp.wait_ge(vec_free, 2 * NG)
            for g in range(NG):
                row = vec[:, g * DIST:(g + 1) * DIST].unsqueeze(1).broadcast_to([HG, P, DIST])
                sp.dma_start(vec_dram.ap()[g * HG:(g + 1) * HG], row).then_inc(vec_stored, 16)
            load_chunk(3)
            sp.wait_ge(vec_stored, 16 * NG)
            for head in range(HA):
                w = 2 * P if head < HG else N
                toeplitz = bass.AP(vec_dram, head * P * DIST + P - 1 + N - w, [[DIST - 1, P], [1, w]])
                sp.dma_start(bias_near[:, head, :] if head < HG else bias_far[:, head - HG, :], toeplitz).then_inc(bias_in, 16)
            for c in range(4, NIN - 1):
                load_chunk(c)
            sp.wait_ge(negc_ready, 1)
            sp.dma_start(negc_dram, fe).then_inc(negc_stored, 16)
            for c in range(NIN - 1, NIN + 1):
                load_chunk(c)
            sp.wait_ge(scores_ready, UA)
            sp.wait_ge(negc_stored, 16)
            for i in range(4):
                sp.dma_start(negc[:, 2 * i:2 * i + 2, :], negc_dram[2 * i:2 * i + 2, :].rearrange("(o h) t -> o h t", o=1).broadcast_to([P, 2, N])).then_inc(negc_in[i], 16)
            for c in range(NIN + 1, NCHUNK):
                load_chunk(c)
            sp.wait_ge(pv_psum, UA)
            for j in range(2):
                sp.dma_start(wpa[j], w_proj_a[j * P:(j + 1) * P, :]).then_inc(proj_in, 16)
            sp.wait_ge(split_lo, ND * NCHUNK)
            for j in range(4):
                sp.dma_start(wpb[j], w_proj_b[j * P:(j + 1) * P, :]).then_inc(proj_in, 16)
            sp.wait_ge(scores_added, UA + UB)
            load_chunk(NCHUNK)
            b, c = order[("y", 5)]
            sp.wait_ge(tr_ready[b], c + 1)
            for t in range(NT):
                sp.dma_start(x1[t], x_rows[t * P:(t + 1) * P, :]).then_inc(x1_in[t], 16)
            load_chunk(NCHUNK + 1)

            def load_w(n, k, e):
                t = (w_gate_e, w_up_e, w_down_e)[k]
                src = t[bass.ds(e, 1)].rearrange("o (p j) f -> p (o j) f", p=P)
                dst = (wgu[n][:, :, 0:F], wgu[n][:, :, F:2 * F], wd[n])[k]
                sp.dma_start(dst, src).then_inc(w_in_sem[n][k], 16)

            sp.wait_ge(merged_ready, ND)
            sp.dma_start(wgu[3][:, :, 0:F], w_gate_s.rearrange("(p j) f -> p j f", p=P)).then_inc(shared_in, 16)
            sp.dma_start(wgu[3][:, :, F:2 * F], w_up_s.rearrange("(p j) f -> p j f", p=P)).then_inc(shared_in, 16)
            sp.dma_start(wd[3], w_down_s.rearrange("(p j) f -> p j f", p=P)).then_inc(shared_in, 16)
            sp.dma_start(wr, w_router.rearrange("(p j) e -> p j e", p=P)).then_inc(router_in, 16)
            for k in range(3):
                load_w(0, k, 0)
            for t in range(NT):
                sp.wait_ge(hn_ready, t + 1)
                sp.dma_start(hn_dram[t * P:(t + 1) * P, :], hn[:, t, :]).then_inc(hn_stored, 16)
            sp.wait_ge(dense_ready, O_UNITS)
            for n in (1, 2):
                for k in range(3):
                    load_w(n, k, n)
            sp.wait_ge(wd_ready, 2)
            load_w(3, 2, 3)

            def store_base(t):
                sp.wait_ge(y_ready, 2 * (t + 1))
                sp.dma_start(out_rows[t * P:(t + 1) * P, :], y[t % 2]).then_inc(based[t % 2], 16)

            for t in range(SH - 2):
                store_base(t)
            sp.wait_ge(gu_psum, SH)
            for k in range(2):
                load_w(3, k, 3)
            for t in range(SH - 2, SH):
                store_base(t)

            regs = [sp.alloc_register(f"turn_value{i}") for i in range(4)]
            with sp.Fori(1, E // 4) as m:
                for n in range(4):
                    k = 4 * m + n
                    last = (n - 1) % 4
                    for reg, v in zip(regs, (lands(k - 1, 16, last), lands(k, 16, n), SH + k - 3, 2 * (k - 2))):
                        sp.reg_mov(reg, v)
                    before, own, read_gu, read_d = (bass.RuntimeValue.of_register_unchecked(r, min_val=1, max_val=2 * 16 * E) for r in regs)
                    sp.wait_ge(w_in_sem[last][1], before)
                    sp.wait_ge(gu_psum, read_gu)
                    load_w(n, 0, k)
                    sp.wait_ge(w_in_sem[last][2], before)
                    load_w(n, 1, k)
                    sp.wait_ge(w_in_sem[n][0], own)
                    sp.wait_ge(wd_ready, read_d)
                    load_w(n, 2, k)

            more = sp.value_load(rounds_i[0:1, 0:1], min_val=0, max_val=ROUNDS - 1)
            with sp.If(more > 0):
                with sp.Fori(0, more * E) as it:
                    sp.wait_ge(o_free, it + 1)
                    for k in range(3):
                        load_w(0, k, it % E)
            with sp.Else():
                pass

        @block.gpsimd
        def _(pool):
            nc.gpsimd.memset(minus_half[:], -0.5).then_inc(pool_set, 1)
            pool.wait_ge(pool_set, 1)

            def root(dst, src, n, width):
                pool.wait_ge(mean_ready, n)
                nc.gpsimd.tensor_tensor(dst, src, minus_half[:, 0:width], ALU.pow).then_inc(rnorm_ready, 1)

            n = 0
            for t in range(NT):
                n += 1
                root(hn_r[:, t:t + 1], hn_ms[:, t:t + 1], n, 1)
            for q in range(B_UNITS):
                if makes_qk(q):
                    n += 1
                    root(rnorm[:, q % 2, :], mean[:, q % 2, :], n, HB)
            for t in range(NT):
                n += 1
                root(hn_r[:, t:t + 1], hn_ms[:, t:t + 1], n, 1)
            pool.wait_ge(hn_stored, 16 * NT)
            for b in range(2):
                pool.wait_ge(tr_ready[b], uses[b])
            for i in range(4):
                nc.gpsimd.memset(xg[i], 0.0).then_inc(pool_set, 1)
            pool.wait_ge(pool_set, 5)
            last_row = pool.to_reg(N - 1)

            def take_turn(before):
                after(pool, turns, before)
                nc.gpsimd.tensor_tensor(turn[:], minus_half[0:16, 0:1], minus_half[0:16, 0:1], ALU.add).then_inc(turns, 1)

            def gather(slot, before, done):
                take_turn(before)
                pool.indirect_dma_start(out=xg[slot][0:SLOTS, :], out_offset=None, in_=hn_dram,
                                        in_offset=bass.IndirectOffsetOnAxis(idxg[slot][0:SLOTS, 0:1], 0),
                                        bounds_check=last_row, oob_is_err=False).then_inc(done, 16)

            def scatter(slot, idx, before, done):
                take_turn(before)
                pool.indirect_dma_start(out=out_rows, out_offset=bass.IndirectOffsetOnAxis(idx[0:SLOTS, 0:1], 0),
                                        in_=y[slot][0:SLOTS, :], in_offset=None, bounds_check=last_row, oob_is_err=False,
                                        compute_op=ALU.add).then_inc(done, 16)

            def gather_k(k, slot, before):
                after(pool, xT_psum, k - 3)
                pool.wait_ge(idx_ready, k + 1)
                gather(slot, before, gathered[slot])

            def scatter_k(k, u, before):
                pool.wait_ge(y_ready, 2 * (SH + k + 1))
                pool.wait_ge(idx_kept, k + 1)
                after(pool, scattered, 16 * k)
                scatter(u % 2, idxs[u], before, scattered)

            for k in range(5):
                gather_k(k, k % 4, k)
            for b in based:
                pool.wait_ge(b, 8 * SH)

            def pair(k, u):
                scatter_k(k, u, 5 + 2 * k)
                gather_k(k + 5, (u + 1) % 4, 6 + 2 * k)

            for k in range(4):
                pair(k, k)
            with pool.Fori(1, (E - 5) // 4) as m:
                for u in range(4):
                    pair(4 * m + u, u)
            for k in range((E - 5) // 4 * 4, E - 5):
                pair(k, k % 4)
            for k in range(E - 5, E):
                scatter_k(k, k % 4, 5 + 2 * (E - 5) + k - (E - 5))
            pool.wait_ge(scattered, 16 * E)

            more = pool.value_load(rounds_i[0:1, 0:1], min_val=0, max_val=ROUNDS - 1)
            with pool.If(more > 0):
                with pool.Fori(0, more * E) as it:
                    pool.wait_ge(o_idx, it + 1)
                    gather(0, 2 * E + 2 * it, o_gathered)
                    pool.wait_ge(o_y, it + 1)
                    scatter(0, idxg[0], 2 * E + 2 * it + 1, o_scattered)
                    pool.wait_ge(o_scattered, 16 * it + 16)
            with pool.Else():
                pass

        @block.scalar
        def _(act):
            chain = [0]

            def link(ins):
                chain[0] += 1
                ins.then_inc(act_chain, 1)
                act.wait_ge(act_chain, chain[0])

            sums = [0]

            def square(out_, in_, **kw):
                sums[0] += 1
                nc.scalar.activation(out_, in_, ACT.Square, **kw).then_inc(squared, 1)

            for t in range(NT):
                act.wait_ge(x_in[t], 16)
                after(act, squared, sums[0])
                square(sq_x, xin[t], accum_out=hn_ss[:, t:t + 1])

            def split_block(c, j):
                act.wait_ge(chunk_in[j // HALF], chunk_landed(c))
                if j < HALF:
                    after(act, dense_ready, NT * (c - 1))
                else:
                    after(act, half_used, c)
                nc.scalar.activation(split_of(w_hi, c, j), raw_of(c, j), ACT.Copy).then_inc(split_hi, 1)

            def copy_vec(g):
                for h in range(2):
                    act.wait_ge(vec_psum, 2 * g + h + 1)
                    nc.scalar.activation(vec[:, g * DIST + h * (DIST // 2):g * DIST + (h + 1) * (DIST // 2)], psS[h][0:HG, 0:DIST // 2],
                                         ACT.Copy).then_inc(vec_free, 1)

            for t in range(NT):
                if t >= 1:
                    copy_vec(t - 1)
                for b in range(2):
                    act.wait_ge(tr_used[b], t + 1)
                cols = slice(t * P, (t + 1) * P)
                nc.scalar.activation(hT_hi[:, :, cols], hT[:, :, cols], ACT.Copy).then_inc(hT_hi_ready, 1)
                for j in range((0, 0, 2, 5)[t], (0, 2, 5, ND)[t]):
                    split_block(0, j)

            def copy_qk(n):
                b, c = order[("qk", n)]
                act.wait_ge(tr_ready[b], c + 1)
                t = n % NT
                kind = unit_kind(n)
                cols = slice(t * P, (t + 1) * P)
                src = psT[b][:].rearrange("p (h q) -> p h q", q=P)
                if kind == "qk":
                    p0 = 4 * (n // NT)
                    cut = min(max(HA // 2 - p0, 0), 4)
                    parts = [(0, qTa, p0, 0, cut), (1, kTa, p0 - HA // 2, cut, 4)]
                else:
                    parts = [(2, qTb, 0, 0, 4)] if kind == "qb" else [(3, kTb, 0, 0, 4)]
                parts = [x for x in parts if x[3] < x[4]]
                for gain, dst, p0, a, z in parts:
                    last = nc.scalar.activation(dst[:, p0 + a:p0 + z, cols], src[:, a:z, :], ACT.Copy, scale=gains[:, gain:gain + 1])
                last.then_inc(tr_used[b], 1)

            def dense(n):
                kind, t, ps = unit_kind(n), n % NT, psD[n % 2]
                for c, j in to_split(n):
                    split_block(c, j)
                act.wait_ge(dense_ready, n + 1)
                if makes_qk(n):
                    after(act, summed, sq_count[0])
                    sq_count[0] += 1
                    square(sq[:, 0:COLS], ps[:])
                elif kind == "gate":
                    m = n - B_UNITS
                    act.wait_ge(small_in, 16 * 3)
                    nc.scalar.activation(gates[:, m, :], ps[:], ACT.Identity, bias=bgateT[:, m:m + 1]).then_inc(dense_used[n % 2], 1)
                else:
                    _, c0, cols = in_chunks[n // NT]
                    if kind == "vb":
                        act.wait_ge(negc_stored, 16)
                    dst = va[:, t, c0 - 2 * WA:c0 - 2 * WA + cols] if kind == "va" else vb[:, t, :]
                    if n // NT == VA_LAST:
                        nc.scalar.activation(frow[:, t, :], ps[:, cols:cols + HB], ACT.Copy)
                    nc.scalar.activation(dst, ps[:, 0:cols], ACT.Copy).then_inc(dense_used[n % 2], 1)

            def copy_p(key, dst):
                b, c = order[key]
                act.wait_ge(tr_ready[b], c + 1)
                w = dst.shape[1]
                nc.scalar.activation(dst, psT[b][:, 0:w * P].rearrange("p (b q) -> p b q", q=P), ACT.Copy).then_inc(tr_used[b], 1)

            def exp_a(u):
                act.wait_ge(scores_ready, u + 1)
                w = P * len(blocks_a(u))
                nc.scalar.activation(sc_a[u % 2][:, 0:w], sc_a[u % 2][:, 0:w], ACT.Exp, bias=negmax[:, u % 2, 0:1],
                                     accum_out=rowsum[:, u % 2, 0:1]).then_inc(exp_ready, 1)

            def exp_b(v):
                act.wait_ge(scores_ready, UA + v + 1)
                c0 = 0
                for s, i in enumerate(tiles_b(v)):
                    w = P * (i + 1)
                    last = nc.scalar.activation(sc_b[v % 2][:, c0:c0 + w], sc_b[v % 2][:, c0:c0 + w], ACT.Exp,
                                                bias=negmax[:, v % 2, s:s + 1], accum_out=rowsum[:, v % 2, s:s + 1])
                    c0 += w
                last.then_inc(exp_ready, 1)

            sq_count = [0]
            act.wait_ge(setup_done, 1)
            act.wait_ge(squared, NT)
            for n in range(A_UNITS):
                if n == A_UNITS - 1:
                    exp_a(0)
                dense(n)
                if makes_qk(n - 1):
                    copy_qk(n - 1)

            for u in range(1, UA + 1):
                nb = len(blocks_a(u - 1))
                after(act, pv_psum, u - 1)
                for r in range(0, -(-nb // 4), 2):
                    copy_p(("pa", u - 1, r), pT_a[:, 4 * r:min(4 * r + 4, nb), :])
                if u < UA:
                    exp_a(u)
                else:
                    exp_b(0)
                n = finishes(u)
                if n is not None:
                    dense(n)
                    if makes_qk(n - 1):
                        copy_qk(n - 1)
                if u == 2:
                    act.wait_ge(f_abs, 1)
                    nc.scalar.activation(fe, fa, ACT.Exp, scale=-1.0).then_inc(f_exp, 1)
                    act.wait_ge(f_exp, 1)
                    nc.scalar.activation(fl, fe, ACT.Ln, bias=1.0).then_inc(f_ln, 1)
            for v in range(1, UB + 1):
                act.wait_ge(pv_psum, UA + v - 2)
                copy_p(("pb", v - 1, 0), pT_b[(v - 1) % 2][:, 0:4, :])
                if v < UB:
                    exp_b(v)
                dense(B_UNITS + v - 1)
            for r in (1, 3, 5):
                b, c = order[("y", r)]
                act.wait_ge(tr_ready[b], c + 1)
                nc.scalar.activation(yTa[:, r, :] if r < 2 else yTb[:, r - 2, :], psT[b][:], ACT.Copy).then_inc(tr_used[b], 1)
            act.wait_ge(dense_used[0], G_UNITS // 2)
            act.wait_ge(dense_used[1], G_UNITS // 2)
            for m in range(ND):
                for g in (m, ND + m):
                    nc.scalar.activation(gates[:, g, :], gates[:, g, :], ACT.Sigmoid).then_inc(sig_ready, 1)
            for m in range(ND):
                act.wait_ge(added, m + 1)
                nc.scalar.activation(hT_hi[:, m, :], merged[m % 2], ACT.Copy).then_inc(merged_hi, 1)
                split_block(NCHUNK, m)
            for n in range(G_UNITS, O_UNITS):
                for c, j in to_split(n):
                    split_block(c, j)
                if n >= O_UNITS - NT:
                    t = n % NT
                    act.wait_ge(x1_ready, n - G_UNITS + 1)
                    act.wait_ge(squared, sums[0])
                    square(sq_h, x1[t], accum_out=hn_ss[:, t:t + 1])
            def split_wd(slot, h):
                cols = slice(h * 512, (h + 1) * 512)
                return nc.scalar.activation(wd_hi[:, :, cols], wd[slot][:, :, cols], ACT.Copy)

            act.wait_ge(shared_in, 48)
            act.wait_ge(dense_ready, O_UNITS)
            for h in range(2):
                split_wd(3, h).then_inc(wd_hi_ready, 1)
            act.wait_ge(logits_psum, 1)
            nc.scalar.activation(scoresT, psI[0:E, :], ACT.Sigmoid).then_inc(scores_sig, 1)

            def silu_of(n, rows):
                return nc.scalar.activation(silu[n][0:rows, :], psG[n][0:rows, 0:F], ACT.Silu)

            def copy_midT(n, rows):
                return nc.scalar.activation(midT[n][0][:, :, 0:rows], psM[:, 0:NF * P].rearrange("p (j s) -> p j s", j=NF)[:, :, 0:rows], ACT.Copy)

            def copy_y(n, h):
                return nc.scalar.activation(y[n][0:SLOTS, h * 512:(h + 1) * 512], psY[h][0:SLOTS, :], ACT.Copy)

            def silu_i(it, n, rows):
                act.wait_ge(gu_psum, it + 1)
                after(act, mid_ready, it - 1)
                silu_of(n, rows).then_inc(silu_ready, 1)

            def y_i(it, n):
                after(act, scattered, 16 * (it - SH - 1))
                for h in range(2):
                    act.wait_ge(y_psum, 2 * it + h + 1)
                    copy_y(n, h).then_inc(y_ready, 1)

            def midT_i(it, n, rows):
                act.wait_ge(midT_psum, it + 1)
                after(act, y_psum, 2 * (it - 1))
                copy_midT(n, rows).then_inc(midT_hi, 1)

            def wd_i(it, slot):
                act.wait_ge(w_in_sem[slot][2], lands(it - SH, 16, slot))
                for h in range(2):
                    act.wait_ge(y_psum, 2 * it - 1 + h)
                    split_wd(slot, h).then_inc(wd_hi_ready, 1)

            def step(it, n, slot):
                silu_i(it, n, SLOTS)
                y_i(it - 1, 1 - n)
                midT_i(it, n, SLOTS)
                wd_i(it, slot)

            for it in range(SH + 1):
                silu_i(it, it % 2, P if it < SH else SLOTS)
                if it == 0:
                    continue
                if it == 1:
                    midT_i(0, 0, P)
                midT_i(it, it % 2, P if it < SH else SLOTS)
            wd_i(SH, 0)
            for b in based:
                act.wait_ge(b, 8 * SH)
            for it in range(SH + 1, SH + 4):
                step(it, it % 2, it % 4)
            with act.Fori(SH // 4 + 1, ITEMS // 4) as m:
                for u in range(4):
                    step(4 * m + u, u % 2, u)
            y_i(ITEMS - 1, 1)

            more = act.value_load(rounds_i[0:1, 0:1], min_val=0, max_val=ROUNDS - 1)
            with act.If(more > 0):
                with act.Fori(0, more * E) as it:
                    act.wait_ge(o_gu, it + 1)
                    silu_of(0, SLOTS).then_inc(o_silu, 1)
                    act.wait_ge(w_in_sem[0][2], 4 * E + 16 * it + 16)
                    split_wd(0, 0)
                    split_wd(0, 1).then_inc(o_wd_hi, 1)
                    act.wait_ge(o_midT_psum, it + 1)
                    copy_midT(0, SLOTS).then_inc(o_midT_hi, 1)
                    act.wait_ge(o_y_psum, it + 1)
                    copy_y(0, 0)
                    copy_y(0, 1).then_inc(o_y, 1)
            with act.Else():
                pass

        @block.vector
        def _(dve):
            chain = [0]

            def link(ins):
                chain[0] += 1
                ins.then_inc(dve_chain, 1)
                dve.wait_ge(dve_chain, chain[0])

            means = [0]

            def mean_of(dst, src, count):
                means[0] += 1
                nc.vector.tensor_scalar(dst, src, 1.0 / count, EPS, ALU.mult, ALU.add).then_inc(mean_ready, 1)
                dve.wait_ge(rnorm_ready, means[0])

            nc.vector.memset(relb[REL_BUCKETS:REL_BUCKETS + 1, :], 1.0)
            nc.vector.memset(ones_b[:], 1.0).then_inc(ones_set, 1)
            dve.wait_ge(const_in, 32)
            nc.vector.tensor_copy(iota_b[:], cst[:, P:2 * P])
            nc.vector.tensor_copy(tri_b[:], cst[:, 2 * P:3 * P])
            nc.vector.tensor_copy(mask_b[:], cst[:, 3 * P:4 * P])
            nc.vector.tensor_copy(ident_b[:], ident)

            def copy_wide(key, dst, g):
                for b in range(2):
                    k, c = order[(*key, b)]
                    dve.wait_ge(tr_ready[k], c + 1)
                    h = ND // 2
                    nc.vector.tensor_tensor(dst[:, b * h:(b + 1) * h, key[1] * P:(key[1] + 1) * P],
                                            psT[k][:].rearrange("p (j q) -> p j q", q=P),
                                            g[:, b * h:(b + 1) * h].unsqueeze(2).broadcast_to([P, h, P]), ALU.mult).then_inc(tr_used[k], 1)

            def split_block(c, j):
                dve.wait_ge(split_hi, ND * c + j + 1)
                nc.vector.tensor_tensor(split_of(w_lo, c, j), raw_of(c, j), split_of(w_hi, c, j).bitcast(f32), ALU.subtract).then_inc(split_lo, 1)

            def low_hT(t):
                cols = slice(t * P, (t + 1) * P)
                dve.wait_ge(hT_hi_ready, t + 1)
                nc.vector.tensor_tensor(hT_lo[:, :, cols], hT[:, :, cols], hT_hi[:, :, cols].bitcast(f32), ALU.subtract).then_inc(hT_lo_ready, 1)

            for t in range(NT):
                dve.wait_ge(squared, t + 1)
                mean_of(hn_ms[:, t:t + 1], hn_ss[:, t:t + 1], D)
                if t >= 2:
                    b, c = order[("x", t - 2, 1)]
                    dve.wait_ge(tr_ready[b], c + 1)
                nc.vector.tensor_scalar(xn[t % 2], xin[t], hn_r[:, t:t + 1], None, ALU.mult).then_inc(xn_ready, 1)
                if t >= 1:
                    copy_wide(("x", t - 1), hT, gmixT)
                if t >= 2:
                    low_hT(t - 2)
            copy_wide(("x", NT - 1), hT, gmixT)
            for j in range(ND):
                split_block(0, j)
            for t in range(NT - 2, NT):
                low_hT(t)
            dve.wait_ge(gains_in, 16 * 8)
            for c in (0, 2):
                last = nc.vector.tensor_scalar(gains[:, c:c + 1], gains[:, c:c + 1], HEAD_DIM ** -0.5, None, ALU.mult)
            last.then_inc(setup_done, 1)
            def forget_logits():
                b, c = order[("f",)]
                dve.wait_ge(tr_ready[b], c + 1)
                dve.wait_ge(forget_in, 16)
                nc.vector.tensor_scalar(fx, psT[b][0:HB, :], bforget[:, 0:1], None, ALU.add).then_inc(tr_used[b], 1)
                dve.wait_ge(tr_used[b], c + 1)
                nc.vector.scalar_tensor_tensor(fa, fx, -1.0, fx, ALU.mult, ALU.max).then_inc(f_abs, 1)

            def forget_sums():
                dve.wait_ge(f_ln, 1)
                link(nc.vector.scalar_tensor_tensor(fx, fx, 0.0, fl, ALU.min, ALU.subtract))
                link(nc.vector.memset(fl, 1.0))
                link(nc.vector.tensor_tensor_scan(fa, fl, fx, 0.0, ALU.mult, ALU.add))
                nc.vector.tensor_scalar(fe, fa, -1.0, None, ALU.mult).then_inc(negc_ready, 1)

            def forget_turned():
                b, c = order[("cq",)]
                dve.wait_ge(tr_ready[b], c + 1)
                nc.vector.tensor_copy(cq[:], psT[b][:].rearrange("p (t h) -> p t h", t=NT)[:, :, 0:HB]).then_inc(tr_used[b], 1)

            def dense(n):
                mean_squares(n)
                over_norm(n)

            def mean_squares(n):
                for c, j in to_split(n):
                    split_block(c, j)
                if makes_qk(n):
                    s = n % 2
                    rows[0] += 1
                    dve.wait_ge(squared, NT + rows[0])
                    nc.vector.tensor_reduce(sumsq[:, s, :], sq[:, 0:COLS].rearrange("p (h d) -> p h d", d=HEAD_DIM), AX.X, ALU.add).then_inc(summed, 1)
                    dve.wait_ge(summed, rows[0])
                    nc.vector.tensor_scalar(mean[:, s, :], sumsq[:, s, :], 1.0 / HEAD_DIM, EPS, ALU.mult, ALU.add).then_inc(mean_ready, 1)
                    means[0] += 1

            def over_norm(n):
                if n is not None and makes_qk(n):
                    s = n % 2
                    dve.wait_ge(rnorm_ready, means[0])
                    if n >= 2 and makes_qk(n - 2):
                        b, c = order[("qk", n - 2)]
                        dve.wait_ge(tr_ready[b], c + 1)
                    nc.vector.tensor_tensor(qkrow[s].rearrange("p (h d) -> p h d", d=HEAD_DIM), psD[s][:].rearrange("p (h d) -> p h d", d=HEAD_DIM),
                                            rnorm[:, s, :].unsqueeze(2).broadcast_to([P, HB, HEAD_DIM]), ALU.mult).then_inc(dense_used[s], 1)

            def copy_p(key, dst):
                b, c = order[key]
                dve.wait_ge(tr_ready[b], c + 1)
                nc.vector.tensor_copy(dst, psT[b][:, 0:dst.shape[1] * P].rearrange("p (b q) -> p b q", q=P)).then_inc(tr_used[b], 1)

            def maxima(buf, n, sizes):
                c0 = 0
                for s, w in enumerate(sizes):
                    last = nc.vector.reduce_max(rowmax[:, n % 2, s:s + 1], buf[:, c0:c0 + w], AX.X)
                    c0 += w
                link(last)
                nc.vector.tensor_scalar(negmax[:, n % 2, 0:len(sizes)], rowmax[:, n % 2, 0:len(sizes)], -1.0, None, ALU.mult).then_inc(scores_ready, 1)

            def add_a(u):
                h, i = u // NT, u % NT
                dve.wait_ge(scores_psum, u + 1)
                if u >= 2:
                    dve.wait_ge(pv_psum, u - 1)
                c0 = 0
                for g, (b0, b1) in enumerate(key_blocks_a(u)):
                    w = P * (b1 - b0)
                    u0 = P * (b0 - i) + N - P
                    row = bias_far[:, (g - 1) * HG + h, :] if g else bias_near[:, h, :]
                    u0 -= 0 if g else N - 2 * P
                    last = nc.vector.tensor_tensor(sc_a[u % 2][:, c0:c0 + w], psS[g][:, 0:w], row[:, u0:u0 + w], ALU.add)
                    c0 += w
                last.then_inc(scores_added, 1)

            def max_a(u):
                dve.wait_ge(scores_added, u + 1)
                maxima(sc_a[u % 2], u, [P * len(blocks_a(u))])

            def add_b(v):
                h = v // 2
                dve.wait_ge(scores_psum, UA + v + 1)
                dve.wait_ge(negc_in[h // 2], 16)
                dve.wait_ge(pv_psum, UA + v - 1)
                c0 = 0
                for s, i in enumerate(tiles_b(v)):
                    w = P * (i + 1)
                    last = nc.vector.scalar_tensor_tensor(sc_b[v % 2][:, c0:c0 + w], psS[s][:, 0:w], cq[:, i, h:h + 1], negc[:, h, 0:w],
                                                          ALU.add, ALU.add)
                    c0 += w
                last.then_inc(scores_added, 1)

            def max_b(v):
                dve.wait_ge(scores_added, UA + v + 1)
                maxima(sc_b[v % 2], v, [P * (i + 1) for i in tiles_b(v)])

            rows = [0]
            for n in range(A_UNITS):
                if n == A_UNITS - 1:
                    dve.wait_ge(bias_in, 16 * HA)
                    add_a(0)
                    max_a(0)
                dense(n)
            for u in range(1, UA + 1):
                add, find_max, w = (add_a, max_a, u) if u < UA else (add_b, max_b, 0)
                add(w)
                nb = len(blocks_a(u - 1))
                if nb > 4:
                    copy_p(("pa", u - 1, 1), pT_a[:, 4:min(8, nb), :])
                over_norm(finishes(u - 1))
                find_max(w)
                dve.wait_ge(exp_ready, u)
                link(nc.vector.reciprocal(rowinv[:, (u - 1) % 2, 0:1], rowsum[:, (u - 1) % 2, 0:1]))
                if finishes(u) is not None:
                    mean_squares(finishes(u))
                if u == 1:
                    forget_logits()
                if u == 3:
                    forget_sums()
                if u == 5:
                    forget_turned()
                dve.wait_ge(pv_psum, u)
                h, i = (u - 1) // NT, (u - 1) % NT
                nc.vector.tensor_scalar(yrow_a[:, i, h * HEAD_DIM:(h + 1) * HEAD_DIM], psV[:, 0:HEAD_DIM], rowinv[:, (u - 1) % 2, 0:1], None,
                                        ALU.mult).then_inc(y_norm, 1)
            for v in range(1, UB + 1):
                if v < UB:
                    add_b(v)
                copy_p(("pb", v - 1, 1), pT_b[(v - 1) % 2][:, 4:5, :])
                if v < UB:
                    max_b(v)
                dve.wait_ge(exp_ready, UA + v)
                link(nc.vector.reciprocal(rowinv[:, (v - 1) % 2, :], rowsum[:, (v - 1) % 2, :]))
                dense(B_UNITS + v - 1)
                dve.wait_ge(pv_psum, UA + v)
                h = (v - 1) // 2
                for s, i in enumerate(tiles_b(v - 1)):
                    last = nc.vector.tensor_scalar(yrow_b[:, i, h * HEAD_DIM:(h + 1) * HEAD_DIM], psV[:, s * HEAD_DIM:(s + 1) * HEAD_DIM],
                                                   rowinv[:, (v - 1) % 2, s:s + 1], None, ALU.mult)
                last.then_inc(y_norm, 1)
            for r in (0, 2, 4):
                b, c = order[("y", r)]
                dve.wait_ge(tr_ready[b], c + 1)
                nc.vector.tensor_copy(yTa[:, r, :] if r < 2 else yTb[:, r - 2, :], psT[b][:]).then_inc(tr_used[b], 1)
            def low_merged(m):
                dve.wait_ge(merged_hi, m + 1)
                nc.vector.tensor_tensor(hT_lo[:, m, :], merged[m % 2], hT_hi[:, m, :].bitcast(f32), ALU.subtract).then_inc(merged_ready, 1)

            for m in range(ND):
                dve.wait_ge(proj_psum, m + 1)
                dve.wait_ge(sig_ready, 2 * m + 2)
                nc.vector.tensor_tensor(gated[0], psD[m % 2][:], gates[:, m, :], ALU.mult)
                link(nc.vector.tensor_tensor(gated[1], psS[m % 2][:], gates[:, ND + m, :], ALU.mult))
                nc.vector.tensor_tensor(merged[m % 2], gated[0], gated[1], ALU.add).then_inc(added, 1)
                if m >= 1:
                    low_merged(m - 1)
                    split_block(NCHUNK, m - 1)
                dve.wait_ge(added, m + 1)
            low_merged(ND - 1)
            split_block(NCHUNK, ND - 1)

            def norm_x1(t):
                dve.wait_ge(squared, NT + rows[0] + t + 1)
                mean_of(hn_ms[:, t:t + 1], hn_ss[:, t:t + 1], D)
                nc.vector.tensor_scalar(hn[:, t, :], x1[t], hn_r[:, t:t + 1], None, ALU.mult).then_inc(hn_ready, 1)

            dve.wait_ge(small_in, 16 * 3)
            for n in range(G_UNITS, O_UNITS):
                h, t = divmod(n - G_UNITS, NT)
                for c, j in to_split(n):
                    split_block(c, j)
                dve.wait_ge(dense_ready, n + 1)
                dve.wait_ge(x1_in[t], 16)
                cols = slice(h * COLS, (h + 1) * COLS)
                nc.vector.tensor_tensor(x1[t][:, cols], psD[n % 2][:], x1[t][:, cols], ALU.add).then_inc(x1_ready, 1)
                if h == 1:
                    norm_x1(t)
                    if t >= 1:
                        copy_wide(("h", t - 1), h2T, gffnT)
            for t in range(NT):
                nc.vector.tensor_copy(table[:, t, :, 0], cst[:, 4 * P + t:4 * P + t + 1].broadcast_to([P, E]))
                nc.vector.tensor_copy(table[:, t, :, 1], cst[:, 4 * P + NT:4 * P + NT + 1].broadcast_to([P, E]))
            nc.vector.memset(table[:, :, :, 2:3], 1.0)
            copy_wide(("h", NT - 1), h2T, gffnT)
            def make_onehot(n, e):
                col = pos[:, :, bass.ds(e, 1)]
                return nc.vector.tensor_tensor(onehot[n][:, :, 0:SLOTS], iota_b[:, 0:SLOTS].unsqueeze(1).broadcast_to([P, NT, SLOTS]),
                                               col.broadcast_to([P, NT, SLOTS]), ALU.is_equal)

            def read_idx(slot, done):
                nc.vector.tensor_scalar(idxg[slot][0:SLOTS, :], psI[0:SLOTS, 0:1], psI[0:SLOTS, 1:2], float(NO_TOKEN), ALU.add, ALU.add)
                nc.vector.tensor_scalar(gate[0:SLOTS, slot:slot + 1], psI[0:SLOTS, 3:4], psI[0:SLOTS, 4:5], psI[0:SLOTS, 5:6], ALU.add, ALU.add).then_inc(done, 1)

            def copy_xT(n):
                h = ND // 2
                for c in range(2):
                    last = nc.vector.tensor_tensor(xT[n][:, c * h:(c + 1) * h, 0:SLOTS], psT[c][:].rearrange("p (j s) -> p j s", j=h)[:, :, 0:SLOTS],
                                                   gffnT[:, c * h:(c + 1) * h].unsqueeze(2).broadcast_to([P, h, SLOTS]), ALU.mult)
                return last

            def times_up(n, rows_, g):
                return nc.vector.scalar_tensor_tensor(mid[n][0:rows_, :], silu[n][0:rows_, :], g, psG[n][0:rows_, F:2 * F], ALU.mult, ALU.mult)

            def onehot_k(k, n):
                after(dve, idx_psum, k - 1)
                make_onehot(n, k).then_inc(onehot_ready, 1)

            def idx_k(k, slot):
                dve.wait_ge(idx_psum, k + 1)
                read_idx(slot, idx_ready)

            def xT_k(k, n):
                dve.wait_ge(xT_psum, k + 1)
                after(dve, gu_psum, SH + k - 1)
                copy_xT(n).then_inc(xT_ready, 1)

            def low_midT(n, rows_):
                src = psM[:, 0:NF * P].rearrange("p (j s) -> p j s", j=NF)[:, :, 0:rows_]
                return nc.vector.tensor_tensor(midT[n][1][:, :, 0:rows_], src, midT[n][0][:, :, 0:rows_].bitcast(f32), ALU.subtract)

            def low_wd(slot, h):
                cols = slice(h * 512, (h + 1) * 512)
                return nc.vector.tensor_tensor(wd_lo[:, :, cols], wd[slot][:, :, cols], wd_hi[:, :, cols].bitcast(f32), ALU.subtract)

            def low_midT_i(it, n, rows_):
                dve.wait_ge(midT_hi, it + 1)
                low_midT(n, rows_).then_inc(midT_ready, 1)

            def mid_i(it, n, rows_, g):
                dve.wait_ge(silu_ready, it + 1)
                after(dve, midT_psum, it - 1)
                times_up(n, rows_, g).then_inc(mid_ready, 1)

            def y_shared(t):
                if t >= 2:
                    dve.wait_ge(based[t % 2], 16 * (t // 2))
                for h in range(2):
                    dve.wait_ge(y_psum, 2 * t + h + 1)
                    nc.vector.tensor_tensor(y[t % 2][:, h * 512:(h + 1) * 512], psY[h][:], x1[t][:, h * 512:(h + 1) * 512], ALU.add).then_inc(y_ready, 1)

            for h in range(2):
                dve.wait_ge(wd_hi_ready, 1 + h)
                low_wd(3, h).then_inc(wd_ready, 1)
            dve.wait_ge(scores_turned, 1)
            link(nc.vector.tensor_tensor(sel, scores, rbias[:, :].unsqueeze(1).broadcast_to([P, NT, E]), ALU.add))
            for t in range(NT):
                last = nc.vector.max(m8[:, t, :], sel[:, t, :])
            link(last)
            for t in range(NT):
                last = nc.vector.match_replace(rep[:, t, :], m8[:, t, :], sel[:, t, :], NEVER)
            link(last)
            link(nc.vector.tensor_tensor(M, rep, sel, ALU.not_equal))
            nc.vector.tensor_copy(Mb, M).then_inc(mask_ready, 1)
            mid_i(0, 0, P, 1.0)
            link(nc.vector.tensor_tensor(gt, M, scores, ALU.mult))
            link(nc.vector.tensor_reduce(gsum[:], gt, AX.X, ALU.add))
            link(nc.vector.reciprocal(ginv[:], gsum[:]))
            for t in range(NT):
                last = nc.vector.tensor_scalar(gt[:, t, :], gt[:, t, :], ginv[:, t:t + 1], ROUTE_SCALE, ALU.mult, ALU.mult)
            link(last)
            link(nc.vector.tensor_copy(table[:, :, :, 3], gt))
            link(nc.vector.tensor_tensor(gres, gt, table[:, :, :, 3], ALU.subtract))
            link(nc.vector.tensor_copy(table[:, :, :, 4], gres))
            link(nc.vector.tensor_tensor(gt, gres, table[:, :, :, 4], ALU.subtract))
            nc.vector.tensor_copy(table[:, :, :, 5], gt)
            low_midT_i(0, 0, P)
            dve.wait_ge(counts_psum, 1)
            link(nc.vector.tensor_tensor(gres, psI[:, 0:NT * E].rearrange("p (t e) -> p t e", t=NT), M, ALU.mult))
            link(nc.vector.tensor_scalar(pos, gres, -1.0, None, ALU.add))
            link(nc.vector.reduce_max(cmax[:], psT[1][:, 0:E], AX.X))
            link(nc.vector.tensor_scalar(over[:, 0:ROUNDS - 1], thresholds, cmax[:, 0:1], None, ALU.is_lt))
            link(nc.vector.reduce_sum(oround[:], over[:, 0:ROUNDS - 1], AX.X))
            nc.vector.tensor_copy(rounds_i[:], oround[:]).then_inc(routed, 1)
            dve.wait_ge(routed, 1)
            onehot_k(0, 0)
            mid_i(1, 1, P, 1.0)
            y_shared(0)
            idx_k(0, 0)
            onehot_k(1, 1)
            low_midT_i(1, 1, P)
            mid_i(2, 0, P, 1.0)
            y_shared(1)
            idx_k(1, 1)
            onehot_k(2, 0)
            low_midT_i(2, 0, P)
            idx_k(2, 2)
            onehot_k(3, 1)
            mid_i(3, 1, P, 1.0)
            xT_k(0, 0)
            y_shared(2)
            low_midT_i(3, 1, P)
            idx_k(3, 3)
            onehot_k(4, 0)

            def expert(k, u, ix=True, oh=True, xt=True):
                dve.wait_ge(idx_ready, k + 1)
                mid_i(SH + k, u % 2, SLOTS, gate[0:SLOTS, u:u + 1])
                if xt:
                    xT_k(k + 1, (u + 1) % 2)
                if isinstance(k, int) and k == 0:
                    y_shared(SH - 1)
                after(dve, scattered, 16 * (k - 3))
                nc.vector.tensor_copy(idxs[u][0:SLOTS, :], idxg[u][0:SLOTS, :]).then_inc(idx_kept, 1)
                low_midT_i(SH + k, u % 2, SLOTS)
                if ix:
                    dve.wait_ge(mid_ready, SH + k + 1)
                    dve.wait_ge(idx_kept, k + 1)
                    idx_k(k + 4, u)
                if oh:
                    onehot_k(k + 5, (u + 1) % 2)
                for h in range(2):
                    dve.wait_ge(wd_hi_ready, 2 * k + 3 + h)
                    low_wd(u, h).then_inc(wd_ready, 1)

            for k in range(4):
                expert(k, k)
            with dve.Fori(1, E // 4 - 2) as m:
                for u in range(4):
                    expert(4 * m + u, u)
            for k in range(E - 8, E):
                expert(k, k % 4, ix=k + 4 < E, oh=k + 5 < E, xt=k + 1 < E)

            more = dve.value_load(rounds_i[0:1, 0:1], min_val=0, max_val=ROUNDS - 1)
            with dve.If(more > 0):
                with dve.Fori(0, more) as r:
                    nc.vector.tensor_scalar(pos, pos, -float(SLOTS), None, ALU.add).then_inc(o_pos, 1)
                    with dve.Fori(0, E) as e:
                        it = r * E + e
                        dve.wait_ge(o_pos, r + 1)
                        make_onehot(0, e).then_inc(o_onehot, 1)
                        dve.wait_ge(o_idx_psum, it + 1)
                        read_idx(0, o_idx)
                        dve.wait_ge(o_xT_psum, it + 1)
                        copy_xT(0).then_inc(o_xT, 1)
                        dve.wait_ge(o_silu, it + 1)
                        times_up(0, SLOTS, gate[0:SLOTS, 0:1]).then_inc(o_mid, 1)
                        dve.wait_ge(o_wd_hi, it + 1)
                        low_wd(0, 0)
                        low_wd(0, 1).then_inc(o_wd, 1)
                        dve.wait_ge(o_midT_hi, it + 1)
                        low_midT(0, SLOTS).then_inc(o_midT, 1)
                        dve.wait_ge(o_scattered, 16 * it + 16)
            with dve.Else():
                pass

        @block.tensor
        def _(pe):
            def transposes(key, parts):
                b, c = order[key]
                after(pe, tr_used[b], c)
                for n, (src, k) in enumerate(parts):
                    last = nc.tensor.transpose(psT[b][0:src.shape[1], n * P:n * P + k], src, ident[0:k, 0:k])
                last.then_inc(tr_ready[b], 1)

            pe.wait_ge(ones_set, 1)
            for _ in range(WARM_UP):
                nc.tensor.matmul(psV[:, 0:P], ones_b[:], ones_b[:], start=True, stop=True)
            pe.wait_ge(const_in, 32)

            def bias_by_distance(g):
                for h in range(2):
                    after(pe, vec_free, 2 * (g - 1) + h + 1)
                    nc.tensor.matmul(psS[h][0:HG, 0:DIST // 2], relb[:, g * HG:(g + 1) * HG],
                                     table_b[:, g * DIST + h * (DIST // 2):g * DIST + (h + 1) * (DIST // 2)], start=True, stop=True).then_inc(vec_psum, 1)

            for t in range(NT):
                pe.wait_ge(xn_ready, t + 1)
                if t >= 1:
                    pe.wait_ge(table_in, 32)
                    bias_by_distance(t - 1)
                for b in range(2):
                    transposes(("x", t, b), [(xn[t % 2][:, j::ND], P) for j in range(b * ND // 2, (b + 1) * ND // 2)])
            for b in range(2):
                pe.wait_ge(tr_used[b], NT)
            def dense_step(n, j):
                c, t = n // NT, n % NT
                if j == 0:
                    if n < G_UNITS:
                        after(pe, dense_used[n % 2], n // 2)
                    elif n < G_UNITS + 2:
                        pe.wait_ge(added, ND - 1 + n % 2)
                    else:
                        pe.wait_ge(x1_ready, n - G_UNITS - 1)
                    if n < NT:
                        pe.wait_ge(hT_lo_ready, t + 1)
                if t == 0:
                    pe.wait_ge(split_lo, ND * c + j + 1)
                if n == G_UNITS:
                    pe.wait_ge(merged_ready, j + 1)
                w = [split_of(x, c, j) for x in (w_hi, w_lo)]
                h = [x[:, j, :] for x in (hT_hi, hT_lo)]
                for k, (a, b) in enumerate(((0, 0), (0, 1), (1, 0))):
                    if B_UNITS <= n < G_UNITS:
                        left, right = w[a][:, t * P:(t + 1) * P], h[b]
                    else:
                        left, right = h[a][:, t * P:(t + 1) * P], w[b]
                    last = nc.tensor.matmul(psD[n % 2][:, 0:chunk_cols(c)], left, right, start=(j == 0 and k == 0), stop=(j == ND - 1 and k == 2))
                if t == NT - 1 and j == HALF - 1:
                    last.then_inc(half_used, 1)
                if j == ND - 1:
                    last.then_inc(dense_ready, 1)

            def dense(n):
                for j in range(ND):
                    dense_step(n, j)

            def transpose_qk(n):
                pe.wait_ge(qkrow_done(n)[0], qkrow_done(n)[1])
                transposes(("qk", n), [(qkrow[n % 2][:, i * P:(i + 1) * P], P) for i in range(4)])

            def qkrow_done(n):
                return dense_used[n % 2], n // 2 + 1

            def scores_a(u):
                h, i = u // NT, u % NT
                after(pe, scores_ready, u)
                for g, (b0, b1) in enumerate(key_blocks_a(u)):
                    head = g * HG + h
                    rows = slice(head % 2 * HEAD_DIM, (head % 2 + 1) * HEAD_DIM)
                    last = nc.tensor.matmul(psS[g][:, 0:P * (b1 - b0)], qTa[rows, head // 2, i * P:(i + 1) * P],
                                            kTa[rows, head // 2, b0 * P:b1 * P], start=True, stop=True)
                last.then_inc(scores_psum, 1)

            def transpose_pa(u):
                pe.wait_ge(exp_ready, u + 1)
                nb = len(blocks_a(u))
                for r in range(-(-nb // 4)):
                    transposes(("pa", u, r), [(sc_a[u % 2][:, b * P:(b + 1) * P], P) for b in range(4 * r, min(4 * r + 4, nb))])

            def weighted_a(u):
                h = u // NT
                found = blocks_a(u)
                for r in range(-(-len(found) // 4)):
                    b, c = order[("pa", u, r)]
                    pe.wait_ge(tr_used[b], c + 1)
                after(pe, y_norm, u)
                for n, (g, b) in enumerate(found):
                    head = g * HG + h
                    last = nc.tensor.matmul(psV[:, 0:HEAD_DIM], pT_a[:, n, :], va[:, b, head * HEAD_DIM:(head + 1) * HEAD_DIM],
                                            start=(n == 0), stop=(n == len(found) - 1))
                last.then_inc(pv_psum, 1)

            def scores_b(v):
                h = v // 2
                rows = slice(h % 2 * HEAD_DIM, (h % 2 + 1) * HEAD_DIM)
                after(pe, scores_ready, UA + v)
                for s, i in enumerate(tiles_b(v)):
                    nc.tensor.matmul(psS[s][:, 0:P * (i + 1)], qTb[rows, h // 2, i * P:(i + 1) * P], kTb[rows, h // 2, 0:(i + 1) * P],
                                     start=True, stop=False)
                    last = nc.tensor.matmul(psS[s][:, i * P:(i + 1) * P], ident_b[:], mask_b[:], start=False, stop=True)
                last.then_inc(scores_psum, 1)

            def weighted_b(v):
                h = v // 2
                for r in range(2):
                    b, c = order[("pb", v, r)]
                    pe.wait_ge(tr_used[b], c + 1)
                pe.wait_ge(y_norm, UA + v)
                found = blocks_b(v)
                for n, (i, b) in enumerate(found):
                    s = tiles_b(v).index(i)
                    last = nc.tensor.matmul(psV[:, s * HEAD_DIM:(s + 1) * HEAD_DIM], pT_b[v % 2][:, n, :], vb[:, b, h * HEAD_DIM:(h + 1) * HEAD_DIM],
                                            start=(b == 0), stop=(b == i))
                last.then_inc(pv_psum, 1)

            def last_use(kinds, bank, below=None):
                return max(c + 1 for (kind, *r), (b, c) in order.items() if kind in kinds and b == bank and (below is None or r[0] < below))

            for n in range(A_UNITS):
                if n == A_UNITS - 1:
                    pe.wait_ge(vec_free, 2 * NG)
                    for b in range(2):
                        pe.wait_ge(tr_used[b], last_use(("qk",), b, A_UNITS))
                    scores_a(0)
                dense(n)
                if makes_qk(n - 1):
                    transpose_qk(n - 1)

            for u in range(1, UA + 1):
                if u < UA:
                    scores_a(u)
                else:
                    for b in range(2):
                        pe.wait_ge(tr_used[b], last_use(("qk",), b))
                    scores_b(0)
                transpose_pa(u - 1)
                for n, j in spread(u):
                    dense_step(n, j)
                n = finishes(u)
                if n is not None and makes_qk(n - 1):
                    transpose_qk(n - 1)
                if u == 1:
                    for b in range(2):
                        pe.wait_ge(dense_used[b], A_UNITS // 2)
                    transposes(("f",), [(frow[:, t, :], P) for t in range(NT)])
                if u == 5:
                    pe.wait_ge(negc_ready, 1)
                    transposes(("cq",), [(fa[:, t * P:(t + 1) * P], HB) for t in range(NT)])
                weighted_a(u - 1)
            for b in range(2):
                pe.wait_ge(dense_used[b], B_UNITS // 2)
            for v in range(1, UB + 1):
                if v < UB:
                    scores_b(v)
                pe.wait_ge(exp_ready, UA + v)
                for r, (b0, b1) in enumerate(((0, 4), (4, 5))):
                    transposes(("pb", v - 1, r), [(sc_b[(v - 1) % 2][:, b * P:(b + 1) * P], P) for b in range(b0, b1)])
                dense(B_UNITS + v - 1)
                weighted_b(v - 1)
            pe.wait_ge(y_norm, UA + UB)
            for r in range(6):
                rows, c = (yrow_a, r) if r < 2 else (yrow_b, r - 2)
                transposes(("y", r), [(rows[:, t, c * P:(c + 1) * P], P) for t in range(NT)])
            def y_turned(r):
                b, c = order[("y", r)]
                pe.wait_ge(tr_used[b], c + 1)

            for b in range(2):
                pe.wait_ge(dense_used[b], G_UNITS // 2)
            pe.wait_ge(proj_in, 16 * 6)
            for m in range(ND):
                after(pe, added, m - 1)
                for j in range(2):
                    if m == 0:
                        y_turned(j)
                    nc.tensor.matmul(psD[m % 2][:], wpa[j][:, m * P:(m + 1) * P], yTa[:, j, :], start=(j == 0), stop=(j == 1))
                for j in range(4):
                    if m == 0:
                        y_turned(2 + j)
                    last = nc.tensor.matmul(psS[m % 2][:], wpb[j][:, m * P:(m + 1) * P], yTb[:, j, :], start=(j == 0), stop=(j == 3))
                last.then_inc(proj_psum, 1)
            def transpose_h(t):
                pe.wait_ge(hn_ready, t + 1)
                for b in range(2):
                    transposes(("h", t, b), [(hn[:, t, j::ND], P) for j in range(b * ND // 2, (b + 1) * ND // 2)])

            for n in range(G_UNITS, O_UNITS):
                dense(n)
                if n > O_UNITS - NT:
                    transpose_h(n % NT - 1)
            def gate_up(n, rows, lhs, slot):
                for j in range(ND):
                    last = nc.tensor.matmul(psG[n][0:rows, :], lhs[:, j, 0:rows], wgu[slot][:, j, :], start=(j == 0), stop=(j == ND - 1))
                return last

            def transpose_mid(n, rows):
                for j in range(NF):
                    last = nc.tensor.transpose(psM[:, j * P:j * P + rows], mid[n][0:rows, j::NF], ident[0:rows, 0:rows])
                return last

            def down(n, h, rows):
                w = (wd_hi, wd_lo)
                for j in range(NF):
                    for k, (a, b) in enumerate(((0, 0), (0, 1), (1, 0))):
                        last = nc.tensor.matmul(psY[h][0:rows, :], midT[n][a][:, j, 0:rows], w[b][:, j, h * 512:(h + 1) * 512],
                                                start=(j == 0 and k == 0), stop=(j == NF - 1 and k == 2))
                return last

            def find_slots(n, e):
                for t in range(NT):
                    last = nc.tensor.matmul(psI[0:SLOTS, 0:6], onehot[n][:, t, 0:SLOTS], table[:, t, bass.ds(e, 1), :].rearrange("p a b -> p (a b)"),
                                            start=(t == 0), stop=(t == NT - 1))
                return last

            def transpose_rows(slot):
                for j in range(ND):
                    c = j % (ND // 2) * P
                    last = nc.tensor.transpose(psT[j // (ND // 2)][:, c:c + SLOTS], xg[slot][0:SLOTS, j::ND], ident[0:SLOTS, 0:SLOTS])
                return last

            def is_shared(it):
                return isinstance(it, int) and it < SH

            def up_i(it, n, slot):
                after(pe, mid_ready, it - 1)
                if is_shared(it):
                    pe.wait_ge(shared_in, 48)
                    gate_up(n, P, h2T[:, :, it * P:(it + 1) * P], 3).then_inc(gu_psum, 1)
                else:
                    for k in range(2):
                        pe.wait_ge(w_in_sem[slot][k], lands(it - SH, 16, slot))
                    pe.wait_ge(xT_ready, it - SH + 1)
                    gate_up(n, SLOTS, xT[n], slot).then_inc(gu_psum, 1)

            def down_i(it, n):
                pe.wait_ge(midT_ready, it + 1)
                for h in range(2):
                    pe.wait_ge(wd_ready, 1 + h if is_shared(it) else 2 * (it - SH) + 3 + h)
                    after(pe, y_ready, 2 * (it - 1) + h + 1)
                    down(n, h, P if is_shared(it) else SLOTS).then_inc(y_psum, 1)

            def midT_i(it, n):
                pe.wait_ge(mid_ready, it + 1)
                after(pe, midT_ready, it)
                transpose_mid(n, P if is_shared(it) else SLOTS).then_inc(midT_psum, 1)

            def find_i(it, n):
                pe.wait_ge(onehot_ready, it + 1)
                after(pe, idx_ready, it)
                find_slots(n, it).then_inc(idx_psum, 1)

            def step(it, u, xt=True, ix=True):
                n = u % 2
                up_i(it, n, u)
                if xt:
                    k, slot = it + 1 - SH, (u + 1) % 4
                    pe.wait_ge(gathered[slot], lands(k, 16, slot))
                    after(pe, xT_ready, k)
                    transpose_rows(slot).then_inc(xT_psum, 1)
                down_i(it - 1, 1 - n)
                midT_i(it, n)
                if ix:
                    find_i(it, n)

            for b in range(2):
                pe.wait_ge(tr_used[b], order[("h", 0, b)][1] + 1)
            up_i(0, 0, 0)
            transpose_h(NT - 1)
            pe.wait_ge(router_in, 16)
            for b in range(2):
                pe.wait_ge(tr_used[b], uses[b])
            for j in range(ND):
                last = nc.tensor.matmul(psI[0:E, :], wr[:, j, :], h2T[:, j, :], start=(j == 0), stop=(j == ND - 1))
            last.then_inc(logits_psum, 1)
            pe.wait_ge(scores_sig, 1)
            for t in range(NT):
                last = nc.tensor.transpose(psT[0][:, t * E:(t + 1) * E], scoresT[:, t * P:(t + 1) * P], ident[0:E, 0:E])
            last.then_inc(scores_turned, 1)
            up_i(1, 1, 1)
            pe.wait_ge(mask_ready, 1)
            for t in range(NT):
                for s in range(t + 1):
                    nc.tensor.matmul(psI[:, t * E:(t + 1) * E], tri_b[:] if s == t else ones_b[:], Mb[:, s, :], start=(s == 0), stop=(s == t))
            for t in range(NT):
                last = nc.tensor.matmul(psT[1][:, 0:E], ones_b[:], Mb[:, t, :], start=(t == 0), stop=(t == NT - 1))
            last.then_inc(counts_psum, 1)
            midT_i(0, 0)
            down_i(0, 0)
            find_i(0, 0)
            midT_i(1, 1)
            up_i(2, 0, 2)
            down_i(1, 1)
            find_i(1, 1)
            midT_i(2, 0)
            find_i(2, 0)
            for it in range(3, SH + 4):
                step(it, it % 4)
            with pe.Fori(2, ITEMS // 4 - 1) as m:
                for u in range(4):
                    step(4 * m + u, u)
            for it in range(ITEMS - 4, ITEMS):
                step(it, it % 4, xt=it + 1 < ITEMS, ix=False)
            down_i(ITEMS - 1, 1)

            more = pe.value_load(rounds_i[0:1, 0:1], min_val=0, max_val=ROUNDS - 1)
            with pe.If(more > 0):
                pe.wait_ge(scattered, 16 * E)
                with pe.Fori(0, more * E) as it:
                    nc.tensor.matmul(psM[0:1, 0:1], ident_b[:, 0:1], ident_b[:, 0:1], start=True, stop=True).then_inc(o_free, 1)
                    pe.wait_ge(o_onehot, it + 1)
                    find_slots(0, it % E).then_inc(o_idx_psum, 1)
                    pe.wait_ge(o_gathered, 16 * it + 16)
                    transpose_rows(0).then_inc(o_xT_psum, 1)
                    pe.wait_ge(o_xT, it + 1)
                    for k in range(2):
                        pe.wait_ge(w_in_sem[0][k], 4 * E + 16 * it + 16)
                    gate_up(0, SLOTS, xT[0], 0).then_inc(o_gu, 1)
                    pe.wait_ge(o_mid, it + 1)
                    transpose_mid(0, SLOTS).then_inc(o_midT_psum, 1)
                    pe.wait_ge(o_midT, it + 1)
                    pe.wait_ge(o_wd, it + 1)
                    down(0, 0, SLOTS)
                    down(0, 1, SLOTS).then_inc(o_y_psum, 1)
                    pe.wait_ge(o_y, it + 1)
            with pe.Else():
                pass


_INS = ["x", "g_mix", "w_in", "q_norm_a", "k_norm_a", "q_norm_b", "k_norm_b", "rel_bias", "b_forget", "w_gate", "b_gate",
        "w_proj_a", "w_proj_b", "w_out", "g_ffn", "w_router", "router_bias", "w_gate_e", "w_up_e", "w_down_e",
        "w_gate_s", "w_up_s", "w_down_s"]


def shape_constants():
    tiles = SEQ // P
    rounds = -(-SEQ // SLOTS)
    c = np.zeros((P, 4 * P + tiles + 1 + rounds), np.float32)
    c[:, 0:P] = np.eye(P)
    c[:, P:2 * P] = np.arange(P)[None]
    c[:, 2 * P:3 * P] = np.triu(np.ones((P, P)))
    c[:, 3 * P:4 * P] = np.triu(np.full((P, P), MASKED), 1)
    c[:, 4 * P:4 * P + tiles] = np.arange(tiles)[None] * P - NO_TOKEN
    c[:, 4 * P + tiles] = np.arange(P)
    c[:, 4 * P + tiles + 1:] = SLOTS * np.arange(1, rounds + 1)[None]
    dist = SEQ - 1 - np.arange(DIST)
    exact = REL_BUCKETS // 2
    n = np.maximum(dist, 1).astype(np.float32)
    large = exact + (np.log(n / np.float32(exact)) / np.float32(math.log(REL_MAX_DIST / exact)) * np.float32(REL_BUCKETS - exact)).astype(np.int32)
    bucket = np.where(dist < exact, dist, np.minimum(large, REL_BUCKETS - 1))
    table = np.zeros((REL_BUCKETS + 1, len(DIL_GROUPS), DIST), np.float32)
    for g, (window, step) in enumerate(DIL_GROUPS):
        seen = (dist >= 0) & (dist <= window) & (dist % step == 0)
        for b in range(REL_BUCKETS):
            table[b, g] = seen & (bucket == b)
        table[REL_BUCKETS, g] = np.where(seen, 0.0, MASKED)
    return c, table.reshape(REL_BUCKETS + 1, -1)


def kernel(**inputs):
    import concourse.bacc as bacc
    from concourse import mybir as mb
    from concourse.bass_utils import run_bass_kernel_spmd as run

    nc = bacc.Bacc("TRN2", target_bir_lowering=False, num_devices=1)
    consts, bias_table = shape_constants()
    given = {name: np.ascontiguousarray(inputs[name]) for name in _INS}
    given["b_gate"] = np.ascontiguousarray(given["b_gate"].reshape(-1, P).T)
    given |= {"consts": consts, "bias_table": bias_table}
    args = [nc.dram_tensor(f"in_{name}", a.shape, mb.dt.from_np(a.dtype), kind="ExternalInput").ap() for name, a in given.items()]
    out = nc.dram_tensor("out_0", given["x"].shape, mb.dt.float32, kind="ExternalOutput").ap()
    layer(nc, *args, out)
    r = run(nc, [{f"in_{name}": a for name, a in given.items()}], core_ids=[0])
    return r.results[0]["out_0"]
```
